# Optimizing a Trainium2 kernel written in Bass

```python
import jax, jax.numpy as jnp
from jax import lax
import numpy as np

D_MODEL = 1024
BATCH = 1
SEQ = 512
DEPTH = 2
DEC_BATCH = 8
DEC_SEQ = 1
PAST_LEN = 4096
PAGE_SIZE = 128

N_EVEN = (DEPTH + 1) // 2
N_ODD = DEPTH // 2
D_POOL = D_MODEL // 2
POOL_WINDOWS = (2, 4, 8, 16)
N_POOL_GROUPS = len(POOL_WINDOWS)
POOL_GROUP_DIM = D_POOL // N_POOL_GROUPS
POOL_HIST = max(POOL_WINDOWS) - 1
D_CONV = D_MODEL // 2
CONV_WIDTH = 3
CONV_HIST = CONV_WIDTH - 1
D_IN_EVEN = D_POOL + 3 * D_CONV
D_SGU = D_MODEL
CHUNK = 128
N_SGU_HEADS = 8
SGU_HEAD_DIM = D_SGU // N_SGU_HEADS
N_GROUPS = 4
EXPERTS_PER_GROUP = 4
N_EXPERTS = N_GROUPS * EXPERTS_PER_GROUP
TOP_K = 2
D_EXPERT = 512
EPS = 1e-6

kernel_name = "hybrid_pool_conv_sgu_hmoe_step"

def rmsnorm(x, g):
    xf = x.astype(jnp.float32)
    xf = xf * lax.rsqrt(jnp.mean(xf * xf, axis=-1, keepdims=True) + EPS)
    return (xf * g.astype(jnp.float32)).astype(x.dtype)

def pool_mixer(u, hist, w_pool, pool_scale):
    B, L, _ = u.shape
    ext = u if hist is None else jnp.concatenate([hist.astype(u.dtype), u], axis=1)
    n_prev = ext.shape[1] - L
    cs = jnp.cumsum(ext.astype(jnp.float32), axis=1)
    cs = jnp.pad(cs, ((0, 0), (1, 0), (0, 0)))
    hi = jnp.arange(n_prev + 1, n_prev + L + 1)
    cs_hi = cs[:, hi]
    outs = []
    for g, w in enumerate(POOL_WINDOWS):
        sl = slice(g * POOL_GROUP_DIM, (g + 1) * POOL_GROUP_DIM)
        lo = jnp.maximum(hi - w, 0)
        cnt = (hi - lo).astype(jnp.float32)[None, :, None]
        mean = (cs_hi[:, :, sl] - cs[:, lo, sl]) / cnt
        outs.append(mean - u[:, :, sl].astype(jnp.float32))
    d = jnp.concatenate(outs, axis=-1).astype(u.dtype).reshape(B, L, N_POOL_GROUPS, POOL_GROUP_DIM)
    y = jnp.einsum('blgc,gcd->blgd', d, w_pool).reshape(B, L, D_POOL)
    return y * pool_scale, ext[:, -POOL_HIST:]

def conv_mixer(b_gate, c_gate, x_b, hist, conv_w):
    z = c_gate * x_b
    L = z.shape[1]
    ext = jnp.concatenate([hist.astype(z.dtype), z], axis=1)
    y = conv_w[0] * ext[:, 0:L]
    for k in range(1, CONV_WIDTH):
        y = y + conv_w[k] * ext[:, k:k + L]
    return b_gate * y, ext[:, -CONV_HIST:]

def even_mixer(h, hist_pool, hist_conv, w_in, w_pool, pool_scale, conv_w, w_out):
    p = h @ w_in
    u_a = p[..., :D_POOL]
    b_g = p[..., D_POOL:D_POOL + D_CONV]
    c_g = p[..., D_POOL + D_CONV:D_POOL + 2 * D_CONV]
    x_b = p[..., D_POOL + 2 * D_CONV:]
    y_a, new_pool = pool_mixer(u_a, hist_pool, w_pool, pool_scale)
    y_b, new_conv = conv_mixer(b_g, c_g, x_b, hist_conv, conv_w)
    y = jnp.concatenate([y_a, y_b], axis=-1) @ w_out
    return y, new_pool, new_conv

def sgu_mixer(h, w_in, g_v, w_s, b_s, w_out):
    p = jax.nn.gelu(h @ w_in)
    u = p[..., :D_SGU]
    v = rmsnorm(p[..., D_SGU:], g_v)
    B, L, _ = v.shape
    c = min(L, CHUNK)
    n = L // c
    mask = jnp.tril(jnp.ones((c, c), dtype=w_s.dtype))
    w = w_s[:, :c, :c] * mask
    vh = v.reshape(B, n, c, N_SGU_HEADS, SGU_HEAD_DIM)
    mixed = jnp.einsum('hts,bnshd->bnthd', w, vh) + b_s[:, :c].T[None, None, :, :, None]
    y = (u * mixed.reshape(B, L, D_SGU)) @ w_out
    return y, v[:, -c:]

def hier_moe(h, w_rg, b_rg, w_re, b_re, w1, w3, w2):
    B, L, D = h.shape
    t = h.reshape(B * L, D)
    tf = t.astype(jnp.float32)
    pg = jax.nn.softmax(tf @ w_rg.astype(jnp.float32) + b_rg.astype(jnp.float32), axis=-1)
    pg_top, gi = lax.top_k(pg, 1)
    le = (tf @ w_re.astype(jnp.float32) + b_re.astype(jnp.float32)).reshape(-1, N_GROUPS, EXPERTS_PER_GROUP)
    le_sel = jnp.take_along_axis(le, gi[:, :, None], axis=1)[:, 0]
    pe = jax.nn.softmax(le_sel, axis=-1)
    pe_top, ei = lax.top_k(pe, TOP_K)
    pe_top = pe_top / jnp.sum(pe_top, axis=-1, keepdims=True)
    w_tok = pg_top * pe_top
    e_glob = gi * EXPERTS_PER_GROUP + ei
    gate = jnp.sum(jax.nn.one_hot(e_glob, N_EXPERTS, dtype=jnp.float32) * w_tok[..., None], axis=1)
    hid = jax.nn.silu(jnp.einsum('td,edf->tef', t, w1)) * jnp.einsum('td,edf->tef', t, w3)
    hid = hid * gate.astype(t.dtype)[:, :, None]
    y = jnp.einsum('tef,efd->td', hid, w2)
    return y.reshape(B, L, D)

def setup_inputs(seed: int = 0) -> dict:
    key = jax.random.key(seed)
    ks = jax.random.split(key, 24)
    f32 = jnp.float32

    def nrm(k, shape, scale):
        return jax.random.normal(k, shape, f32) * scale

    return {
        "x_prompt": nrm(ks[0], (BATCH, SEQ, D_MODEL), 1.0),
        "x_sample": nrm(ks[1], (DEC_BATCH, DEC_SEQ, D_MODEL), 1.0),
        "state_pool": nrm(ks[2], (N_EVEN, DEC_BATCH, POOL_HIST, D_POOL), 1.0),
        "state_conv": nrm(ks[3], (N_EVEN, DEC_BATCH, CONV_HIST, D_CONV), 1.0),
        "norm_mix": 1.0 + nrm(ks[4], (DEPTH, D_MODEL), 0.05),
        "w_in_even": nrm(ks[5], (N_EVEN, D_MODEL, D_IN_EVEN), D_MODEL ** -0.5),
        "w_pool": nrm(ks[6], (N_EVEN, N_POOL_GROUPS, POOL_GROUP_DIM, POOL_GROUP_DIM), POOL_GROUP_DIM ** -0.5),
        "pool_scale": 1.0 + nrm(ks[7], (N_EVEN, D_POOL), 0.1),
        "conv_w": nrm(ks[8], (N_EVEN, CONV_WIDTH, D_CONV), CONV_WIDTH ** -0.5),
        "w_out_even": nrm(ks[9], (N_EVEN, D_POOL + D_CONV, D_MODEL), (D_POOL + D_CONV) ** -0.5),
        "w_in_odd": nrm(ks[10], (N_ODD, D_MODEL, 2 * D_SGU), D_MODEL ** -0.5),
        "sgu_norm": 1.0 + nrm(ks[11], (N_ODD, D_SGU), 0.05),
        "w_sgu": nrm(ks[12], (N_ODD, N_SGU_HEADS, CHUNK, CHUNK), CHUNK ** -0.5),
        "b_sgu": 1.0 + nrm(ks[13], (N_ODD, N_SGU_HEADS, CHUNK), 0.1),
        "w_out_odd": nrm(ks[14], (N_ODD, D_SGU, D_MODEL), D_SGU ** -0.5),
        "norm_ffn": 1.0 + nrm(ks[15], (DEPTH, D_MODEL), 0.05),
        "w_router_group": nrm(ks[16], (DEPTH, D_MODEL, N_GROUPS), D_MODEL ** -0.5),
        "b_router_group": nrm(ks[17], (DEPTH, N_GROUPS), 0.01),
        "w_router_expert": nrm(ks[18], (DEPTH, D_MODEL, N_EXPERTS), D_MODEL ** -0.5),
        "b_router_expert": nrm(ks[19], (DEPTH, N_EXPERTS), 0.01),
        "w_gate": nrm(ks[20], (DEPTH, N_EXPERTS, D_MODEL, D_EXPERT), D_MODEL ** -0.5),
        "w_up": nrm(ks[21], (DEPTH, N_EXPERTS, D_MODEL, D_EXPERT), D_MODEL ** -0.5),
        "w_down": nrm(ks[22], (DEPTH, N_EXPERTS, D_EXPERT, D_MODEL), D_EXPERT ** -0.5),
        "norm_final": 1.0 + nrm(ks[23], (D_MODEL,), 0.05),
    }

def reference(x_prompt, x_sample, state_pool, state_conv, norm_mix, w_in_even, w_pool, pool_scale,
              conv_w, w_out_even, w_in_odd, sgu_norm, w_sgu, b_sgu, w_out_odd, norm_ffn,
              w_router_group, b_router_group, w_router_expert, b_router_expert,
              w_gate, w_up, w_down, norm_final):

    def run(x, pool_hists, conv_hists):
        new_pool, new_conv, new_v = [], [], []
        for i in range(DEPTH):
            j = i // 2
            h = rmsnorm(x, norm_mix[i])
            if i % 2 == 0:
                y, np_, nc_ = even_mixer(h, pool_hists[j], conv_hists[j], w_in_even[j], w_pool[j],
                                         pool_scale[j], conv_w[j], w_out_even[j])
                new_pool.append(np_)
                new_conv.append(nc_)
            else:
                y, nv_ = sgu_mixer(h, w_in_odd[j], sgu_norm[j], w_sgu[j], b_sgu[j], w_out_odd[j])
                new_v.append(nv_)
            x = x + y
            x = x + hier_moe(rmsnorm(x, norm_ffn[i]), w_router_group[i], b_router_group[i],
                             w_router_expert[i], b_router_expert[i], w_gate[i], w_up[i], w_down[i])
        return rmsnorm(x, norm_final), jnp.stack(new_pool), jnp.stack(new_conv), jnp.stack(new_v)

    zero_conv = jnp.zeros((BATCH, CONV_HIST, D_CONV), x_prompt.dtype)
    y_prompt, pool_p, conv_p, v_p = run(x_prompt, [None] * N_EVEN, [zero_conv] * N_EVEN)
    y_sample, pool_s, conv_s, v_s = run(x_sample, [state_pool[j] for j in range(N_EVEN)],
                                        [state_conv[j] for j in range(N_EVEN)])
    return (y_prompt, y_sample, pool_p, pool_s, conv_p, conv_s, v_p, v_s)


_drawn_inputs = setup_inputs


def setup_inputs(seed=0):
    import zlib

    import numpy as np

    out = dict(_drawn_inputs(seed))
    spreads = {}
    factors = {'b_router_group': 6.733, 'b_router_expert': 4.366}
    for name, (base, spread) in spreads.items():
        noise = np.random.default_rng([zlib.crc32(name.encode()), seed]).standard_normal(out[name].shape)
        drawn = base * np.exp(spread * noise) if base else spread * noise
        out[name] = __import__('jax').numpy.asarray(drawn.astype(out[name].dtype))
    for name, factor in factors.items():
        out[name] = (out[name] * factor).astype(out[name].dtype)
    return out
```

```python
from contextlib import ExitStack

import concourse.bass as bass
from concourse import mybir

F32 = mybir.dt.float32
BF16 = mybir.dt.bfloat16
I32 = mybir.dt.int32
U32 = mybir.dt.uint32
ALU = mybir.AluOpType
ACT = mybir.ActivationFunctionType
AX_X = mybir.AxisListType.X

P = 128
D = 1024
SEQ = 512
NS = 8
T = SEQ + NS
HALF = T // 2
NT = 5
ROWS = [P, P, P, P, NS]
KC = D // P
NG, EPG = 4, 4
NE = NG * EPG
DE = 512
FC = DE // P
PH, CH = 15, 2
WINDOWS = (2, 4, 8, 16)
NH = 8
EPS = 1e-6
PAIRS = 2 * T
MAX_OVER = 8
MAX_BLOCKS = NE + MAX_OVER
TABLE = MAX_BLOCKS + 2
BIG = -3.0e38


def need(eng, sem, count):
    if isinstance(count, int) and count <= 0:
        return
    eng.wait_ge(sem, count)


class Chain:

    def __init__(self, eng, sem):
        self.eng, self.sem, self.n = eng, sem, 0

    def __call__(self, ins):
        self.n += 1
        ins.then_inc(self.sem, 1)
        self.eng.wait_ge(self.sem, self.n)


def trunk(nc, x_prompt, x_sample, state_pool, state_conv, norm_mix, w_in_even, w_pool, pool_scale,
          conv_w, w_out_even, w_in_odd, sgu_norm, w_sgu, b_sgu, w_out_odd, norm_ffn, w_rg, b_rg,
          w_re, b_re, w_gate, w_up, w_down, norm_final, y_prompt, y_sample, pool_p, pool_s,
          conv_p, conv_s, v_p, v_s):
    with ExitStack() as ctx:
        def sb(name, shape, dt=F32):
            return ctx.enter_context(nc.sbuf_tensor(name, shape, dt))

        def sem(name):
            return ctx.enter_context(nc.semaphore(name))

        def dram(name, shape):
            return nc.dram_tensor(name, shape, F32, kind="Internal").ap()

        xrows = dram("xrows", (PAIRS + P, D))
        yrows = dram("yrows", (MAX_BLOCKS * P, D))

        wbuf = [[sb(f"wbuf_{k}{p}", [P, 4096]) for p in range(2)] for k in ("gate", "up", "down")]
        x = sb("x", [P, NT, D])
        arena_a = sb("arena_a", [P, 16 * T])
        arena_b = sb("arena_b", [P, KC * T])
        arena_c = sb("arena_c", [P, NT * D])
        ident = sb("ident", [P, P])
        before = sb("before", [P, P])
        upto = sb("upto", [P, P])
        ones = sb("ones", [P, P])
        zero_col = sb("zero_col", [P, P])
        wsT = sb("wsT", [P, NH, P])
        w00 = sb("w00", [NS, NH])
        wdiag = sb("wdiag", [NS, NH, NS])
        NV = 9
        vecT = sb("vecT", [P, KC, NV])
        wr = sb("wr", [P, 2, KC, NG + NE])
        br = sb("br", [P, 2, NG + NE])
        per_layer = sb("per_layer", [P, 4 * P + 4 * NS * (PH + CH)])
        wpool_sb = per_layer[:, 0:512].rearrange("p (g d) -> p g d", g=4)
        histT = per_layer[:, 512:992].rearrange("p (g b t) -> p g b t", g=4, b=NS)
        chistT = per_layer[:, 992:1056].rearrange("p (g b t) -> p g b t", g=4, b=NS)
        g_sgu = per_layer[:, 0:D]
        junk = sb("junk", [P, D], BF16)
        eps = sb("eps", [P, 1])
        ss = sb("ss", [P, 5, NT])
        rt = sb("rt", [P, 5, NT])
        rs = sb("rs", [P, 5, NT])
        lg = sb("lg", [P, NT, NG + NE])
        r4 = sb("r4", [P, 4, NT, 4])
        r1 = sb("r1", [P, 12, NT])
        r16 = sb("r16", [P, 5, NT, NE])
        ohs = sb("ohs", [P, 3, NT, 4])
        c16 = sb("c16", [P, 10, NE])
        over = sb("over", [P, MAX_OVER, NE])
        over2 = sb("over2", [P, MAX_OVER, NE])
        o8 = sb("o8", [P, 4, MAX_OVER])
        slots_f = sb("slots_f", [P, 4, NT])
        slots = sb("slots", [P, 4, NT], U32)
        gates = sb("gates", [P, 2, NT])
        pri = sb("pri", [P, 4])
        eidx = sb("eidx", [P, NE])
        jidx = sb("jidx", [P, MAX_OVER])
        thr = sb("thr", [P, 4])
        thr2 = sb("thr2", [P, 4])
        valid = sb("valid", [P, NT])
        table_f = sb("table_f", [P, 2 * TABLE + 1])
        table = sb("table", [P, 2 * TABLE + 1], I32)
        rcnt = sb("rcnt", [P, 4, 16])
        hs = sb("hs", [P, 4, NS])
        hs2 = sb("hs2", [P, 4, NS])
        head = sb("head", [P, 4, 16])

        pT = arena_a[:, :].rearrange("p (m t) -> p m t", m=16)
        raw = arena_a
        raw_ws = raw[:, 0:1024].rearrange("p (h s) -> p h s", h=NH)
        raw_vec = raw[0:NV, 1024:2048]
        raw_hist = raw[0:NS * PH, 2048:2560]
        raw_chist = raw[0:NS * CH, 2560:3072]
        raw_zero = raw[:, 3072:4096]
        rT = arena_a[:, 0:KC * T].rearrange("p (c t) -> p c t", c=KC)
        xg = [arena_a[:, k * D:(k + 1) * D] for k in range(2)]
        xgT = arena_a[:, 2048:3072].rearrange("p (c s) -> p c s", c=KC)
        act_g = arena_a[:, 3072:3584]
        hid = arena_a[:, 3584:4096]
        hidT = arena_a[:, 4096:4608].rearrange("p (c s) -> p c s", c=FC)
        yg = [arena_a[:, k * D:(k + 1) * D] for k in range(8)]
        hT = arena_b[:, :].rearrange("p (c t) -> p c t", c=KC)
        yo = [arena_b[:, k * D:(k + 1) * D] for k in range(2)]
        g_fin = arena_b[:, 2048:3072]
        b_bc = arena_b[:, 0:1024].rearrange("p (h t) -> p h t", h=NH)
        xs = arena_c[:, :].rearrange("p (j d) -> p j d", j=NT)
        sumA = arena_c[:, 0:16 + SEQ]
        sumB = arena_c[:, 528:1056 + 0]
        dif = arena_c[:, 1056:1056 + 4 * T].rearrange("p (g t) -> p g t", g=4)
        ost_u = arena_c[0:PH + NS, 3136:3136 + 512]
        ost_z = arena_c[0:CH + NS, 3648:3648 + 512]

        ps = ctx.enter_context(nc.psum_tensor("ps", [P, 8, 512], F32))

        def bank2(b):
            return ps[:, b:b + 2, :].rearrange("p b n -> p (b n)")

        ld_x = [sem(f"ld_x{j}") for j in range(NT)]
        ld_vec, ld_hist, ld_ws, ld_small = sem("ld_vec"), sem("ld_hist"), sem("ld_ws"), sem("ld_small")
        ld_g = [sem("ld_gsgu"), sem("ld_bsgu"), sem("ld_gfin")]
        ld_in = [[sem(f"ld_in{l}{q}") for q in range(4)] for l in range(2)]
        ld_out = [[sem(f"ld_out{l}{h}") for h in range(2)] for l in range(2)]
        ld_w = [[[sem(f"ld_w{l}{k}{p}") for p in range(2)] for k in range(3)] for l in range(2)]
        const_step, consts = sem("const_step"), sem("consts")
        dve_step = sem("dve_step")
        tails = sem("tails")
        vec_t, vec_e = sem("vec_t"), sem("vec_e")
        sq_done, rt_done, rc_done, xs_done = sem("sq_done"), sem("rt_done"), sem("rc_done"), sem("xs_done")
        tr_done, ev_d, ev_a = sem("tr_done"), sem("ev_d"), sem("ev_a")
        mm_done, mm_free = sem("mm_done"), sem("mm_free")
        z_done, conv_done, dif_done, yb_done = sem("z_done"), sem("conv_done"), sem("dif_done"), sem("yb_done")
        pool_mm, ya_done = sem("pool_mm"), sem("ya_done")
        ost_t, ost_e = sem("ost_t"), sem("ost_e")
        wo_done, x_upd = sem("wo_done"), sem("x_upd")
        vt_done, v_cp, v_sq, v_rt, vn_done = sem("vt_done"), sem("v_cp"), sem("v_sq"), sem("v_rt"), sem("vn_done")
        mix_mm, mix_done = sem("mix_mm"), sem("mix_done")
        out_st, state_st = sem("out_st"), sem("state_st")
        lg_mm, lg_done = sem("lg_mm"), sem("lg_done")
        ex_in, ex_out = sem("ex_in"), sem("ex_out")
        rank_in, rank_mm, slots_ok = sem("rank_in"), sem("rank_mm"), sem("slots_ok")
        moe = []
        for l in range(2):
            moe.append({k: sem(f"m{l}_{k}") for k in (
                "scat", "xT_mm", "xT_d", "xT_a", "h1_mm", "silu", "h3_mm", "hid", "hT_mm", "hT_e",
                "y_mm", "y_d", "y_a")})
            moe[l]["ld_x"] = [sem(f"m{l}_ld_x{p}") for p in range(2)]
            moe[l]["st_y"] = [sem(f"m{l}_st_y{p}") for p in range(2)]
        ld_y = [[sem(f"ld_y{l}{j}") for j in range(NT)] for l in range(2)]
        y_add, results_in = sem("y_add"), sem("results_in")
        fin_done, fin_st = sem("fin_done"), sem("fin_st")

        QUARTERS = [[2, 3, 0, 1], [2, 3, 0, 1]]
        quarter_buf = [wbuf[0][0], wbuf[1][0], wbuf[0][1], wbuf[1][1]]
        half_buf = [wbuf[2][0], wbuf[2][1]]

        def tok(j):
            return slice(j * P, j * P + ROWS[j])

        def in_cols(w, q):
            return w[0].rearrange("(c p) n -> p c n", p=P)[:, :, q * 512:(q + 1) * 512]

        def as_kn(buf, k):
            return buf[:, :].rearrange("p (c n) -> p c n", c=k)

        def expert_view(w, l):
            return w[l].rearrange("e (c p) n -> e p c n", p=P)

        experts = [[expert_view(w, l) for w in (w_gate, w_up, w_down)] for l in range(2)]

        def load_pairs(eng):
            return NE // 2 + eng.value_load(table[0:1, 2 * TABLE:2 * TABLE + 1], min_val=0,
                                            max_val=MAX_OVER // 2)

        def run_blocks(eng, l, body):
            eng.wait_ge(slots_ok, l + 1)
            pairs = load_pairs(eng)
            for b in range(3):
                body(b, b % 2, b, False)
            with eng.Fori(2, pairs) as i:
                body(2 * i - 1, 1, i, False)
                body(2 * i, 0, i, False)
            body(2 * pairs - 1, 1, pairs, True)
            return pairs

        def before_same(b, par, i):
            return b // 2 if isinstance(b, int) else (i - 1 if par == 1 else i)

        block = ctx.enter_context(nc.Block())

        @block.sync
        def _(sp):
            xp = x_prompt[0].rearrange("(j p) d -> j p d", p=P)
            for j in range(NT):
                src = xp[j] if j < 4 else x_sample.rearrange("b s d -> (b s) d")
                sp.dma_start(x[0:ROWS[j], j, :], src).then_inc(ld_x[j], 16)

            def projections(l, w_in, w_out):
                for n in range(4):
                    if l == 1:
                        m = moe[0]
                        last = [2 * pairs - 1, 2 * pairs - 1, 2 * pairs, 2 * pairs][n]
                        sp.wait_ge((m["h1_mm"], m["h3_mm"])[n % 2], last)
                    sp.dma_start(as_kn(quarter_buf[n], KC), in_cols(w_in, QUARTERS[l][n])
                                 ).then_inc(ld_in[l][n], 16)
                for h in range(2):
                    if l == 1:
                        sp.wait_ge(moe[0]["y_mm"], 2 * pairs - 1 + h)
                    sp.dma_start(as_kn(half_buf[h], KC),
                                 w_out[0].rearrange("(c p) n -> p c n", p=P)[:, :, h * 512:(h + 1) * 512]
                                 ).then_inc(ld_out[l][h], 16)

            def load_weights(l, k, par, src):
                sp.dma_start(as_kn(wbuf[k][par], KC if k < 2 else FC), src).then_inc(ld_w[l][k][par], 16)

            def experts_of(l):
                m = moe[l]
                for par in range(2):
                    for k in range(3):
                        if k < 2:
                            sp.wait_ge(mm_done, 16 * l + 4 * (2 * par + k) + 4)
                        else:
                            sp.wait_ge(wo_done, NT * (l + 1))
                        load_weights(l, k, par, experts[l][k][par])
                sp.wait_ge(slots_ok, l + 1)
                pairs = load_pairs(sp)
                with sp.Fori(1, pairs) as i:
                    for par in range(2):
                        b = 2 * i + par
                        e = sp.value_load(table[0:1, bass.ds(b, 1)], min_val=0, max_val=NE - 1)
                        for k, used in enumerate(("h1_mm", "h3_mm", "y_mm")):
                            sp.wait_ge(m[used], b - 1)
                            load_weights(l, k, par, experts[l][k][bass.ds(e, 1)].rearrange(
                                "a p c n -> (a p) c n"))
                return pairs

            projections(0, w_in_even, w_out_even)
            pairs = experts_of(0)
            projections(1, w_in_odd, w_out_odd)
            experts_of(1)

        @block.gpsimd
        def _(pool):
            step = Chain(pool, const_step)
            step(pool.memset(ident[:, :], 0.0))
            step(pool.affine_select(out=ident[:, :], in_=ident[:, :], compare_op=ALU.not_equal, fill=1.0,
                                    base=0, pattern=[[-1, P]], channel_multiplier=1))
            step(pool.memset(ones[:, :], 1.0))
            pool.affine_select(out=before[:, :], in_=ones[:, :], compare_op=ALU.is_gt, fill=0.0,
                               base=0, pattern=[[1, P]], channel_multiplier=-1)
            pool.affine_select(out=upto[:, :], in_=ones[:, :], compare_op=ALU.is_ge, fill=0.0,
                               base=0, pattern=[[1, P]], channel_multiplier=-1)
            flt = dict(allow_small_or_imprecise_dtypes=True)
            pool.memset(eps[:, :], EPS)
            pool.memset(ss[:, :, :], 1.0)
            pool.memset(lg[:, :, :], 0.0)
            pool.iota(pri[:, :], [[-1, 4]], base=4, channel_multiplier=0, **flt)
            pool.iota(eidx[:, :], [[1, NE]], base=0, channel_multiplier=0, **flt)
            pool.iota(jidx[:, :], [[1, MAX_OVER]], base=0, channel_multiplier=0, **flt)
            pool.iota(thr[:, :], [[P, 4]], base=P, channel_multiplier=0, **flt)
            pool.iota(thr2[:, :], [[2, 4]], base=0, channel_multiplier=0, **flt)
            pool.memset(valid[:, :], 1.0)
            step(pool.memset(table_f[:, :], 0.0))
            step(pool.affine_select(out=valid[:, NT - 1:NT], in_=ones[:, 0:1], compare_op=ALU.is_gt,
                                    fill=0.0, base=NS, pattern=[[0, 1]], channel_multiplier=-1))
            pool.memset(slots_f[:, :, :], 0.0)
            step(pool.memset(raw_zero, 0.0))
            pool.sem_inc(consts, 1)
            pool.dma_start(xrows[PAIRS:PAIRS + P, :], raw_zero).then_inc(tails, 16)
            pool.dma_start(yrows[NE * P:, :].rearrange("(k p) d -> p k d", p=P),
                           raw_zero.unsqueeze(1).to_broadcast([P, MAX_OVER, D])).then_inc(tails, 16)
            pool.dma_start(pool_s[0, :, 0:PH - 1, :], state_pool[0, :, 1:PH, :]).then_inc(state_st, 16)
            pool.dma_start(conv_s[0, :, 0:1, :], state_conv[0, :, 1:2, :]).then_inc(state_st, 16)

            for l in range(2):
                m = moe[l]
                if l == 1:
                    pool.dma_start(g_sgu, sgu_norm[0].partition_broadcast(P)).then_inc(ld_g[0], 16)
                    pool.wait_ge(mm_done, 32)
                    pool.dma_start(arena_b[:, 0:1024],
                                   b_sgu[0].rearrange("h t -> (h t)").partition_broadcast(P)
                                   ).then_inc(ld_g[1], 16)
                pool.wait_ge(slots_ok, l + 1)
                pool.wait_ge(tails, 32)
                for j in range(NT):
                    for k in range(2):
                        pool.indirect_dma_start(
                            out=xrows[:, :],
                            out_offset=bass.IndirectOffsetOnAxis(ap=slots[0:ROWS[j], k, j:j + 1], axis=0),
                            in_=xs[0:ROWS[j], j, :], in_offset=None).then_inc(m["scat"], 16)
                pool.wait_ge(m["scat"], 16 * 2 * NT)
                if l == 1:
                    pool.dma_start(g_fin, norm_final.partition_broadcast(P)).then_inc(ld_g[2], 16)

                def load_rows(b, par):
                    r = pool.value_load(table[0:1, bass.ds(TABLE + b, 1)], min_val=0, max_val=PAIRS)
                    pool.dma_start(xg[par], xrows[bass.ds(r, P), :]).then_inc(m["ld_x"][par], 16)

                load_rows(0, 0)
                load_rows(1, 1)

                def body(b, par, i, last):
                    if not last:
                        pool.wait_ge(m["xT_mm"], b + 1)
                        load_rows(b + 2, par)
                    if isinstance(b, int) and b == 0:
                        return
                    pool.wait_ge(m["y_d"], b)
                    pool.wait_ge(m["y_a"], b)
                    pool.dma_start(yrows[bass.ds((b - 1) * P, P), :], yo[1 - par]
                                   ).then_inc(m["st_y"][1 - par], 16)

                pairs = run_blocks(pool, l, body)
                pool.wait_ge(m["y_d"], 2 * pairs)
                pool.wait_ge(m["y_a"], 2 * pairs)
                pool.dma_start(yrows[bass.ds((2 * pairs - 1) * P, P), :], yo[1]
                               ).then_inc(m["st_y"][1], 16)
                pool.wait_ge(m["st_y"][0], 16 * pairs)
                pool.wait_ge(m["st_y"][1], 16 * pairs)
                pool.wait_ge(m["ld_x"][0], 16 * pairs + 16)
                pool.sem_inc(results_in, 1)
                pool.wait_ge(results_in, l + 1)
                for j in range(NT):
                    for k in range(2):
                        q = 2 * j + k
                        if q >= 8:
                            pool.wait_ge(y_add, 2 * NT * l + q - 7)
                        pool.indirect_dma_start(
                            out=yg[q % 8][0:ROWS[j], :], out_offset=None, in_=yrows[:, :],
                            in_offset=bass.IndirectOffsetOnAxis(ap=slots[0:ROWS[j], 2 + k, j:j + 1],
                                                                axis=0)).then_inc(ld_y[l][j], 16)

        @block.tensor
        def _(pe):
            def transpose_tile(ph, j, src, first_bank):
                for c in range(KC):
                    last = pe.transpose(ps[:, first_bank + c // 4, (c % 4) * P:(c % 4) * P + ROWS[j]],
                                        src[0:ROWS[j], c * P:(c + 1) * P], ident[0:ROWS[j], 0:ROWS[j]])
                return last

            def normed_tile(ph, j):
                n = NT * ph + j
                pe.wait_ge(xs_done, n + 1)
                need(pe, ev_d, n - 1)
                need(pe, ev_a, n - 1)
                transpose_tile(ph, j, xs[:, j, :], 4 + 2 * (j % 2)).then_inc(tr_done, 1)

            def project_in(l, extra):
                n = 16 * l
                for q in range(4):
                    w = as_kn(quarter_buf[q], KC)
                    pe.wait_ge(ld_in[l][q], 16)
                    if q == 0:
                        pe.wait_ge(ev_d, NT * (2 * l + 1))
                        pe.wait_ge(ev_a, NT * (2 * l + 1))
                    for mcol in range(4):
                        pair = 2 * (n % 2)
                        need(pe, mm_free, n - 1)
                        for k in range(KC):
                            for h in range(2):
                                last = pe.matmul(ps[:, pair + h, 0:HALF], w[:, k, mcol * P:(mcol + 1) * P],
                                                 hT[:, k, h * HALF:(h + 1) * HALF],
                                                 start=(k == 0), stop=(k == KC - 1))
                        last.then_inc(mm_done, 1)
                        n += 1
                        extra(n - 16 * l)

            def project_out(l, ready):
                for h in range(2):
                    pe.wait_ge(ld_out[l][h], 16)
                for j in range(NT):
                    ready(j)
                    pair = 2 * (j % 2)
                    need(pe, x_upd, NT * l + j - 1 if j >= 2 else 0)
                    for h in range(2):
                        w = as_kn(half_buf[h], KC)
                        for k in range(KC):
                            last = pe.matmul(ps[0:ROWS[j], pair + h, :], pT[:, k, tok(j)], w[:, k, :],
                                             start=(k == 0), stop=(k == KC - 1))
                    last.then_inc(wo_done, 1)
                    if j >= 1:
                        normed_tile(2 * l + 1, j - 1)
                        if j >= 2:
                            router(l, j - 2)
                normed_tile(2 * l + 1, NT - 1)
                router(l, NT - 2)
                router(l, NT - 1)

            def router(l, j):
                n = NT * (2 * l + 1) + j
                pe.wait_ge(ev_d, n + 1)
                pe.wait_ge(ev_a, n + 1)
                need(pe, lg_done, NT * l + j)
                for k in range(KC):
                    last = pe.matmul(ps[0:ROWS[j], (4, 6)[j % 2], 0:NG + NE], rT[:, k, tok(j)],
                                     wr[:, l, k, :], start=(k == 0), stop=(k == KC - 1))
                last.then_inc(lg_mm, 1)

            def ranks(l):
                A = r16[:, 2, :, :]
                pe.wait_ge(rank_in, l + 1)
                for j in range(NT):
                    for i in range(j + 1):
                        pe.matmul(ps[:, 4, j * NE:(j + 1) * NE], ones[:, :] if i < j else before[:, :],
                                  A[:, i, :], start=(i == 0), stop=(i == j), skip_group_check=True)
                for i in range(NT):
                    last = pe.matmul(ps[:, 5, 0:NE], ones[:, :], A[:, i, :], start=(i == 0), stop=(i == NT - 1))
                last.then_inc(rank_mm, 1)

            def experts_blocks(l):
                m = moe[l]

                def rows_T(b, par):
                    pe.wait_ge(m["ld_x"][par], 16 * (before_x + 1))
                    for c in range(KC):
                        last = pe.transpose(ps[:, 5 + c // 4, (c % 4) * P:(c % 4 + 1) * P],
                                            xg[par][:, c * P:(c + 1) * P], ident[:, :])
                    last.then_inc(m["xT_mm"], 1)

                def up(kind, bank, b, par, i, done):
                    pe.wait_ge(ld_w[l][kind][par], 16 * (before_same(b, par, i) + 1))
                    w = as_kn(wbuf[kind][par], KC)
                    for k in range(KC):
                        last = pe.matmul(ps[:, bank, :], xgT[:, k, :], w[:, k, :],
                                         start=(k == 0), stop=(k == KC - 1))
                    last.then_inc(m[done], 1)

                def hidden_T(b):
                    need(pe, m["hid"], b + 1)
                    need(pe, m["hT_e"], b)
                    for c in range(FC):
                        last = pe.transpose(ps[:, 4, c * P:(c + 1) * P], hid[:, c * P:(c + 1) * P], ident[:, :])
                    last.then_inc(m["hT_mm"], 1)

                def down(b, par, n):
                    pe.wait_ge(ld_w[l][2][par], 16 * n)
                    need(pe, m["hT_e"], b + 1)
                    need(pe, m["y_d"], b)
                    need(pe, m["y_a"], b)
                    w = as_kn(wbuf[2][par], FC)
                    for k in range(FC):
                        for h in range(2):
                            last = pe.matmul(ps[:, 2 + h, :], hidT[:, k, :], w[:, k, h * 512:(h + 1) * 512],
                                             start=(k == 0), stop=(k == FC - 1))
                    last.then_inc(m["y_mm"], 1)

                before_x = 0
                rows_T(0, 0)

                def body(b, par, i, last):
                    nonlocal before_x
                    first = isinstance(b, int) and b == 0
                    pe.wait_ge(m["xT_d"], b + 1)
                    pe.wait_ge(m["xT_a"], b + 1)
                    need(pe, m["silu"], b)
                    up(0, 0, b, par, i, "h1_mm")
                    if not first:
                        hidden_T(b - 1)
                    need(pe, m["hid"], b)
                    up(1, 1, b, par, i, "h3_mm")
                    if not last:
                        before_x = (b + 1) // 2 if isinstance(b, int) else i
                        rows_T(b + 1, 1 - par)
                    if not first:
                        down(b - 1, 1 - par, (b + 1) // 2 if isinstance(b, int) else i)

                pairs = run_blocks(pe, l, body)
                hidden_T(2 * pairs - 1)
                down(2 * pairs - 1, 1, pairs)

            pe.wait_ge(consts, 1)
            pe.wait_ge(ld_vec, 16 * 9)
            for c in range(KC):
                last = pe.transpose(ps[:, 0, c * NV:(c + 1) * NV], raw_vec[:, c * P:(c + 1) * P], ident[0:NV, 0:NV])
            last.then_inc(vec_t, 1)
            for j in range(NT):
                normed_tile(0, j)
            pe.wait_ge(ld_hist, 32)
            for g in range(4):
                pe.transpose(ps[:, 1, g * NS * PH:(g + 1) * NS * PH], raw_hist[:, g * P:(g + 1) * P],
                             ident[0:NS * PH, 0:NS * PH])
            for g in range(4):
                last = pe.transpose(ps[:, 0, 256 + g * NS * CH:256 + (g + 1) * NS * CH],
                                    raw_chist[:, g * P:(g + 1) * P], ident[0:NS * CH, 0:NS * CH])
            last.then_inc(vec_t, 1)
            pe.wait_ge(ld_ws, 16)
            for h in range(NH):
                last = pe.transpose(ps[:, 2 + h // 4, (h % 4) * P:(h % 4 + 1) * P], raw_ws[:, h, :], ident[:, :])
            last.then_inc(vec_t, 1)
            pe.wait_ge(vec_e, 3)

            def extra0(n):
                if n == 10:
                    pe.wait_ge(z_done, 4)
                    for g in range(4):
                        last = pe.transpose(ps[0:CH + NS, 4, g * P:(g + 1) * P],
                                            pT[:, 12 + g, SEQ - CH:T], ident[:, :])
                    last.then_inc(ost_t, 1)
                if n == 14:
                    pe.wait_ge(mm_free, 12)
                    for g in range(4):
                        last = pe.transpose(ps[0:PH + NS, 5, g * P:(g + 1) * P],
                                            pT[:, g, SEQ - PH:T], ident[:, :])
                    last.then_inc(ost_t, 1)

            project_in(0, extra0)
            pe.wait_ge(ld_small, 16 * 8)
            pe.wait_ge(mm_free, 16)
            for g in range(4):
                pe.wait_ge(dif_done, g + 1)
                need(pe, ya_done, g - 1)
                for h in range(2):
                    last = pe.matmul(ps[:, 2 * (g % 2) + h, 0:HALF], wpool_sb[:, g, :],
                                     dif[:, g, h * HALF:(h + 1) * HALF], start=True, stop=True)
                last.then_inc(pool_mm, 1)

            def ready0(j):
                if j == 0:
                    pe.wait_ge(ya_done, 4)
                    pe.wait_ge(yb_done, 4)

            project_out(0, ready0)
            ranks(0)
            experts_blocks(0)

            for j in range(NT):
                normed_tile(2, j)

            def extra1(n):
                if 8 <= n < 8 + NT:
                    j = n - 8
                    pe.wait_ge(mm_free, 16 + 8)
                    need(pe, v_cp, j - 1)
                    for c in range(KC):
                        last = pe.transpose(ps[0:ROWS[j], 4 + 2 * (j % 2) + c // 4, (c % 4) * P:(c % 4 + 1) * P],
                                            pT[:, 8 + c, tok(j)], ident[:, :])
                    last.then_inc(vt_done, 1)

            project_in(1, extra1)
            for j in range(NT):
                pe.wait_ge(vn_done, j + 1)
                need(pe, mix_done, j - 1)
                for h in range(NH):
                    rhs = wsT[:, h, :] if j < 4 else wdiag[:, h, :]
                    last = pe.matmul(ps[:, 4 + 2 * (j % 2) + h // 4, (h % 4) * P:(h % 4) * P + ROWS[j]],
                                     xs[0:ROWS[j], j, h * P:(h + 1) * P], rhs, start=True, stop=True,
                                     skip_group_check=True)
                last.then_inc(mix_mm, 1)

            def ready1(j):
                pe.wait_ge(mix_done, j + 1)
                if j == 0:
                    pe.wait_ge(mm_free, 32)

            project_out(1, ready1)
            ranks(1)
            experts_blocks(1)

        @block.scalar
        def _(act):
            for r, src in enumerate((norm_mix[0:1, :], norm_mix[1:2, :], norm_ffn[0:1, :], norm_ffn[1:2, :],
                                     sgu_norm[0:1, :])):
                act.dma_start(raw_vec[r:r + 1, :], src).then_inc(ld_vec, 16)
            for h in range(2):
                act.dma_start(raw_vec[5:6, h * 512:(h + 1) * 512], pool_scale[0:1, :]).then_inc(ld_vec, 16)
                act.dma_start(raw_vec[6:9, h * 512:(h + 1) * 512], conv_w[0]).then_inc(ld_vec, 16)
            act.dma_start(raw_hist, state_pool[0].rearrange("b t c -> (b t) c")).then_inc(ld_hist, 16)
            act.dma_start(raw_chist, state_conv[0].rearrange("b t c -> (b t) c")).then_inc(ld_hist, 16)
            act.dma_start(raw_ws, w_sgu[0].rearrange("h t s -> t h s")).then_inc(ld_ws, 16)
            act.dma_start(wpool_sb[:, :, :], w_pool[0].rearrange("g c d -> c g d")).then_inc(ld_small, 16)
            for l in range(2):
                act.dma_start(wr[:, l, :, 0:NG], w_rg[l].rearrange("(c p) e -> p c e", p=P)).then_inc(ld_small, 16)
                act.dma_start(wr[:, l, :, NG:], w_re[l].rearrange("(c p) e -> p c e", p=P)).then_inc(ld_small, 16)
            act.dma_start(br[:, :, 0:NG], b_rg.partition_broadcast(P)).then_inc(ld_small, 16)
            act.dma_start(br[:, :, NG:], b_re.partition_broadcast(P)).then_inc(ld_small, 16)
            act.dma_start(w00[:, :], w_sgu[0, :, 0, 0:1].rearrange("h a -> (h a)").partition_broadcast(NS),
                          allow_slow_non_contiguous=True).then_inc(ld_small, 16)

            def root(ph, j, src):
                n = NT * ph + j
                r = slice(0, ROWS[j])
                act.activation(junk[r, :], src, ACT.Square, accum_out=ss[r, ph, j:j + 1]).then_inc(sq_done, 1)
                act.wait_ge(sq_done, n + 1)
                act.activation(rt[r, ph, j:j + 1], ss[r, ph, j:j + 1], ACT.Sqrt, bias=eps[r, :], scale=1.0 / D
                               ).then_inc(rt_done, 1)

            def evacuate(ph, j, dst):
                n = NT * ph + j
                row = (0, 2, 1, 3)[ph]
                act.wait_ge(tr_done, n + 1)
                for c in range(4, KC):
                    last = act.activation(dst[:, c, tok(j)],
                                          ps[:, 5 + 2 * (j % 2), (c - 4) * P:(c - 4) * P + ROWS[j]],
                                          ACT.Copy, scale=vecT[:, c, row:row + 1])
                last.then_inc(ev_a, 1)

            def take_projection(l, func):
                for n in range(16):
                    chunk = 4 * QUARTERS[l][n // 4] + n % 4
                    act.wait_ge(mm_done, 16 * l + n + 1)
                    if l == 0 and n == 0:
                        act.wait_ge(vec_e, 3)
                        act.wait_ge(tails, 32)
                    for h in range(2):
                        last = act.activation(pT[:, chunk, h * HALF:(h + 1) * HALF],
                                              ps[:, 2 * (n % 2) + h, 0:HALF], func)
                    last.then_inc(mm_free, 1)
                    if l == 1 and n >= 8 + 1 and n - 9 < NT:
                        v_square(n - 9)

            def v_square(j):
                r = slice(0, ROWS[j])
                act.wait_ge(v_cp, j + 1)
                need(act, v_sq, j)
                act.activation(junk[r, :], xs[r, j, :], ACT.Square, accum_out=ss[r, 4, j:j + 1]).then_inc(v_sq, 1)

            def exponentials(l):
                act.wait_ge(ex_in, 2 * l + 1)
                act.activation(r4[:, 1, :, :], r4[:, 0, :, :], ACT.Exp).then_inc(ex_out, 1)
                act.wait_ge(ex_in, 2 * l + 2)
                act.activation(r1[:, 5, :], r1[:, 4, :], ACT.Exp).then_inc(ex_out, 1)

            def experts_blocks(l):
                m = moe[l]
                row = 2 + l

                def rows_T(b):
                    need(act, m["xT_mm"], b + 1)
                    for c in range(4, KC):
                        last = act.activation(xgT[:, c, :], ps[:, 6, (c - 4) * P:(c - 3) * P], ACT.Copy,
                                              scale=vecT[:, c, row:row + 1])
                    last.then_inc(m["xT_a"], 1)

                def result(b, par, stored):
                    act.wait_ge(m["y_mm"], b + 1)
                    need(act, m["st_y"][par], 16 * stored)
                    act.copy(yo[par][:, 512:1024], ps[:, 3, :]).then_inc(m["y_a"], 1)

                rows_T_first = True

                def body(b, par, i, last):
                    nonlocal rows_T_first
                    if rows_T_first:
                        rows_T(0)
                        rows_T_first = False
                    act.wait_ge(m["h1_mm"], b + 1)
                    need(act, m["hid"], b)
                    act.activation(act_g, ps[:, 0, :], ACT.Silu).then_inc(m["silu"], 1)
                    if not last:
                        act.wait_ge(m["h3_mm"], b + 1)
                        rows_T(b + 1)
                    if not (isinstance(b, int) and b == 0):
                        result(b - 1, 1 - par, (b - 1) // 2 if isinstance(b, int) else i - 1)

                pairs = run_blocks(act, l, body)
                result(2 * pairs - 1, 1, pairs - 1)

            for j in range(NT):
                act.wait_ge(ld_x[j], 16)
                if j == 0:
                    act.wait_ge(consts, 1)
                root(0, j, x[0:ROWS[j], j, :])
            act.wait_ge(vec_e, 1)
            for j in range(NT):
                evacuate(0, j, hT)
            for l in range(2):
                take_projection(l, ACT.Copy if l == 0 else ACT.Gelu_apprx_tanh)
                if l == 0:
                    act.wait_ge(ost_t, 1)
                    act.copy(ost_z, ps[0:CH + NS, 4, :]).then_inc(ost_e, 1)
                    act.wait_ge(ost_t, 2)
                    act.copy(ost_u, ps[0:PH + NS, 5, :]).then_inc(ost_e, 1)
                    act.wait_ge(ost_e, 2)
                    act.dma_start(conv_p[0, 0], ost_z[0:CH, :]).then_inc(out_st, 16)
                    act.dma_start(conv_s[0, :, CH - 1, :], ost_z[CH:CH + NS, :]).then_inc(out_st, 16)
                    act.dma_start(pool_p[0, 0], ost_u[0:PH, :]).then_inc(out_st, 16)
                    act.dma_start(pool_s[0, :, PH - 1, :], ost_u[PH:PH + NS, :]).then_inc(out_st, 16)
                    for g in range(4):
                        act.wait_ge(pool_mm, g + 1)
                        for h in range(2):
                            last = act.activation(pT[:, g, h * HALF:(h + 1) * HALF],
                                                  ps[:, 2 * (g % 2) + h, 0:HALF], ACT.Copy,
                                                  scale=vecT[:, g, 5:6])
                        last.then_inc(ya_done, 1)
                else:
                    act.wait_ge(v_sq, NT)
                    act.activation(rt[:, 4, :], ss[:, 4, :], ACT.Sqrt, bias=eps[:, :], scale=1.0 / D
                                   ).then_inc(v_rt, 1)
                    act.wait_ge(vn_done, NT)
                    act.dma_start(v_p[0, 0], xs[:, 3, :]).then_inc(out_st, 16)
                    act.dma_start(v_s[0].rearrange("b s d -> (b s) d"), xs[0:NS, 4, :]).then_inc(out_st, 16)
                ph = 2 * l + 1
                for j in range(NT):
                    act.wait_ge(x_upd, NT * l + j + 1)
                    root(ph, j, x[0:ROWS[j], j, :])
                    if j >= 1:
                        evacuate(ph, j - 1, rT)
                evacuate(ph, NT - 1, rT)
                exponentials(l)
                experts_blocks(l)
                if l == 0:
                    for j in range(NT):
                        act.wait_ge(y_add, 2 * (j + 1))
                        root(2, j, x[0:ROWS[j], j, :])
                    for j in range(NT):
                        evacuate(2, j, hT)
            for j in range(NT):
                r = slice(0, ROWS[j])
                act.wait_ge(y_add, 2 * NT + 2 * (j + 1))
                act.activation(junk[r, :], x[r, j, :], ACT.Square, accum_out=ss[r, 4, j:j + 1]).then_inc(v_sq, 1)
                act.wait_ge(v_sq, NT + j + 1)
                act.activation(rt[r, 4, j:j + 1], ss[r, 4, j:j + 1], ACT.Sqrt, bias=eps[r, :], scale=1.0 / D
                               ).then_inc(v_rt, 1)
            yp = y_prompt[0].rearrange("(j p) d -> j p d", p=P)
            for j in range(NT):
                act.wait_ge(fin_done, j + 1)
                dst = yp[j] if j < 4 else y_sample.rearrange("b s d -> (b s) d")
                act.dma_start(dst, x[0:ROWS[j], j, :]).then_inc(fin_st, 16)
            act.wait_ge(fin_st, 16 * NT)
            act.wait_ge(out_st, 16 * 6)
            act.wait_ge(state_st, 32)

        @block.vector
        def _(dve):
            step = Chain(dve, dve_step)

            def scale_rows(ph, j):
                n = NT * ph + j
                r = slice(0, ROWS[j])
                dve.wait_ge(rt_done, n + 1)
                dve.reciprocal(rs[r, ph, j:j + 1], rt[r, ph, j:j + 1]).then_inc(rc_done, 1)
                dve.wait_ge(rc_done, n + 1)
                dve.tensor_scalar(xs[r, j, :], x[r, j, :], rs[r, ph, j:j + 1], None, ALU.mult
                                  ).then_inc(xs_done, 1)

            def gain(row, n):
                return vecT[:, 0:4, row:row + 1].to_broadcast([P, 4, n])

            def evacuate(ph, j, dst):
                n = NT * ph + j
                row = (0, 2, 1, 3)[ph]
                dve.wait_ge(tr_done, n + 1)
                src = ps[:, 4 + 2 * (j % 2), :].rearrange("p (c t) -> p c t", c=4)[:, :, 0:ROWS[j]]
                dve.tensor_tensor(dst[:, 0:4, tok(j)], src, gain(row, ROWS[j]), ALU.mult).then_inc(ev_d, 1)

            def bc(ap, shape):
                return ap.to_broadcast(shape)

            def first_best(src, best, eq, onehot, mask=None):
                s = [P, NT, 4]
                step(dve.tensor_reduce(best, src, AX_X, ALU.max))
                step(dve.tensor_tensor(eq, src, bc(best.unsqueeze(2), s), ALU.is_equal))
                step(dve.tensor_tensor(eq, eq, bc(pri[:, :].unsqueeze(1), s), ALU.mult))
                step(dve.tensor_reduce(r1[:, 11, :], eq, AX_X, ALU.max))
                step(dve.tensor_tensor(onehot, eq, bc(r1[:, 11, :].unsqueeze(2), s), ALU.is_equal))

            def route(l):
                s4 = [P, NT, 4]
                s16 = [P, NT, 4, 4]
                goh, oh1, oh2 = ohs[:, 0, :, :], ohs[:, 1, :, :], ohs[:, 2, :, :]
                lgg, lge = lg[:, :, 0:NG], lg[:, :, NG:]
                first_best(lgg, r1[:, 0, :], r4[:, 2, :, :], goh)
                step(dve.tensor_tensor(goh, goh, bc(valid[:, :].unsqueeze(2), s4), ALU.mult))
                dve.tensor_tensor(r4[:, 0, :, :], lgg, bc(r1[:, 0, :].unsqueeze(2), s4), ALU.subtract
                                  ).then_inc(ex_in, 1)
                t16 = r16[:, 0, :, :].rearrange("p t (g j) -> p t g j", g=NG)
                lge4 = lge.rearrange("p t (g j) -> p t g j", g=NG)
                step(dve.tensor_tensor(t16, lge4, bc(goh.unsqueeze(3), s16), ALU.mult))
                le = r4[:, 3, :, :]
                step(dve.tensor_reduce(le, r16[:, 0, :, :].rearrange("p t (g j) -> p t j g", g=NG), AX_X, ALU.add))
                first_best(le, r1[:, 1, :], r4[:, 2, :, :], oh1)
                step(dve.scalar_tensor_tensor(out=le, in0=oh1, scalar=BIG, in1=le, op0=ALU.mult, op1=ALU.add))
                first_best(le, r1[:, 2, :], r4[:, 2, :, :], oh2)
                dve.tensor_tensor(r1[:, 4, :], r1[:, 2, :], r1[:, 1, :], ALU.subtract).then_inc(ex_in, 1)
                A1, A2, A = (r16[:, k, :, :] for k in (0, 1, 2))
                for k, oh in ((0, oh1), (1, oh2)):
                    step(dve.tensor_tensor(r16[:, k, :, :].rearrange("p t (g j) -> p t g j", g=NG),
                                           bc(goh.unsqueeze(3), s16), bc(oh.unsqueeze(2), s16), ALU.mult))
                dve.tensor_tensor(A, A1, A2, ALU.add).then_inc(rank_in, 1)
                dve.wait_ge(ex_out, 2 * l + 2)
                step(dve.tensor_reduce(r1[:, 6, :], r4[:, 1, :, :], AX_X, ALU.add))
                step(dve.reciprocal(r1[:, 7, :], r1[:, 6, :]))
                step(dve.tensor_scalar(r1[:, 8, :], r1[:, 5, :], 1.0, None, ALU.add))
                step(dve.reciprocal(r1[:, 9, :], r1[:, 8, :]))
                step(dve.tensor_tensor(gates[:, 0, :], r1[:, 7, :], r1[:, 9, :], ALU.mult))
                step(dve.tensor_tensor(gates[:, 1, :], gates[:, 0, :], r1[:, 5, :], ALU.mult))
                dve.wait_ge(rank_mm, l + 1)
                cnt, csum, xoff, ov, ocs, oex, big, dlt, xo2, zz = (c16[:, k, :] for k in range(10))
                step(dve.tensor_copy(cnt, ps[:, 5, 0:NE]))
                step(dve.memset(zz, 0.0))
                step(dve.tensor_tensor_scan(csum, cnt, zz, 0.0, ALU.add, ALU.add))
                step(dve.tensor_tensor(xoff, csum, cnt, ALU.subtract))
                th = over[:, 0:4, :].rearrange("p a e -> p (a e)").rearrange("p (e a) -> p e a", e=NE)
                step(dve.tensor_tensor(th, bc(cnt.unsqueeze(2), [P, NE, 4]),
                                       bc(thr[:, :].unsqueeze(1), [P, NE, 4]), ALU.is_gt))
                step(dve.tensor_reduce(ov, th, AX_X, ALU.add))
                step(dve.tensor_tensor_scan(ocs, ov, zz, 0.0, ALU.add, ALU.add))
                step(dve.tensor_tensor(oex, ocs, ov, ALU.subtract))
                step(dve.tensor_scalar(big, oex, float(NE - 1), float(P), ALU.add, ALU.mult))
                step(dve.scalar_tensor_tensor(out=dlt, in0=eidx[:, :], scalar=float(P), in1=big,
                                              op0=ALU.mult, op1=ALU.subtract))
                sE = [P, NT, NE]
                R, xr, yr = r16[:, 3, :, :], r16[:, 4, :, :], r16[:, 2, :, :]
                step(dve.tensor_copy(R, ps[:, 4, 0:NT * NE].rearrange("p (t e) -> p t e", t=NT)))
                step(dve.tensor_tensor(xr, R, bc(xoff.unsqueeze(1), sE), ALU.add))
                step(dve.tensor_scalar(yr, R, float(P), None, ALU.is_lt))
                step(dve.tensor_tensor(yr, yr, bc(dlt.unsqueeze(1), sE), ALU.mult))
                step(dve.tensor_tensor(yr, yr, R, ALU.add))
                step(dve.tensor_tensor(yr, yr, bc(big.unsqueeze(1), sE), ALU.add))
                for n, (rows, sel) in enumerate(((xr, A1), (xr, A2), (yr, A1), (yr, A2))):
                    step(dve.tensor_tensor(R, rows, sel, ALU.mult))
                    step(dve.tensor_reduce(slots_f[:, n, :], R, AX_X, ALU.add))
                step(dve.tensor_copy(slots[:, :, :], slots_f[:, :, :]))
                sO = [P, MAX_OVER, NE]
                jb = bc(jidx[:, :].unsqueeze(2), sO)
                step(dve.tensor_tensor(over[:, :, :], bc(oex.unsqueeze(1), sO), jb, ALU.is_le))
                step(dve.tensor_tensor(over2[:, :, :], bc(ocs.unsqueeze(1), sO), jb, ALU.is_gt))
                step(dve.tensor_tensor(over[:, :, :], over[:, :, :], over2[:, :, :], ALU.mult))
                step(dve.tensor_tensor(over2[:, :, :], over[:, :, :], bc(eidx[:, :].unsqueeze(1), sO), ALU.mult))
                step(dve.tensor_reduce(table_f[:, NE:NE + MAX_OVER], over2[:, :, :], AX_X, ALU.add))
                step(dve.scalar_tensor_tensor(out=xo2, in0=oex, scalar=-float(P), in1=xoff,
                                              op0=ALU.mult, op1=ALU.add))
                step(dve.tensor_tensor(over2[:, :, :], over[:, :, :], bc(xo2.unsqueeze(1), sO), ALU.mult))
                step(dve.tensor_reduce(o8[:, 0, :], over2[:, :, :], AX_X, ALU.add))
                step(dve.tensor_reduce(o8[:, 1, :], over[:, :, :], AX_X, ALU.add))
                step(dve.tensor_scalar(o8[:, 2, :], jidx[:, :], 1.0, float(P), ALU.add, ALU.mult))
                step(dve.tensor_tensor(o8[:, 3, :], o8[:, 1, :], o8[:, 2, :], ALU.mult))
                step(dve.tensor_tensor(table_f[:, TABLE + NE:TABLE + MAX_BLOCKS], o8[:, 0, :], o8[:, 3, :], ALU.add))
                step(dve.tensor_copy(table_f[:, 0:NE], eidx[:, :]))
                step(dve.tensor_copy(table_f[:, TABLE:TABLE + NE], xoff))
                step(dve.tensor_tensor(o8[:, 0, 0:4], bc(ocs[:, NE - 1:NE], [P, 4]), thr2[:, :], ALU.is_gt))
                step(dve.tensor_reduce(table_f[:, 2 * TABLE:], o8[:, 0, 0:4], AX_X, ALU.add))
                dve.tensor_copy(table[:, :], table_f[:, :]).then_inc(slots_ok, 1)

            def experts_blocks(l):
                m = moe[l]

                def rows_T(b):
                    need(dve, m["xT_mm"], b + 1)
                    src = ps[:, 5, :].rearrange("p (c s) -> p c s", c=4)
                    dve.tensor_tensor(xgT[:, 0:4, :], src, gain(2 + l, P), ALU.mult).then_inc(m["xT_d"], 1)

                def hidden_T(b):
                    dve.wait_ge(m["hT_mm"], b + 1)
                    need(dve, m["y_mm"], b)
                    dve.tensor_copy(hidT.rearrange("p c s -> p (c s)"), ps[:, 4, :]).then_inc(m["hT_e"], 1)

                def result(b, par, stored):
                    dve.wait_ge(m["y_mm"], b + 1)
                    need(dve, m["st_y"][par], 16 * stored)
                    dve.tensor_copy(yo[par][:, 0:512], ps[:, 2, :]).then_inc(m["y_d"], 1)

                started = False

                def body(b, par, i, last):
                    nonlocal started
                    first = isinstance(b, int) and b == 0
                    if not started:
                        rows_T(0)
                        started = True
                    if not first:
                        hidden_T(b - 1)
                    dve.wait_ge(m["silu"], b + 1)
                    dve.wait_ge(m["h3_mm"], b + 1)
                    need(dve, m["hT_mm"], b)
                    dve.tensor_tensor(hid, act_g, ps[:, 1, :], ALU.mult).then_inc(m["hid"], 1)
                    if not last:
                        rows_T(b + 1)
                    if not first:
                        result(b - 1, 1 - par, (b - 1) // 2 if isinstance(b, int) else i - 1)

                pairs = run_blocks(dve, l, body)
                hidden_T(2 * pairs - 1)
                result(2 * pairs - 1, 1, pairs - 1)

            def combine(l, j):
                r = slice(0, ROWS[j])
                dve.wait_ge(ld_y[l][j], 32)
                for k in range(2):
                    n = 2 * NT * l + 2 * j + k
                    if k:
                        dve.wait_ge(y_add, n)
                    dve.scalar_tensor_tensor(out=x[r, j, :], in0=yg[(2 * j + k) % 8][r, :],
                                             scalar=gates[r, k, j:j + 1], in1=x[r, j, :],
                                             op0=ALU.mult, op1=ALU.add).then_inc(y_add, 1)

            def add_projection(l, j):
                r = slice(0, ROWS[j])
                dve.wait_ge(wo_done, NT * l + j + 1)
                dve.tensor_tensor(x[r, j, :], x[r, j, :], bank2(2 * (j % 2))[r, :], ALU.add).then_inc(x_upd, 1)

            def logits(l, j):
                r = slice(0, ROWS[j])
                dve.wait_ge(lg_mm, NT * l + j + 1)
                dve.tensor_tensor(lg[r, j, :], ps[r, (4, 6)[j % 2], 0:NG + NE], br[r, l, :], ALU.add
                                  ).then_inc(lg_done, 1)

            def after_projection(l):
                ph = 2 * l + 1
                for j in range(NT):
                    add_projection(l, j)
                    if j >= 1:
                        scale_rows(ph, j - 1)
                        evacuate(ph, j - 1, rT)
                    if j >= 2:
                        logits(l, j - 2)
                scale_rows(ph, NT - 1)
                evacuate(ph, NT - 1, rT)
                logits(l, NT - 2)
                logits(l, NT - 1)
                dve.wait_ge(lg_done, NT * (l + 1))
                route(l)

            dve.wait_ge(consts, 1)
            dve.wait_ge(vec_t, 1)
            dve.tensor_copy(vecT[:, :, :].rearrange("p c v -> p (c v)"), ps[:, 0, 0:KC * NV]).then_inc(vec_e, 1)
            for j in range(NT):
                dve.wait_ge(ld_x[j], 16)
                scale_rows(0, j)
                if j >= 1:
                    if j == 1:
                        dve.wait_ge(vec_e, 1)
                    evacuate(0, j - 1, hT)
            evacuate(0, NT - 1, hT)
            dve.wait_ge(vec_t, 2)
            step(dve.tensor_copy(histT.rearrange("p g b t -> p (g b t)"), ps[:, 1, 0:4 * NS * PH]))
            dve.tensor_copy(chistT.rearrange("p g b t -> p (g b t)"),
                            ps[:, 0, 256:256 + 4 * NS * CH]).then_inc(vec_e, 1)
            dve.wait_ge(vec_t, 3)
            dve.tensor_tensor(wsT[:, :, :], ps[:, 2:4, :].rearrange("p b (h t) -> p (b h) t", h=4),
                              bc(upto[:, :].unsqueeze(1), [P, NH, P]), ALU.mult).then_inc(vec_e, 1)
            dve.wait_ge(ld_small, 16 * 8)
            step(dve.tensor_tensor(wdiag[:, :, :], bc(ident[0:NS, 0:NS].unsqueeze(1), [NS, NH, NS]),
                                   bc(w00[:, :].unsqueeze(2), [NS, NH, NS]), ALU.mult))
            step(dve.memset(rcnt[:, :, :], 1.0))
            for g, win in enumerate(WINDOWS):
                for t in range(win):
                    dve.memset(rcnt[:, g, t:t + 1], 1.0 / (t + 1))
                if win < 16:
                    dve.memset(rcnt[:, g, win:16], 1.0 / win)
            step(dve.memset(sumA[:, 0:16], 0.0))
            step(dve.memset(sumB[:, 0:16], 0.0))

            for g in range(4):
                dve.wait_ge(mm_free, 4 + g + 1)
                z, acc = pT[:, 12 + g, :], pT[:, 8 + g, :]
                dve.tensor_tensor(z, acc, z, ALU.mult).then_inc(z_done, 1)
                dve.wait_ge(z_done, g + 1)
                cw = [vecT[:, g, 6 + k:7 + k] for k in range(3)]
                step(dve.tensor_scalar(acc, z, cw[2], None, ALU.mult))
                for k, back in ((1, 1), (0, 2)):
                    step(dve.scalar_tensor_tensor(out=acc[:, back:SEQ], in0=z[:, 0:SEQ - back], scalar=cw[k],
                                                  in1=acc[:, back:SEQ], op0=ALU.mult, op1=ALU.add))
                    step(dve.scalar_tensor_tensor(out=acc[:, SEQ:T], in0=chistT[:, g, :, k], scalar=cw[k],
                                                  in1=acc[:, SEQ:T], op0=ALU.mult, op1=ALU.add))
            for g, win in enumerate(WINDOWS):
                dve.wait_ge(mm_free, 8 + g + 1)
                u = pT[:, g, :]
                cur, nxt = sumA, sumB
                step(dve.tensor_copy(cur[:, 16:17], u[:, 0:1]))
                step(dve.tensor_tensor(cur[:, 17:16 + SEQ], u[:, 1:SEQ], u[:, 0:SEQ - 1], ALU.add))
                for k in range(1, g + 1):
                    back = 2 ** k
                    step(dve.tensor_tensor(nxt[:, 16:16 + SEQ], cur[:, 16:16 + SEQ],
                                           cur[:, 16 - back:16 + SEQ - back], ALU.add))
                    cur, nxt = nxt, cur
                step(dve.scalar_tensor_tensor(out=dif[:, g, 16:SEQ], in0=cur[:, 32:16 + SEQ], scalar=1.0 / win,
                                              in1=u[:, 16:SEQ], op0=ALU.mult, op1=ALU.subtract))
                step(dve.tensor_tensor(head[:, g, :], cur[:, 16:32], rcnt[:, g, :], ALU.mult))
                step(dve.tensor_tensor(dif[:, g, 0:16], head[:, g, :], u[:, 0:16], ALU.subtract))
                step(dve.tensor_reduce(hs[:, g, :], histT[:, g, :, PH - win + 1:PH], AX_X, ALU.add))
                step(dve.tensor_tensor(hs2[:, g, :], hs[:, g, :], u[:, SEQ:T], ALU.add))
                dve.scalar_tensor_tensor(out=dif[:, g, SEQ:T], in0=hs2[:, g, :], scalar=1.0 / win,
                                         in1=u[:, SEQ:T], op0=ALU.mult, op1=ALU.subtract).then_inc(dif_done, 1)
            for g in range(4):
                dve.wait_ge(mm_free, 12 + g + 1)
                dve.tensor_tensor(pT[:, 4 + g, :], pT[:, 4 + g, :], pT[:, 8 + g, :], ALU.mult).then_inc(yb_done, 1)
            dve.wait_ge(out_st, 16 * 4)
            after_projection(0)
            experts_blocks(0)
            for j in range(NT):
                combine(0, j)
                if j >= 1:
                    scale_rows(2, j - 1)
            scale_rows(2, NT - 1)
            for j in range(NT):
                evacuate(2, j, hT)

            for j in range(NT):
                r = slice(0, ROWS[j])
                dve.wait_ge(vt_done, j + 1)
                dve.tensor_copy(xs[r, j, :], bank2(4 + 2 * (j % 2))[r, :]).then_inc(v_cp, 1)
            dve.wait_ge(v_rt, 1)
            step(dve.reciprocal(rs[:, 4, :], rt[:, 4, :]))
            dve.wait_ge(ld_g[0], 16)
            for j in range(NT):
                r = slice(0, ROWS[j])
                dve.scalar_tensor_tensor(out=xs[r, j, :], in0=xs[r, j, :], scalar=rs[r, 4, j:j + 1],
                                         in1=g_sgu[r, :], op0=ALU.mult, op1=ALU.mult).then_inc(vn_done, 1)
            dve.wait_ge(ld_g[1], 16)
            dve.wait_ge(mm_free, 32)
            for j in range(NT):
                dve.wait_ge(mix_mm, j + 1)
                n = ROWS[j]
                mixed = ps[:, 4 + 2 * (j % 2):6 + 2 * (j % 2), :].rearrange("p b (h t) -> p (b h) t", h=4)[:, :, 0:n]
                bias = b_bc if j < 4 else bc(b_bc[:, :, 0:1], [P, NH, n])
                mx = arena_a[:, 8 * T + (j % 2) * 1024:8 * T + (j % 2 + 1) * 1024].rearrange(
                    "p (h t) -> p h t", h=NH)[:, :, 0:n]
                step(dve.tensor_tensor(mx, mixed, bias, ALU.add))
                dve.tensor_tensor(pT[:, 0:8, tok(j)], pT[:, 0:8, tok(j)], mx, ALU.mult).then_inc(mix_done, 1)
            dve.wait_ge(out_st, 16 * 6)
            after_projection(1)
            experts_blocks(1)
            dve.wait_ge(ld_g[2], 16)

            def finish(j):
                r = slice(0, ROWS[j])
                dve.wait_ge(v_rt, 1 + j + 1)
                step(dve.reciprocal(rs[r, 4, j:j + 1], rt[r, 4, j:j + 1]))
                dve.scalar_tensor_tensor(out=x[r, j, :], in0=x[r, j, :], scalar=rs[r, 4, j:j + 1],
                                         in1=g_fin[r, :], op0=ALU.mult, op1=ALU.mult).then_inc(fin_done, 1)

            for j in range(NT):
                combine(1, j)
                if j >= 1:
                    finish(j - 1)
            finish(NT - 1)


_INS = ["x_prompt", "x_sample", "state_pool", "state_conv", "norm_mix", "w_in_even", "w_pool", "pool_scale",
        "conv_w", "w_out_even", "w_in_odd", "sgu_norm", "w_sgu", "b_sgu", "w_out_odd", "norm_ffn",
        "w_router_group", "b_router_group", "w_router_expert", "b_router_expert", "w_gate", "w_up", "w_down",
        "norm_final"]
_OUTS = [(1, 512, 1024), (8, 1, 1024), (1, 1, 15, 512), (1, 8, 15, 512), (1, 1, 2, 512), (1, 8, 2, 512),
         (1, 1, 128, 1024), (1, 8, 1, 1024)]


def kernel(**inputs):
    import numpy as _np
    import concourse.bacc as _bacc
    from concourse import mybir as _mybir
    from concourse.bass_utils import run_bass_kernel_spmd as _run

    nc = _bacc.Bacc("TRN2", target_bir_lowering=False, num_devices=1)
    arrays, args = {}, []
    for name in _INS:
        a = _np.ascontiguousarray(inputs[name])
        arrays[f"in_{name}"] = a
        args.append(nc.dram_tensor(f"in_{name}", a.shape, _mybir.dt.from_np(a.dtype), kind="ExternalInput").ap())
    for i, shape in enumerate(_OUTS):
        args.append(nc.dram_tensor(f"out_{i}", shape, _mybir.dt.float32, kind="ExternalOutput").ap())
    trunk(nc, *args)
    r = _run(nc, [arrays], core_ids=[0])
    return tuple(r.results[0][f"out_{i}"] for i in range(len(_OUTS)))
```

```python
from contextlib import ExitStack

import concourse.bass as bass
from concourse import mybir

F32 = mybir.dt.float32
F32R = mybir.dt.float32r
BF16 = mybir.dt.bfloat16
I32 = mybir.dt.int32
U32 = mybir.dt.uint32
ALU = mybir.AluOpType
ACT = mybir.ActivationFunctionType
AX_X = mybir.AxisListType.X

P = 128
D = 1024
SEQ = 512
NS = 8
T = SEQ + NS
PARTS = [(0, 2 * P), (2 * P, T)]
NT = 5
ROWS = [P, P, P, P, NS]
KC = D // P
NG, EPG = 4, 4
NE = NG * EPG
DE = 512
FC = DE // P
PH, CH = 15, 2
WINDOWS = (2, 4, 8, 16)
NH = 8
EPS = 1e-6
MAX_OVER = 8
MAX_BLOCKS = NE + MAX_OVER
TABLE = MAX_BLOCKS + 2
BIG = -3.0e38


def need(eng, sem, count):
    if isinstance(count, int) and count <= 0:
        return
    eng.wait_ge(sem, count)


class Chain:

    def __init__(self, eng, sem):
        self.eng, self.sem, self.n = eng, sem, 0

    def __call__(self, ins):
        self.n += 1
        ins.then_inc(self.sem, 1)
        self.eng.wait_ge(self.sem, self.n)


def trunk(nc, x_prompt, x_sample, state_pool, state_conv, norm_mix, w_in_even, w_pool, pool_scale,
          conv_w, w_out_even, w_in_odd, sgu_norm, w_sgu, b_sgu, w_out_odd, norm_ffn, w_rg, b_rg,
          w_re, b_re, w_gate, w_up, w_down, norm_final, y_prompt, y_sample, pool_p, pool_s,
          conv_p, conv_s, v_p, v_s):
    with ExitStack() as ctx:
        def sb(name, shape, dt=F32):
            return ctx.enter_context(nc.sbuf_tensor(name, shape, dt))

        def sb_split(name, shape):
            offset = (nc.sbuf_base + 31) // 32 * 32
            full = sb(name, shape)
            return full, nc.alloc_sbuf_tensor_at(name + "_r", shape, F32R, offset=offset)

        def sem(name):
            return ctx.enter_context(nc.semaphore(name))

        def dram(name, shape):
            return nc.dram_tensor(name, shape, F32, kind="Internal").ap()

        xrows = dram("xrows", (T, D))
        yrows = dram("yrows", (MAX_BLOCKS * P, D))

        wpair = [[sb_split(f"wbuf_{k}{p}", [P, KC * T if (k, p) == ("gate", 1) else 4096])
                  for p in range(2)] for k in ("gate", "up", "down")]
        wbuf = [[full for full, _ in pair] for pair in wpair]
        wbuf_r = [[rounded for _, rounded in pair] for pair in wpair]
        x = sb("x", [P, NT, D])
        arena_a, arena_a_r = sb_split("arena_a", [P, 16 * T])
        arena_b, arena_b_r = sb_split("arena_b", [P, KC * T])
        arena_c, arena_c_r = sb_split("arena_c", [P, NT * D])
        ident = sb("ident", [P, P])
        upto = sb("upto", [P, P])
        ones = sb("ones", [P, P])
        ones_b = sb("ones_b", [P, P], BF16)
        before_b = sb("before_b", [P, P], BF16)
        pairs_b = sb("pairs_b", [P, NT, NE], BF16)
        wsT = sb("wsT", [P, NH, P])
        w00 = sb("w00", [NS, NH])
        wdiag = sb("wdiag", [NS, NH, NS])
        NV = 9
        vecT = sb("vecT", [P, KC, NV])
        wr = sb("wr", [P, 2, KC, NG + NE])
        br = sb("br", [P, 2, NG + NE])
        per_layer = sb("per_layer", [P, 4 * P + 4 * NS * (PH + CH)])
        wpool_sb = per_layer[:, 0:512].rearrange("p (g d) -> p g d", g=4)
        histT = per_layer[:, 512:992].rearrange("p (g b t) -> p g b t", g=4, b=NS)
        chistT = per_layer[:, 992:1056].rearrange("p (g b t) -> p g b t", g=4, b=NS)
        g_sgu = per_layer[:, 0:D]
        eps = sb("eps", [P, 1])
        ss = sb("ss", [P, 5, NT])
        rt = sb("rt", [P, 5, NT])
        rs = sb("rs", [P, 5, NT])
        lg = sb("lg", [P, NT, NG + NE])
        lg2 = sb("lg2", [P, NT * 5, 4])
        eq = sb("eq", [P, NT * 5, 4])
        oh = sb("oh", [P, 2, NT, 5, 4])
        goh = sb("goh", [P, NT, NG])
        best = sb("best", [P, 3, NT * 5])
        ex = sb("ex", [P, NT, 2 * NG])
        ex2 = sb("ex2", [P, NT, NG])
        r1 = sb("r1", [P, 5, NT])
        sel = sb("sel", [P, 2, NT, NE])
        prod = sb("prod", [P, 2, NT, NE])
        rows = sb("rows", [P, NT, NE])
        rank1 = sb("rank1", [P, NT, NE])
        count1 = sb("count1", [P, P])
        tok_id = sb("tok_id", [P, NT, 2], BF16)
        onehot = sb("onehot", [P, 2, NT, P], BF16)
        junk = onehot[:, :, :, :].rearrange("p a j s -> p (a j s)")[:, 0:D]
        ids_f = sb("ids_f", [P, 2])
        ids = sb("ids", [P, 2], U32)
        c16 = sb("c16", [P, 5, NE])
        zero16 = sb("zero16", [P, NE])
        over = prod[:, :, :, :].rearrange("p k t e -> p (k t) e")[:, 0:MAX_OVER, :]
        over2 = sb("over2", [P, MAX_OVER, NE])
        o8 = sb("o8", [P, 4, MAX_OVER])
        slots_f = sb("slots_f", [P, 2, NT])
        slots = sb("slots", [P, 2, NT], U32)
        gates = sb("gates", [P, 2, NT])
        pri = sb("pri", [P, 4])
        eidx = sb("eidx", [P, NE])
        jidx = sb("jidx", [P, MAX_OVER])
        thr = sb("thr", [P, 4])
        thr2 = sb("thr2", [P, 4])
        valid = sb("valid", [P, NT])
        table_f = sb("table_f", [P, 2 * TABLE + 1])
        table = sb("table", [P, 2 * TABLE + 1], I32)
        rcnt = sb("rcnt", [P, 4, 16])
        hs = sb("hs", [P, 4, NS])
        hs2 = sb("hs2", [P, 4, NS])
        head = rows[:, 0:4, :]

        pT = arena_a[:, :].rearrange("p (m t) -> p m t", m=16)
        raw = arena_a
        raw_ws = raw[:, 0:1024].rearrange("p (h s) -> p h s", h=NH)
        raw_vec = raw[0:NV, 1024:2048]
        raw_hist = raw[0:NS * PH, 2048:2560]
        raw_chist = raw[0:NS * CH, 2560:3072]
        rT = arena_a[:, 0:KC * T].rearrange("p (c t) -> p c t", c=KC)
        xg = [arena_a[:, k * D:(k + 1) * D] for k in range(2)]
        xgT = arena_a[:, 2048:3072].rearrange("p (c s) -> p c s", c=KC)
        act_g = arena_a[:, 3072:3584]
        hid = arena_a[:, 3584:4096]
        hidT_lo = arena_a_r[:, 4096:4608]
        hidT = arena_a[:, 4096:4608]
        yg = [arena_a[:, k * D:(k + 1) * D] for k in range(8)]
        hT = arena_b[:, :].rearrange("p (c t) -> p c t", c=KC)
        yo = [arena_b[:, k * D:(k + 1) * D] for k in range(2)]
        g_fin = arena_b[:, 2048:3072]
        hT_lo = arena_b_r[:, :].rearrange("p (c t) -> p c t", c=KC)
        hT_hi = wbuf_r[0][1][:, :].rearrange("p (c t) -> p c t", c=KC)
        pT_r = arena_a_r[:, :].rearrange("p (m t) -> p m t", m=16)
        pT_hi = [[pT_r[:, 12 + c if c < 4 else 4 + c, :] for c in range(KC)],
                 [hT_lo[:, c, :] for c in range(KC)]]
        b_bc = arena_a[:, 8 * T + 2048:8 * T + 3072].rearrange("p (h t) -> p h t", h=NH)
        xs = arena_c[:, :].rearrange("p (j d) -> p j d", j=NT)
        down_hi = arena_c_r[:, 0:4096]
        hidT_hi = arena_c_r[:, 4096:4608]
        sumA = arena_c[:, 0:16 + SEQ]
        sumB = arena_c[:, 528:1056 + 0]
        dif = arena_c[:, 1056:1056 + 4 * T].rearrange("p (g t) -> p g t", g=4)
        ost_u = arena_c[0:PH + NS, 3136:3136 + 512]
        ost_z = arena_c[0:CH + NS, 3648:3648 + 512]
        zeros = arena_c[:, 4608:5120]

        ps = ctx.enter_context(nc.psum_tensor("ps", [P, 8, 512], F32))

        def bank2(b):
            return ps[:, b:b + 2, :].rearrange("p b n -> p (b n)")

        ld_x = [sem(f"ld_x{j}") for j in range(NT)]
        ld_vec, ld_hist, ld_ws, ld_small = sem("ld_vec"), sem("ld_hist"), sem("ld_ws"), sem("ld_small")
        ld_g = [sem("ld_gsgu"), sem("ld_bsgu"), sem("ld_gfin")]
        ld_in = [[sem(f"ld_in{l}{q}") for q in range(4)] for l in range(2)]
        ld_out = [[sem(f"ld_out{l}{h}") for h in range(2)] for l in range(2)]
        ld_w = [[[sem(f"ld_w{l}{k}{p}") for p in range(2)] for k in range(3)] for l in range(2)]
        const_step, consts = sem("const_step"), sem("consts")
        dve_step = sem("dve_step")
        tails = sem("tails")
        vec_t, vec_e = sem("vec_t"), sem("vec_e")
        sq_done, rt_done, rc_done, xs_done = sem("sq_done"), sem("rt_done"), sem("rc_done"), sem("xs_done")
        tr_done, ev_d, ev_a = sem("tr_done"), sem("ev_d"), sem("ev_a")
        mm_done, mm_free = sem("mm_done"), sem("mm_free")
        tile_hi, tile_lo, w_hi, w_lo = sem("tile_hi"), sem("tile_lo"), sem("w_hi"), sem("w_lo")
        wo_hi, wo_lo, p_hi, p_lo = sem("wo_hi"), sem("wo_lo"), sem("p_hi"), sem("p_lo")
        z_done, conv_done, dif_done, yb_done = sem("z_done"), sem("conv_done"), sem("dif_done"), sem("yb_done")
        pool_mm, ya_done = sem("pool_mm"), sem("ya_done")
        ost_t, ost_e = sem("ost_t"), sem("ost_e")
        wo_done, x_upd = sem("wo_done"), sem("x_upd")
        vt_done, v_cp, v_sq, v_rt, vn_done = sem("vt_done"), sem("v_cp"), sem("v_sq"), sem("v_rt"), sem("vn_done")
        mix_mm, mix_done = sem("mix_mm"), sem("mix_done")
        out_st, state_st = sem("out_st"), sem("state_st")
        lg_mm, lg_done = sem("lg_mm"), sem("lg_done")
        ex_in, ex_out = sem("ex_in"), sem("ex_out")
        rank_in, rank_mm, slots_ok, xs_st = sem("rank_in"), sem("rank_mm"), sem("slots_ok"), sem("xs_st")
        table_ok = sem("table_ok")
        moe = []
        for l in range(2):
            moe.append({k: sem(f"m{l}_{k}") for k in (
                "onehot", "id_mm", "ids_f", "ids", "xT_mm", "xT_d", "xT_a", "h1_mm", "silu", "h3_mm", "hid", "hT_mm", "hT_hi", "hT_e",
                "dn_hi", "dn_lo",
                "y_mm", "y_d", "y_a")})
            moe[l]["turn"] = sem(f"m{l}_turn")
            moe[l]["ld_x"] = [sem(f"m{l}_ld_x{p}") for p in range(2)]
            moe[l]["st_y"] = [sem(f"m{l}_st_y{p}") for p in range(2)]
        ld_y = [[sem(f"ld_y{l}{j}") for j in range(NT)] for l in range(2)]
        y_add, results_in = sem("y_add"), sem("results_in")
        fin_done, fin_st = sem("fin_done"), sem("fin_st")

        QUARTERS = [[2, 3, 0, 1], [2, 3, 0, 1]]
        quarter_buf = [wbuf[0][0], wbuf[1][0], wbuf[0][0], wbuf[1][0]]
        quarter_lo = [wbuf_r[0][0], wbuf_r[1][0], wbuf_r[0][0], wbuf_r[1][0]]
        chunk_hi = wbuf_r[1][1][:, :].rearrange("p (m c n) -> p m c n", m=4, c=KC)
        half_buf = [wbuf[2][0], wbuf[2][1]]
        half_lo = [wbuf_r[2][0], wbuf_r[2][1]]
        half_hi = [wbuf_r[0][0], wbuf_r[1][1]]
        OUT_ORDER = [[0, 4, 1, 5, 2, 6, 3, 7], list(range(KC))]
        POOL_AFTER, POOL_BANK = [26, 28, 29, 31], [6, 4, 6, 4]
        PRODUCTS = ([(0, m, t) for t in range(2) for m in range(4)]
                    + [(q, m, t) for q in range(1, 4) for m in range(4) for t in range(2)])

        def tok(j):
            return slice(j * P, j * P + ROWS[j])

        def in_cols(w, q):
            return w[0].rearrange("(c p) n -> p c n", p=P)[:, :, q * 512:(q + 1) * 512]

        def as_kn(buf, k):
            return buf[:, 0:4096].rearrange("p (c n) -> p c n", c=k)

        def chunk_of(buf, m):
            return as_kn(buf, KC)[:, :, m * P:(m + 1) * P]

        def piece_of(buf, p):
            return as_kn(buf, KC)[:, 2 * p:2 * p + 2, :]

        def after_products(c):
            return 2 * c - 4

        def expert_view(w, l):
            return w[l].rearrange("e (c p) n -> e p c n", p=P)

        experts = [[expert_view(w, l) for w in (w_gate, w_up, w_down)] for l in range(2)]

        def load_pairs(eng):
            return NE // 2 + eng.value_load(table[0:1, 2 * TABLE:2 * TABLE + 1], min_val=0,
                                            max_val=MAX_OVER // 2)

        def run_blocks(eng, l, body):
            eng.wait_ge(table_ok, l + 1)
            pairs = load_pairs(eng)
            for b in range(3):
                body(b, b % 2, b, False)
            with eng.Fori(2, pairs) as i:
                body(2 * i - 1, 1, i, False)
                body(2 * i, 0, i, False)
            body(2 * pairs - 1, 1, pairs, True)
            return pairs

        def before_same(b, par, i):
            return b // 2 if isinstance(b, int) else (i - 1 if par == 1 else i)

        block = ctx.enter_context(nc.Block())

        def small_loads(sp):
            sp.dma_start(raw_hist, state_pool[0].rearrange("b t c -> (b t) c")).then_inc(ld_hist, 16)
            sp.dma_start(raw_chist, state_conv[0].rearrange("b t c -> (b t) c")).then_inc(ld_hist, 16)
            sp.dma_start(raw_ws, w_sgu[0].rearrange("h t s -> t h s")).then_inc(ld_ws, 16)
            sp.dma_start(wpool_sb[:, :, :], w_pool[0].rearrange("g c d -> c g d")).then_inc(ld_small, 16)
            for l in range(2):
                sp.dma_start(wr[:, l, :, 0:NG], w_rg[l].rearrange("(c p) e -> p c e", p=P)).then_inc(ld_small, 16)
                sp.dma_start(wr[:, l, :, NG:], w_re[l].rearrange("(c p) e -> p c e", p=P)).then_inc(ld_small, 16)
            sp.dma_start(br[:, :, 0:NG], b_rg.partition_broadcast(P)).then_inc(ld_small, 16)
            sp.dma_start(br[:, :, NG:], b_re.partition_broadcast(P)).then_inc(ld_small, 16)
            sp.dma_start(w00[:, :], w_sgu[0, :, 0, 0:1].rearrange("h a -> (h a)").partition_broadcast(NS),
                          allow_slow_non_contiguous=True).then_inc(ld_small, 16)

        @block.sync
        def _(sp):
            xp = x_prompt[0].rearrange("(j p) d -> j p d", p=P)
            for j in range(NT):
                src = xp[j] if j < 4 else x_sample.rearrange("b s d -> (b s) d")
                sp.dma_start(x[0:ROWS[j], j, :], src).then_inc(ld_x[j], 16)

            def projections(l, w_in, w_out):
                def quarter(n):
                    sp.dma_start(as_kn(quarter_buf[n], KC), in_cols(w_in, QUARTERS[l][n])
                                 ).then_inc(ld_in[l][n], 16)

                for n in range(2):
                    if l == 1:
                        sp.wait_ge(moe[0][("h1_mm", "h3_mm")[n]], 2 * pairs - 1)
                    quarter(n)
                    if l == 0 and n == 0:
                        small_loads(sp)
                if l == 1:
                    for j in range(NT):
                        sp.wait_ge(ld_y[0][j], 32)
                for h in range(2):
                    if l == 1:
                        sp.wait_ge(moe[0]["y_mm"], 2 * pairs - 1 + h)
                    sp.dma_start(as_kn(half_buf[h], KC),
                                 w_out[0].rearrange("(c p) n -> p c n", p=P)[:, :, h * 512:(h + 1) * 512]
                                 ).then_inc(ld_out[l][h], 16)
                for n in range(2, 4):
                    sp.wait_ge(mm_done, 32 * l + 8 * (n - 1))
                    quarter(n)

            def load_weights(l, k, par, src):
                sp.dma_start(as_kn(wbuf[k][par], KC if k < 2 else FC), src).then_inc(ld_w[l][k][par], 16)

            def experts_of(l):
                m = moe[l]
                sp.wait_ge(mm_done, 32 * (l + 1))
                load_weights(l, 1, 0, experts[l][1][0])
                load_weights(l, 0, 1, experts[l][0][1])
                for j in range(NT):
                    sp.wait_ge(xs_done, NT * (2 * l + 1) + j + 1)
                    sp.dma_start(xrows[j * P:j * P + ROWS[j], :], xs[0:ROWS[j], j, :]).then_inc(xs_st, 16)
                sp.wait_ge(wo_done, NT * (l + 1))
                load_weights(l, 0, 0, experts[l][0][0])
                sp.wait_ge(m["ld_x"][1], 16)
                load_weights(l, 2, 0, experts[l][2][0])
                load_weights(l, 1, 1, experts[l][1][1])
                load_weights(l, 2, 1, experts[l][2][1])
                sp.wait_ge(table_ok, l + 1)
                pairs = load_pairs(sp)
                with sp.Fori(1, pairs) as i:
                    for par in range(2):
                        b = 2 * i + par
                        e = sp.value_load(table[0:1, bass.ds(b, 1)], min_val=0, max_val=NE - 1)
                        for k, used in enumerate(("h1_mm", "h3_mm", "y_mm")):
                            sp.wait_ge(m[used], b - 1)
                            load_weights(l, k, par, experts[l][k][bass.ds(e, 1)].rearrange(
                                "a p c n -> (a p) c n"))
                return pairs

            projections(0, w_in_even, w_out_even)
            pairs = experts_of(0)
            projections(1, w_in_odd, w_out_odd)
            experts_of(1)
            yp = y_prompt[0].rearrange("(j p) d -> j p d", p=P)
            for j in range(NT):
                sp.wait_ge(fin_done, j + 1)
                dst = yp[j] if j < 4 else y_sample.rearrange("b s d -> (b s) d")
                sp.dma_start(dst, x[0:ROWS[j], j, :]).then_inc(fin_st, 16)
            sp.wait_ge(fin_st, 16 * NT)
            sp.wait_ge(out_st, 16 * 6)
            sp.wait_ge(state_st, 32)

        @block.gpsimd
        def _(pool):
            step = Chain(pool, const_step)
            step(pool.memset(ident[:, :], 0.0))
            step(pool.affine_select(out=ident[:, :], in_=ident[:, :], compare_op=ALU.not_equal, fill=1.0,
                                    base=0, pattern=[[-1, P]], channel_multiplier=1))
            step(pool.memset(ones[:, :], 1.0))
            pool.affine_select(out=before_b[:, :], in_=ones[:, :], compare_op=ALU.is_gt, fill=0.0,
                               base=0, pattern=[[1, P]], channel_multiplier=-1)
            pool.memset(ones_b[:, :], 1.0)
            pool.memset(zero16[:, :], 0.0)
            pool.affine_select(out=upto[:, :], in_=ones[:, :], compare_op=ALU.is_ge, fill=0.0,
                               base=0, pattern=[[1, P]], channel_multiplier=-1)
            flt = dict(allow_small_or_imprecise_dtypes=True)
            pool.memset(eps[:, :], EPS)
            pool.memset(ss[:, :, :], 1.0)
            pool.memset(lg[:, :, :], 0.0)
            pool.iota(pri[:, :], [[-1, 4]], base=4, channel_multiplier=0, **flt)
            pool.iota(eidx[:, :], [[1, NE]], base=0, channel_multiplier=0, **flt)
            pool.iota(jidx[:, :], [[1, MAX_OVER]], base=0, channel_multiplier=0, **flt)
            pool.iota(thr[:, :], [[P, 4]], base=P, channel_multiplier=0, **flt)
            pool.iota(count1[:, :], [[1, P]], base=1, channel_multiplier=0, **flt)
            pool.iota(tok_id[:, :, 0], [[0, NT]], base=0, channel_multiplier=1, **flt)
            pool.iota(tok_id[:, :, 1], [[P, NT]], base=0, channel_multiplier=0, **flt)
            pool.iota(thr2[:, :], [[2, 4]], base=0, channel_multiplier=0, **flt)
            pool.memset(valid[:, :], 1.0)
            step(pool.memset(table_f[:, :], 0.0))
            step(pool.affine_select(out=valid[:, NT - 1:NT], in_=ones[:, 0:1], compare_op=ALU.is_gt,
                                    fill=0.0, base=NS, pattern=[[0, 1]], channel_multiplier=-1))
            pool.sem_inc(consts, 1)
            pool.wait_ge(tr_done, NT)
            step(pool.memset(zeros, 0.0))
            for k in range(NE, MAX_BLOCKS):
                pool.dma_start(yrows[k * P:(k + 1) * P, :].rearrange("p (h d) -> p h d", h=2),
                               zeros.unsqueeze(1).to_broadcast([P, 2, 512])).then_inc(tails, 16)
            pool.dma_start(pool_s[0, :, 0:PH - 1, :], state_pool[0, :, 1:PH, :]).then_inc(state_st, 16)
            pool.dma_start(conv_s[0, :, 0:1, :], state_conv[0, :, 1:2, :]).then_inc(state_st, 16)

            for l in range(2):
                m = moe[l]
                if l == 1:
                    pool.dma_start(g_sgu, sgu_norm[0].partition_broadcast(P)).then_inc(ld_g[0], 16)
                    pool.wait_ge(vt_done, NT)
                    pool.dma_start(b_bc.rearrange("p h t -> p (h t)"),
                                   b_sgu[0].rearrange("h t -> (h t)").partition_broadcast(P)
                                   ).then_inc(ld_g[1], 16)
                def gather_rows(b, par):
                    pool.wait_ge(m["ids"], b + 1)
                    if not isinstance(b, int):
                        pool.sem_inc(m["turn"], 1)
                    pool.indirect_dma_start(
                        out=xg[par], out_offset=None, in_=xrows[:, :],
                        in_offset=bass.IndirectOffsetOnAxis(ap=ids[:, par:par + 1], axis=0)
                    ).then_inc(m["ld_x"][par], 16)

                pool.wait_ge(xs_st, 16 * NT * (l + 1))
                gather_rows(0, 0)
                gather_rows(1, 1)
                if l == 1:
                    pool.dma_start(g_fin, norm_final.partition_broadcast(P)).then_inc(ld_g[2], 16)

                def body(b, par, i, last):
                    if not last:
                        pool.wait_ge(m["xT_mm"], b + 1)
                        gather_rows(b + 2, par)
                    if isinstance(b, int) and b == 0:
                        return
                    pool.wait_ge(m["y_d"], b)
                    pool.wait_ge(m["y_a"], b)
                    pool.dma_start(yrows[bass.ds((b - 1) * P, P), :], yo[1 - par]
                                   ).then_inc(m["st_y"][1 - par], 16)

                pairs = run_blocks(pool, l, body)
                pool.wait_ge(m["y_d"], 2 * pairs)
                pool.wait_ge(m["y_a"], 2 * pairs)
                pool.dma_start(yrows[bass.ds((2 * pairs - 1) * P, P), :], yo[1]
                               ).then_inc(m["st_y"][1], 16)
                pool.wait_ge(m["st_y"][0], 16 * pairs)
                pool.wait_ge(m["st_y"][1], 16 * pairs)
                pool.wait_ge(m["ld_x"][0], 16 * pairs + 16)
                pool.sem_inc(results_in, 1)
                pool.wait_ge(results_in, l + 1)
                pool.wait_ge(slots_ok, l + 1)
                for j in range(NT):
                    for k in range(2):
                        q = 2 * j + k
                        if q >= 8:
                            pool.wait_ge(y_add, 2 * NT * l + q - 7)
                        pool.indirect_dma_start(
                            out=yg[q % 8][0:ROWS[j], :], out_offset=None, in_=yrows[:, :],
                            in_offset=bass.IndirectOffsetOnAxis(ap=slots[0:ROWS[j], k, j:j + 1],
                                                                axis=0)).then_inc(ld_y[l][j], 16)

        @block.tensor
        def _(pe):
            def transpose_tile(ph, j, src, first_bank):
                for c in range(KC):
                    last = pe.transpose(ps[:, first_bank + c // 4, (c % 4) * P:(c % 4) * P + ROWS[j]],
                                        src[0:ROWS[j], c * P:(c + 1) * P], ident[0:ROWS[j], 0:ROWS[j]])
                return last

            def normed_tile(ph, j):
                n = NT * ph + j
                pe.wait_ge(xs_done, n + 1)
                need(pe, ev_d, n - 1)
                need(pe, ev_a, n - 1)
                if ph % 2:
                    need(pe, lg_done, NT * (ph // 2) + j - 1 if j >= 2 else 0)
                transpose_tile(ph, j, xs[:, j, :], 4 + 2 * (j % 2)).then_inc(tr_done, 1)

            def split_product(out, stationary, moving, chunks=range(KC), before=None):
                terms = [(k, a, b) for k in chunks for a, b in ((0, 0), (0, 1), (1, 0))]
                for i, (k, a, b) in enumerate(terms):
                    if before and i % 3 == 0:
                        before(i // 3)
                    last = pe.matmul(out, stationary[a](k), moving[b](k), start=(i == 0),
                                     stop=(i == len(terms) - 1))
                return last

            def product(l, n):
                q, m, part = PRODUCTS[n]
                t0, t1 = PARTS[part]
                if n in (0, 4):
                    pe.wait_ge(tile_lo, NT * l + (2, NT)[part])
                pe.wait_ge(w_lo, 16 * l + 4 * q + m + 1)
                need(pe, mm_free, 32 * l + n - 3)
                split_product(ps[:, n % 4, 0:t1 - t0],
                              (lambda k: chunk_hi[:, m, k, :], lambda k: chunk_of(quarter_lo[q], m)[:, k, :]),
                              (lambda k: hT_hi[:, k, t0:t1], lambda k: hT_lo[:, k, t0:t1])
                              ).then_inc(mm_done, 1)

            def project_in(l, extra):
                for j in range(NT - 1):
                    normed_tile(2 * l, j)
                if l == 0:
                    pe.wait_ge(vec_e, 2)
                product(l, 0)
                normed_tile(2 * l, NT - 1)
                for n in range(1, 32):
                    product(l, n)
                    extra(n + 1)

            def chunk_ready(n):
                pe.wait_ge(p_lo, n + 1)

            def project_out(l, ready):
                for j in range(NT):
                    ready(j)
                    pair = 2 * (j % 2)
                    need(pe, x_upd, NT * l + j - 1 if j >= 2 else 0)
                    for h in range(2):
                        if j == 0:
                            pe.wait_ge(wo_lo, 8 * l + 7 + h)
                        last = split_product(ps[0:ROWS[j], pair + h, :],
                                             (lambda k: pT_hi[l][k][:, tok(j)], lambda k: pT_r[:, k, tok(j)]),
                                             (lambda k: as_kn(half_hi[h], KC)[:, k, :],
                                              lambda k: as_kn(half_lo[h], KC)[:, k, :]),
                                             OUT_ORDER[l], chunk_ready if l == 0 and j == 0 and h == 0 else None)
                    last.then_inc(wo_done, 1)
                    if j >= 1:
                        normed_tile(2 * l + 1, j - 1)
                        if j >= 2:
                            router(l, j - 2)
                normed_tile(2 * l + 1, NT - 1)
                router(l, NT - 2)
                router(l, NT - 1)

            def router(l, j):
                n = NT * (2 * l + 1) + j
                pe.wait_ge(ev_d, n + 1)
                pe.wait_ge(ev_a, n + 1)
                need(pe, lg_done, NT * l + j)
                for k in range(KC):
                    last = pe.matmul(ps[0:ROWS[j], (4, 6)[j % 2], 0:NG + NE], rT[:, k, tok(j)],
                                     wr[:, l, k, :], start=(k == 0), stop=(k == KC - 1))
                last.then_inc(lg_mm, 1)

            def ranks(l):
                pe.wait_ge(rank_in, l + 1)
                for j in range(NT):
                    for i in range(j + 1):
                        pe.matmul(ps[:, 4, j * NE:(j + 1) * NE], ones_b[:, :] if i < j else before_b[:, :],
                                  pairs_b[:, i, :], start=(i == 0), stop=(i == j), skip_group_check=True)
                for i in range(NT):
                    last = pe.matmul(ps[:, 5, 0:NE], ones_b[:, :], pairs_b[:, i, :], start=(i == 0), stop=(i == NT - 1))
                last.then_inc(rank_mm, 1)

            def experts_blocks(l):
                m = moe[l]

                def rows_T(b, par):
                    pe.wait_ge(m["ld_x"][par], 16 * (before_x + 1))
                    for c in range(KC):
                        last = pe.transpose(ps[:, 5 + c // 4, (c % 4) * P:(c % 4 + 1) * P],
                                            xg[par][:, c * P:(c + 1) * P], ident[:, :])
                    last.then_inc(m["xT_mm"], 1)

                def up(kind, bank, b, par, i, done):
                    pe.wait_ge(ld_w[l][kind][par], 16 * (before_same(b, par, i) + 1))
                    w = as_kn(wbuf[kind][par], KC)
                    for k in range(KC):
                        last = pe.matmul(ps[:, bank, :], xgT[:, k, :], w[:, k, :],
                                         start=(k == 0), stop=(k == KC - 1))
                    last.then_inc(m[done], 1)

                def hidden_T(b):
                    need(pe, m["hid"], b + 1)
                    need(pe, m["hT_e"], b)
                    for c in range(FC):
                        last = pe.transpose(ps[:, 4, c * P:(c + 1) * P], hid[:, c * P:(c + 1) * P], ident[:, :])
                    last.then_inc(m["hT_mm"], 1)

                def down(b, par):
                    need(pe, m["hT_e"], b + 1)
                    need(pe, m["y_d"], b)
                    need(pe, m["y_a"], b)
                    need(pe, m["dn_lo"], b + 1)
                    hid_parts = [v.rearrange("p (c s) -> p c s", c=FC) for v in (hidT_hi, hidT_lo)]
                    w_parts = [v.rearrange("p (c n) -> p c n", c=FC) for v in (down_hi, wbuf_r[2][par][:, :])]
                    for h in range(2):
                        cols = slice(h * 512, (h + 1) * 512)
                        last = split_product(ps[:, 2 + h, :],
                                             (lambda k: hid_parts[0][:, k, :], lambda k: hid_parts[1][:, k, :]),
                                             (lambda k: w_parts[0][:, k, cols], lambda k: w_parts[1][:, k, cols]),
                                             range(FC))
                    last.then_inc(m["y_mm"], 1)

                def down_last(b, n):
                    pe.wait_ge(ld_w[l][2][1], 16 * n)
                    need(pe, m["hT_e"], b + 1)
                    need(pe, m["y_d"], b)
                    need(pe, m["y_a"], b)
                    w = as_kn(wbuf[2][1], FC)
                    for h in range(2):
                        for k in range(FC):
                            last = pe.matmul(ps[:, 2 + h, :], hidT[:, k * P:(k + 1) * P],
                                             w[:, k, h * 512:(h + 1) * 512], start=(k == 0), stop=(k == FC - 1))
                    last.then_inc(m["y_mm"], 1)

                def numbers(b, par):
                    pe.wait_ge(m["onehot"], b + 1)
                    need(pe, m["ids_f"], b)
                    for j in range(NT):
                        last = pe.matmul(ps[:, 7, 4 * par:4 * par + 2], onehot[:, par, j, :], tok_id[:, j, :],
                                         start=(j == 0), stop=(j == NT - 1), skip_group_check=True)
                    last.then_inc(m["id_mm"], 1)

                numbers(0, 0)
                numbers(1, 1)
                before_x = 0
                rows_T(0, 0)

                def body(b, par, i, last):
                    nonlocal before_x
                    first = isinstance(b, int) and b == 0
                    pe.wait_ge(m["xT_d"], b + 1)
                    pe.wait_ge(m["xT_a"], b + 1)
                    need(pe, m["silu"], b)
                    up(0, 0, b, par, i, "h1_mm")
                    if not first:
                        hidden_T(b - 1)
                    if not last:
                        numbers(b + 2, par)
                    need(pe, m["hid"], b)
                    up(1, 1, b, par, i, "h3_mm")
                    if not last:
                        before_x = (b + 1) // 2 if isinstance(b, int) else i
                        rows_T(b + 1, 1 - par)
                    if not first:
                        down(b - 1, 1 - par)

                pairs = run_blocks(pe, l, body)
                hidden_T(2 * pairs - 1)
                down_last(2 * pairs - 1, pairs)

            pe.wait_ge(consts, 1)
            pe.wait_ge(ld_vec, 16 * 5)
            for c in range(KC):
                nv = NV if c < 4 else 5
                last = pe.transpose(ps[:, 0, c * NV:c * NV + nv], raw_vec[0:nv, c * P:(c + 1) * P],
                                    ident[0:nv, 0:nv])
            last.then_inc(vec_t, 1)

            def extra0(n):
                if n == 2:
                    pe.wait_ge(ld_hist, 32)
                    pe.wait_ge(ev_d, NT)
                    pe.wait_ge(ev_a, NT)
                    for g in range(4):
                        pe.transpose(ps[:, 4, g * NS * PH:(g + 1) * NS * PH], raw_hist[:, g * P:(g + 1) * P],
                                     ident[0:NS * PH, 0:NS * PH])
                    for g in range(4):
                        last = pe.transpose(ps[:, 5, g * NS * CH:(g + 1) * NS * CH],
                                            raw_chist[:, g * P:(g + 1) * P], ident[0:NS * CH, 0:NS * CH])
                    last.then_inc(vec_t, 1)
                if n == 6:
                    pe.wait_ge(ld_ws, 16)
                    for h in range(NH):
                        last = pe.transpose(ps[:, 6 + h // 4, (h % 4) * P:(h % 4 + 1) * P],
                                            raw_ws[:, h, :], ident[:, :])
                    last.then_inc(vec_t, 1)
                if n == 20:
                    pe.wait_ge(z_done, 4)
                    for g in range(4):
                        last = pe.transpose(ps[0:CH + NS, 4, g * P:(g + 1) * P],
                                            pT[:, 12 + g, SEQ - CH:T], ident[:, :])
                    last.then_inc(ost_t, 1)
                if n in POOL_AFTER:
                    g = POOL_AFTER.index(n)
                    if g == 0:
                        pe.wait_ge(ld_small, 16 * 8)
                        pe.wait_ge(vec_e, 4)
                    if g == 1:
                        pe.wait_ge(ost_e, 2)
                    pe.wait_ge(dif_done, g + 1)
                    need(pe, ya_done, g - 1)
                    for h, (t0, t1) in enumerate(PARTS):
                        last = pe.matmul(ps[:, POOL_BANK[g] + h, 0:t1 - t0], wpool_sb[:, g, :],
                                         dif[:, g, t0:t1], start=True, stop=True)
                    last.then_inc(pool_mm, 1)
                if n == 25:
                    pe.wait_ge(mm_free, 24)
                    for g in range(4):
                        last = pe.transpose(ps[0:PH + NS, 5, g * P:(g + 1) * P],
                                            pT[:, g, SEQ - PH:T], ident[:, :])
                    last.then_inc(ost_t, 1)

            project_in(0, extra0)
            def ready0(j):
                if j == 0:
                    pe.wait_ge(mm_free, 32)

            project_out(0, ready0)
            ranks(0)
            experts_blocks(0)

            def mix(j):
                pe.wait_ge(vn_done, j + 1)
                need(pe, mix_done, j - 1)
                for h in range(NH):
                    rhs = wsT[:, h, :] if j < 4 else wdiag[:, h, :]
                    last = pe.matmul(ps[:, 4 + 2 * (j % 2) + h // 4, (h % 4) * P:(h % 4) * P + ROWS[j]],
                                     xs[0:ROWS[j], j, h * P:(h + 1) * P], rhs, start=True, stop=True,
                                     skip_group_check=True)
                last.then_inc(mix_mm, 1)

            def extra1(n):
                if n == 31:
                    mix(0)
                if 18 <= n < 18 + 2 * NT and n % 2 == 0:
                    j = (n - 18) // 2
                    pe.wait_ge(mm_free, 32 + 16)
                    need(pe, v_cp, j - 1)
                    for c in range(KC):
                        last = pe.transpose(ps[0:ROWS[j], 4 + 2 * (j % 2) + c // 4, (c % 4) * P:(c % 4 + 1) * P],
                                            pT[:, 8 + c, tok(j)], ident[:, :])
                    last.then_inc(vt_done, 1)

            project_in(1, extra1)
            for j in range(1, NT):
                mix(j)

            def ready1(j):
                pe.wait_ge(p_lo, 8 + j + 1)
                if j == 0:
                    pe.wait_ge(mm_free, 64)

            project_out(1, ready1)
            ranks(1)
            experts_blocks(1)

        @block.scalar
        def _(act):
            act.dma_start(raw_vec[0:2, :], norm_mix).then_inc(ld_vec, 16)
            act.dma_start(raw_vec[2:4, :], norm_ffn).then_inc(ld_vec, 16)
            act.dma_start(raw_vec[4:5, :], sgu_norm).then_inc(ld_vec, 16)
            act.dma_start(raw_vec[5:6, 0:512], pool_scale).then_inc(ld_vec, 16)
            act.dma_start(raw_vec[6:9, 0:512], conv_w[0]).then_inc(ld_vec, 16)

            def root(ph, j, src):
                n = NT * ph + j
                r = slice(0, ROWS[j])
                act.activation(junk[r, :], src, ACT.Square, accum_out=ss[r, ph, j:j + 1]).then_inc(sq_done, 1)
                act.wait_ge(sq_done, n + 1)
                act.activation(rt[r, ph, j:j + 1], ss[r, ph, j:j + 1], ACT.Sqrt, bias=eps[r, :], scale=1.0 / D
                               ).then_inc(rt_done, 1)

            def evacuate(ph, j, dst):
                n = NT * ph + j
                row = (0, 2, 1, 3)[ph]
                act.wait_ge(tr_done, n + 1)
                for c in range(4, KC):
                    last = act.activation(dst[:, c, tok(j)],
                                          ps[:, 5 + 2 * (j % 2), (c - 4) * P:(c - 4) * P + ROWS[j]],
                                          ACT.Copy, scale=vecT[:, c, row:row + 1])
                last.then_inc(ev_a, 1)

            def hi_tile(l, j):
                ph = 2 * l
                act.wait_ge(ev_d, NT * ph + j + 1)
                act.wait_ge(ev_a, NT * ph + j + 1)
                act.copy(hT_hi[:, :, tok(j)], hT[:, :, tok(j)]).then_inc(tile_hi, 1)

            def hi_chunk(l, c):
                q, m = c // 4, c % 4
                act.wait_ge(ld_in[l][q], 16)
                act.copy(chunk_hi[:, m, :, :], chunk_of(quarter_buf[q], m)).then_inc(w_hi, 1)

            def hi_piece(l, h, p):
                act.wait_ge(ld_out[l][h], 16)
                act.copy(piece_of(half_hi[h], p), piece_of(half_buf[h], p)).then_inc(wo_hi, 1)

            def pooled(g):
                act.wait_ge(pool_mm, g + 1)
                for dst, done in ((pT_hi[0][g], p_hi), (pT[:, g, :], ya_done)):
                    for h, (t0, t1) in enumerate(PARTS):
                        last = act.activation(dst[:, t0:t1], ps[:, POOL_BANK[g] + h, 0:t1 - t0],
                                              ACT.Copy, scale=vecT[:, g, 5:6])
                    last.then_inc(done, 1)

            def convolved_hi(g):
                act.wait_ge(yb_done, g + 1)
                act.copy(pT_hi[0][4 + g], pT[:, 4 + g, :]).then_inc(p_hi, 1)

            def take_projection(l, func):
                for n, (q, m, part) in enumerate(PRODUCTS):
                    t0, t1 = PARTS[part]
                    act.wait_ge(mm_done, 32 * l + n + 1)
                    if l == 0 and n == 16:
                        act.wait_ge(vec_e, 4)
                    act.activation(pT[:, 4 * QUARTERS[l][q] + m, t0:t1], ps[:, n % 4, 0:t1 - t0],
                                   func).then_inc(mm_free, 1)
                    for c in range(4, 16):
                        if n == after_products(c):
                            hi_chunk(l, c)
                    if n >= 25 and n % 2:
                        hi_piece(l, 0, m)
                        hi_piece(l, 1, m)
                    if l == 0 and n == 22:
                        act.wait_ge(ost_t, 1)
                        act.copy(ost_z, ps[0:CH + NS, 4, :]).then_inc(ost_e, 1)
                    if l == 0 and n == 26:
                        act.wait_ge(ost_t, 2)
                        act.copy(ost_u, ps[0:PH + NS, 5, :]).then_inc(ost_e, 1)
                    if l == 0 and n in POOL_AFTER:
                        pooled(POOL_AFTER.index(n))
                    if l == 0 and n in (26, 28, 30):
                        convolved_hi((n - 26) // 2)
                    if l == 1 and n >= 20 and n % 2 == 0 and (n - 20) // 2 < NT:
                        v_square((n - 20) // 2)
                        if n == 28:
                            act.wait_ge(v_sq, NT)
                            act.activation(rt[:, 4, :], ss[:, 4, :], ACT.Sqrt, bias=eps[:, :], scale=1.0 / D
                                           ).then_inc(v_rt, 1)

            def v_square(j):
                r = slice(0, ROWS[j])
                act.wait_ge(v_cp, j + 1)
                need(act, v_sq, j)
                act.activation(junk[r, :], xs[r, j, :], ACT.Square, accum_out=ss[r, 4, j:j + 1]).then_inc(v_sq, 1)

            def exponentials(l):
                act.wait_ge(ex_in, l + 1)
                act.activation(ex[:, :, :], ex[:, :, :], ACT.Exp).then_inc(ex_out, 1)

            def experts_blocks(l):
                m = moe[l]
                row = 2 + l

                def rows_T(b):
                    need(act, m["xT_mm"], b + 1)
                    for c in range(4, KC):
                        last = act.activation(xgT[:, c, :], ps[:, 6, (c - 4) * P:(c - 3) * P], ACT.Copy,
                                              scale=vecT[:, c, row:row + 1])
                    last.then_inc(m["xT_a"], 1)

                def result(b, par, stored):
                    act.wait_ge(m["y_mm"], b + 1)
                    need(act, m["st_y"][par], 16 * stored)
                    act.copy(yo[par][:, 512:1024], ps[:, 3, :]).then_inc(m["y_a"], 1)

                def hi_down(b, par, n):
                    act.wait_ge(ld_w[l][2][par], 16 * n)
                    need(act, m["y_mm"], b)
                    act.copy(down_hi, wbuf[2][par][:, :]).then_inc(m["dn_hi"], 1)

                act.wait_ge(xs_st, 16 * NT * (l + 1))
                rows_T(0)

                def body(b, par, i, last):
                    if not (isinstance(b, int) and b == 0):
                        hi_down(b - 1, 1 - par, (b + 1) // 2 if isinstance(b, int) else i)
                    act.wait_ge(m["h1_mm"], b + 1)
                    need(act, m["hid"], b)
                    act.activation(act_g, ps[:, 0, :], ACT.Silu).then_inc(m["silu"], 1)
                    if not last:
                        act.wait_ge(m["h3_mm"], b + 1)
                        rows_T(b + 1)
                    if not (isinstance(b, int) and b == 0):
                        result(b - 1, 1 - par, (b - 1) // 2 if isinstance(b, int) else i - 1)

                pairs = run_blocks(act, l, body)
                result(2 * pairs - 1, 1, pairs - 1)

            for j in range(NT):
                act.wait_ge(ld_x[j], 16)
                if j == 0:
                    act.wait_ge(consts, 1)
                root(0, j, x[0:ROWS[j], j, :])
                if j == 1:
                    act.wait_ge(vec_e, 2)
                if j >= 1:
                    evacuate(0, j - 1, hT)
                    hi_tile(0, j - 1)
                if j >= 2:
                    hi_chunk(0, j - 2)
            evacuate(0, NT - 1, hT)
            hi_tile(0, NT - 1)
            hi_chunk(0, 3)
            for l in range(2):
                take_projection(l, ACT.Copy if l == 0 else ACT.Gelu_apprx_tanh)
                if l == 0:
                    convolved_hi(3)
                    act.wait_ge(ost_e, 2)
                    act.dma_start(conv_p[0, 0], ost_z[0:CH, :]).then_inc(out_st, 16)
                    act.dma_start(conv_s[0, :, CH - 1, :], ost_z[CH:CH + NS, :]).then_inc(out_st, 16)
                    act.dma_start(pool_p[0, 0], ost_u[0:PH, :]).then_inc(out_st, 16)
                    act.dma_start(pool_s[0, :, PH - 1, :], ost_u[PH:PH + NS, :]).then_inc(out_st, 16)
                else:
                    for j in range(NT):
                        act.wait_ge(mix_done, j + 1)
                        act.copy(hT_lo[:, :, tok(j)], pT[:, 0:8, tok(j)]).then_inc(p_hi, 1)
                    act.wait_ge(vn_done, NT)
                    act.dma_start(v_p[0, 0], xs[:, 3, :]).then_inc(out_st, 16)
                    act.dma_start(v_s[0].rearrange("b s d -> (b s) d"), xs[0:NS, 4, :]).then_inc(out_st, 16)
                ph = 2 * l + 1
                for j in range(NT):
                    act.wait_ge(x_upd, NT * l + j + 1)
                    root(ph, j, x[0:ROWS[j], j, :])
                    if j >= 1:
                        evacuate(ph, j - 1, rT)
                evacuate(ph, NT - 1, rT)
                exponentials(l)
                experts_blocks(l)
                if l == 0:
                    for j in range(NT):
                        act.wait_ge(y_add, 2 * (j + 1))
                        root(2, j, x[0:ROWS[j], j, :])
                        if j >= 1:
                            evacuate(2, j - 1, hT)
                            hi_tile(1, j - 1)
                        if j >= 2:
                            hi_chunk(1, j - 2)
                    evacuate(2, NT - 1, hT)
                    hi_tile(1, NT - 1)
                    hi_chunk(1, 3)
            for j in range(NT):
                r = slice(0, ROWS[j])
                act.wait_ge(y_add, 2 * NT + 2 * (j + 1))
                act.activation(junk[r, :], x[r, j, :], ACT.Square, accum_out=ss[r, 4, j:j + 1]).then_inc(v_sq, 1)
                act.wait_ge(v_sq, NT + j + 1)
                act.activation(rt[r, 4, j:j + 1], ss[r, 4, j:j + 1], ACT.Sqrt, bias=eps[r, :], scale=1.0 / D
                               ).then_inc(v_rt, 1)

        @block.vector
        def _(dve):
            step = Chain(dve, dve_step)

            def scale_rows(ph, j):
                n = NT * ph + j
                r = slice(0, ROWS[j])
                dve.wait_ge(rt_done, n + 1)
                dve.reciprocal(rs[r, ph, j:j + 1], rt[r, ph, j:j + 1]).then_inc(rc_done, 1)
                dve.wait_ge(rc_done, n + 1)
                dve.tensor_scalar(xs[r, j, :], x[r, j, :], rs[r, ph, j:j + 1], None, ALU.mult
                                  ).then_inc(xs_done, 1)

            def gain(row, n):
                return vecT[:, 0:4, row:row + 1].to_broadcast([P, 4, n])

            def evacuate(ph, j, dst):
                n = NT * ph + j
                row = (0, 2, 1, 3)[ph]
                dve.wait_ge(tr_done, n + 1)
                src = ps[:, 4 + 2 * (j % 2), :].rearrange("p (c t) -> p c t", c=4)[:, :, 0:ROWS[j]]
                dve.tensor_tensor(dst[:, 0:4, tok(j)], src, gain(row, ROWS[j]), ALU.mult).then_inc(ev_d, 1)

            def bc(ap, shape):
                return ap.to_broadcast(shape)

            def first_best(src, top, onehot):
                s = [P, 5 * NT, 4]
                step(dve.tensor_reduce(top, src, AX_X, ALU.max))
                step(dve.tensor_tensor(eq[:, :, :], src, bc(top.unsqueeze(2), s), ALU.is_equal))
                step(dve.tensor_tensor(eq[:, :, :], eq[:, :, :], bc(pri[:, :].unsqueeze(1), s), ALU.mult))
                step(dve.tensor_reduce(best[:, 2, :], eq[:, :, :], AX_X, ALU.max))
                step(dve.tensor_tensor(onehot, eq[:, :, :], bc(best[:, 2, :].unsqueeze(2), s), ALU.is_equal))

            def one_hot(l, b, par, e=None):
                m = moe[l]
                need(dve, m["id_mm"], b - 1)
                s = [P, NT, P]
                if e is None:
                    e, first = b, 0.0
                else:
                    first = table_f[:, bass.ds(TABLE + b, 1)]
                dve.scalar_tensor_tensor(out=onehot[:, par, :, :], in0=bc(rank1[:, :, bass.ds(e, 1)], s),
                                         scalar=first, in1=bc(count1[:, :].unsqueeze(1), s),
                                         op0=ALU.subtract, op1=ALU.is_equal).then_inc(m["onehot"], 1)

            def token_numbers(l, b, par):
                m = moe[l]
                dve.wait_ge(m["id_mm"], b + 1)
                need(dve, m["xT_mm"], b - 1)
                dve.tensor_reduce(ids_f[:, par:par + 1], ps[:, 7, 4 * par:4 * par + 2], AX_X, ALU.add
                                  ).then_inc(m["ids_f"], 1)
                dve.wait_ge(m["ids_f"], b + 1)
                dve.tensor_copy(ids[:, par:par + 1], ids_f[:, par:par + 1]).then_inc(m["ids"], 1)

            def rows_T(l, b):
                m = moe[l]
                need(dve, m["xT_mm"], b + 1)
                src = ps[:, 5, :].rearrange("p (c s) -> p c s", c=4)
                dve.tensor_tensor(xgT[:, 0:4, :], src, gain(2 + l, P), ALU.mult).then_inc(m["xT_d"], 1)

            def route(l):
                s16 = [P, NT, NG, EPG]
                flat = [oh[:, k, :, :, :].rearrange("p t a j -> p (t a) j") for k in range(2)]
                first_best(lg[:, :, :].rearrange("p t (a j) -> p (t a) j", j=4), best[:, 0, :], flat[0])
                step(dve.tensor_tensor(goh[:, :, :], oh[:, 0, :, 0, :],
                                       bc(valid[:, :].unsqueeze(2), [P, NT, NG]), ALU.mult))
                step(dve.scalar_tensor_tensor(out=lg2[:, :, :], in0=flat[0], scalar=BIG,
                                              in1=lg[:, :, :].rearrange("p t (a j) -> p (t a) j", j=4),
                                              op0=ALU.mult, op1=ALU.add))
                first_best(lg2[:, :, :], best[:, 1, :], flat[1])
                for k in range(2):
                    step(dve.tensor_tensor(sel[:, k, :, :].rearrange("p t (g j) -> p t g j", g=NG),
                                           bc(goh[:, :, :].unsqueeze(3), s16), oh[:, k, :, 1:5, :], ALU.mult))
                dve.tensor_tensor(pairs_b[:, :, :], sel[:, 0, :, :], sel[:, 1, :, :], ALU.add).then_inc(rank_in, 1)
                tops = [best[:, k, :].rearrange("p (t a) -> p t a", t=NT) for k in range(2)]
                step(dve.tensor_tensor(ex[:, :, 0:NG], lg[:, :, 0:NG], bc(tops[0][:, :, 0:1], [P, NT, NG]),
                                       ALU.subtract))
                dve.tensor_tensor(ex[:, :, NG:], tops[1][:, :, 1:5], tops[0][:, :, 1:5], ALU.subtract
                                  ).then_inc(ex_in, 1)
                ov, ocs, oex, big, dlt = (c16[:, k, :] for k in range(5))
                dve.wait_ge(rank_mm, l + 1)
                cnt = ps[:, 5, 0:NE]
                rank = ps[:, 4, 0:NT * NE].rearrange("p (t e) -> p t e", t=NT)
                sE = [P, NT, NE]
                s2 = [P, 2, NT, NE]
                step(dve.scalar_tensor_tensor(out=rank1[:, :, :], in0=rank, scalar=1.0, in1=pairs_b[:, :, :],
                                              op0=ALU.add, op1=ALU.mult))
                th = over[:, 0:4, :].rearrange("p a e -> p (a e)").rearrange("p (e a) -> p e a", e=NE)
                step(dve.tensor_tensor(th, bc(cnt.unsqueeze(2), [P, NE, 4]),
                                       bc(thr[:, :].unsqueeze(1), [P, NE, 4]), ALU.is_gt))
                one_hot(l, 0, 0)
                one_hot(l, 1, 1)
                token_numbers(l, 0, 0)
                token_numbers(l, 1, 1)
                one_hot(l, 2, 0)
                step(dve.tensor_reduce(ov, th, AX_X, ALU.add))
                step(dve.tensor_tensor_scan(ocs, ov, zero16[:, :], 0.0, ALU.add, ALU.add))
                step(dve.tensor_tensor(oex, ocs, ov, ALU.subtract))
                sO = [P, MAX_OVER, NE]
                jb = bc(jidx[:, :].unsqueeze(2), sO)
                step(dve.tensor_tensor(over[:, :, :], bc(oex.unsqueeze(1), sO), jb, ALU.is_le))
                step(dve.tensor_tensor(over2[:, :, :], bc(ocs.unsqueeze(1), sO), jb, ALU.is_gt))
                step(dve.tensor_tensor(over[:, :, :], over[:, :, :], over2[:, :, :], ALU.mult))
                step(dve.tensor_tensor(over2[:, :, :], over[:, :, :], bc(eidx[:, :].unsqueeze(1), sO), ALU.mult))
                step(dve.tensor_reduce(table_f[:, NE:NE + MAX_OVER], over2[:, :, :], AX_X, ALU.add))
                step(dve.tensor_tensor(over2[:, :, :], over[:, :, :], bc(oex.unsqueeze(1), sO), ALU.mult))
                step(dve.tensor_reduce(o8[:, 0, :], over2[:, :, :], AX_X, ALU.add))
                step(dve.tensor_reduce(o8[:, 1, :], over[:, :, :], AX_X, ALU.add))
                step(dve.scalar_tensor_tensor(out=o8[:, 2, :], in0=jidx[:, :], scalar=1.0, in1=o8[:, 1, :],
                                              op0=ALU.add, op1=ALU.mult))
                step(dve.tensor_tensor(o8[:, 3, :], o8[:, 2, :], o8[:, 0, :], ALU.subtract))
                step(dve.tensor_scalar(table_f[:, TABLE + NE:TABLE + MAX_BLOCKS], o8[:, 3, :], float(P), None,
                                       ALU.mult))
                step(dve.tensor_tensor(o8[:, 0, 0:4], bc(ocs[:, NE - 1:NE], [P, 4]), thr2[:, :], ALU.is_gt))
                step(dve.tensor_reduce(table_f[:, 2 * TABLE:], o8[:, 0, 0:4], AX_X, ALU.add))
                step(dve.tensor_copy(table_f[:, 0:NE], eidx[:, :]))
                dve.tensor_copy(table[:, :], table_f[:, :]).then_inc(table_ok, 1)
                rows_T(l, 0)
                step(dve.tensor_scalar(big, oex, float(NE - 1), float(P), ALU.add, ALU.mult))
                step(dve.scalar_tensor_tensor(out=dlt, in0=eidx[:, :], scalar=float(P), in1=big,
                                              op0=ALU.mult, op1=ALU.subtract))
                yr = rows[:, :, :]
                step(dve.tensor_scalar(yr, rank1[:, :, :], float(P), None, ALU.is_le))
                step(dve.tensor_tensor(yr, yr, bc(dlt.unsqueeze(1), sE), ALU.mult))
                step(dve.scalar_tensor_tensor(out=yr, in0=rank1[:, :, :], scalar=-1.0, in1=yr, op0=ALU.add,
                                              op1=ALU.add))
                step(dve.tensor_tensor(yr, yr, bc(big.unsqueeze(1), sE), ALU.add))
                step(dve.tensor_tensor(prod[:, :, :, :], sel[:, :, :, :], bc(yr.unsqueeze(1), s2), ALU.mult))
                step(dve.tensor_reduce(slots_f[:, :, :], prod[:, :, :, :], AX_X, ALU.add))
                dve.tensor_copy(slots[:, :, :], slots_f[:, :, :]).then_inc(slots_ok, 1)
                dve.wait_ge(ex_out, l + 1)
                total, top, e2, both, share = (r1[:, k, :] for k in range(5))
                step(dve.tensor_reduce(total, ex[:, :, 0:NG], AX_X, ALU.add))
                step(dve.reciprocal(top, total))
                step(dve.tensor_tensor(ex2[:, :, :], ex[:, :, NG:], goh[:, :, :], ALU.mult))
                step(dve.tensor_reduce(e2, ex2[:, :, :], AX_X, ALU.add))
                step(dve.tensor_scalar(both, e2, 1.0, None, ALU.add))
                step(dve.reciprocal(share, both))
                step(dve.tensor_tensor(gates[:, 0, :], top, share, ALU.mult))
                step(dve.tensor_tensor(gates[:, 1, :], gates[:, 0, :], e2, ALU.mult))

            def experts_blocks(l):
                m = moe[l]

                def hidden_T(b, split=True):
                    dve.wait_ge(m["hT_mm"], b + 1)
                    need(dve, m["y_mm"], b)
                    if not split:
                        dve.tensor_copy(hidT, ps[:, 4, :]).then_inc(m["hT_e"], 1)
                        return
                    dve.tensor_copy(hidT_hi, ps[:, 4, :]).then_inc(m["hT_hi"], 1)
                    dve.wait_ge(m["hT_hi"], b + 1)
                    dve.tensor_tensor(hidT_lo, ps[:, 4, :], hidT_hi.bitcast(F32), ALU.subtract
                                      ).then_inc(m["hT_e"], 1)

                def lo_down(b, par):
                    dve.wait_ge(m["dn_hi"], b + 1)
                    low(wbuf_r[2][par][:, :], wbuf[2][par][:, :], down_hi, m["dn_lo"])

                def result(b, par, stored):
                    dve.wait_ge(m["y_mm"], b + 1)
                    need(dve, m["st_y"][par], 16 * stored)
                    dve.tensor_copy(yo[par][:, 0:512], ps[:, 2, :]).then_inc(m["y_d"], 1)

                def body(b, par, i, last):
                    first = isinstance(b, int) and b == 0
                    if not first:
                        lo_down(b - 1, 1 - par)
                        hidden_T(b - 1)
                    dve.wait_ge(m["silu"], b + 1)
                    dve.wait_ge(m["h3_mm"], b + 1)
                    need(dve, m["hT_mm"], b)
                    dve.tensor_tensor(hid, act_g, ps[:, 1, :], ALU.mult).then_inc(m["hid"], 1)
                    if not last:
                        rows_T(l, b + 1)
                        token_numbers(l, b + 2, par)
                    if not first:
                        result(b - 1, 1 - par, (b - 1) // 2 if isinstance(b, int) else i - 1)
                    if not last:
                        e = dve.value_load(table[0:1, bass.ds(b + 3, 1)], min_val=0, max_val=NE - 1)
                        one_hot(l, b + 3, 1 - par, e)

                pairs = run_blocks(dve, l, body)
                hidden_T(2 * pairs - 1, split=False)
                result(2 * pairs - 1, 1, pairs - 1)

            def combine(l, j):
                r = slice(0, ROWS[j])
                dve.wait_ge(ld_y[l][j], 32)
                for k in range(2):
                    n = 2 * NT * l + 2 * j + k
                    if k:
                        dve.wait_ge(y_add, n)
                    dve.scalar_tensor_tensor(out=x[r, j, :], in0=yg[(2 * j + k) % 8][r, :],
                                             scalar=gates[r, k, j:j + 1], in1=x[r, j, :],
                                             op0=ALU.mult, op1=ALU.add).then_inc(y_add, 1)

            def add_projection(l, j):
                r = slice(0, ROWS[j])
                dve.wait_ge(wo_done, NT * l + j + 1)
                dve.tensor_tensor(x[r, j, :], x[r, j, :], bank2(2 * (j % 2))[r, :], ALU.add).then_inc(x_upd, 1)

            def logits(l, j):
                r = slice(0, ROWS[j])
                dve.wait_ge(lg_mm, NT * l + j + 1)
                dve.tensor_tensor(lg[r, j, :], ps[r, (4, 6)[j % 2], 0:NG + NE], br[r, l, :], ALU.add
                                  ).then_inc(lg_done, 1)

            def after_projection(l):
                ph = 2 * l + 1
                for j in range(NT):
                    add_projection(l, j)
                    scale_rows(ph, j)
                    if j >= 1:
                        evacuate(ph, j - 1, rT)
                    if j >= 2:
                        logits(l, j - 2)
                evacuate(ph, NT - 1, rT)
                logits(l, NT - 2)
                logits(l, NT - 1)
                dve.wait_ge(lg_done, NT * (l + 1))
                route(l)

            def low(value_r, value, hi, done):
                dve.tensor_tensor(value_r, value, hi.bitcast(F32), ALU.subtract).then_inc(done, 1)

            def lo_tile(l, j):
                dve.wait_ge(tile_hi, NT * l + j + 1)
                low(hT_lo[:, :, tok(j)], hT[:, :, tok(j)], hT_hi[:, :, tok(j)], tile_lo)

            def lo_chunk(l, c):
                q, m = c // 4, c % 4
                dve.wait_ge(w_hi, 16 * l + c + 1)
                low(chunk_of(quarter_lo[q], m), chunk_of(quarter_buf[q], m), chunk_hi[:, m, :, :], w_lo)

            def lo_pieces(l, p):
                for h in range(2):
                    dve.wait_ge(wo_hi, 8 * l + 2 * p + h + 1)
                    low(piece_of(half_lo[h], p), piece_of(half_buf[h], p), piece_of(half_hi[h], p), wo_lo)

            dve.wait_ge(consts, 1)
            dve.wait_ge(vec_t, 1)
            dve.tensor_copy(vecT[:, 0:4, :].rearrange("p c v -> p (c v)"), ps[:, 0, 0:4 * NV]).then_inc(vec_e, 1)
            dve.tensor_copy(vecT[:, 4:KC, 0:5],
                            ps[:, 0, 4 * NV:KC * NV].rearrange("p (c v) -> p c v", v=NV)[:, :, 0:5]
                            ).then_inc(vec_e, 1)
            for j in range(NT):
                dve.wait_ge(ld_x[j], 16)
                scale_rows(0, j)
                if j >= 1:
                    if j == 1:
                        dve.wait_ge(vec_e, 2)
                    evacuate(0, j - 1, hT)
                if j >= 2:
                    lo_tile(0, j - 2)
                if j >= 3:
                    lo_chunk(0, j - 3)
            lo_tile(0, NT - 2)
            evacuate(0, NT - 1, hT)
            lo_chunk(0, 2)
            lo_tile(0, NT - 1)
            lo_chunk(0, 3)
            dve.wait_ge(vec_t, 2)
            step(dve.tensor_copy(histT.rearrange("p g b t -> p (g b t)"), ps[:, 4, 0:4 * NS * PH]))
            dve.tensor_copy(chistT.rearrange("p g b t -> p (g b t)"),
                            ps[:, 5, 0:4 * NS * CH]).then_inc(vec_e, 1)
            dve.wait_ge(vec_t, 3)
            dve.tensor_tensor(wsT[:, :, :], ps[:, 6:8, :].rearrange("p b (h t) -> p (b h) t", h=4),
                              bc(upto[:, :].unsqueeze(1), [P, NH, P]), ALU.mult).then_inc(vec_e, 1)
            dve.wait_ge(ld_small, 16 * 8)
            step(dve.tensor_tensor(wdiag[:, :, :], bc(ident[0:NS, 0:NS].unsqueeze(1), [NS, NH, NS]),
                                   bc(w00[:, :].unsqueeze(2), [NS, NH, NS]), ALU.mult))
            lo_chunk(0, 4)
            step(dve.memset(rcnt[:, :, :], 1.0))
            for g, win in enumerate(WINDOWS):
                for t in range(win):
                    dve.memset(rcnt[:, g, t:t + 1], 1.0 / (t + 1))
                if win < 16:
                    dve.memset(rcnt[:, g, win:16], 1.0 / win)
            step(dve.memset(sumA[:, 0:16], 0.0))
            step(dve.memset(sumB[:, 0:16], 0.0))

            for c in range(5, 8):
                lo_chunk(0, c)
            for g in range(4):
                if g:
                    lo_chunk(0, 7 + g)
                dve.wait_ge(mm_free, 8 + 2 * g + 2)
                z, acc = pT[:, 12 + g, :], pT[:, 8 + g, :]
                dve.tensor_tensor(z, acc, z, ALU.mult).then_inc(z_done, 1)
                dve.wait_ge(z_done, g + 1)
                cw = [vecT[:, g, 6 + k:7 + k] for k in range(3)]
                step(dve.tensor_scalar(acc, z, cw[2], None, ALU.mult))
                for k, back in ((1, 1), (0, 2)):
                    step(dve.scalar_tensor_tensor(out=acc[:, back:SEQ], in0=z[:, 0:SEQ - back], scalar=cw[k],
                                                  in1=acc[:, back:SEQ], op0=ALU.mult, op1=ALU.add))
                    step(dve.scalar_tensor_tensor(out=acc[:, SEQ:T], in0=chistT[:, g, :, k], scalar=cw[k],
                                                  in1=acc[:, SEQ:T], op0=ALU.mult, op1=ALU.add))
            for g, win in enumerate(WINDOWS):
                lo_chunk(0, 11 + g)
                dve.wait_ge(mm_free, 16 + 2 * g + 2)
                u = pT[:, g, :]
                cur, nxt = sumA, sumB
                step(dve.tensor_copy(cur[:, 16:17], u[:, 0:1]))
                step(dve.tensor_tensor(cur[:, 17:16 + SEQ], u[:, 1:SEQ], u[:, 0:SEQ - 1], ALU.add))
                for k in range(1, g + 1):
                    back = 2 ** k
                    step(dve.tensor_tensor(nxt[:, 16:16 + SEQ], cur[:, 16:16 + SEQ],
                                           cur[:, 16 - back:16 + SEQ - back], ALU.add))
                    cur, nxt = nxt, cur
                step(dve.scalar_tensor_tensor(out=dif[:, g, 16:SEQ], in0=cur[:, 32:16 + SEQ], scalar=1.0 / win,
                                              in1=u[:, 16:SEQ], op0=ALU.mult, op1=ALU.subtract))
                step(dve.tensor_tensor(head[:, g, :], cur[:, 16:32], rcnt[:, g, :], ALU.mult))
                step(dve.tensor_tensor(dif[:, g, 0:16], head[:, g, :], u[:, 0:16], ALU.subtract))
                step(dve.tensor_reduce(hs[:, g, :], histT[:, g, :, PH - win + 1:PH], AX_X, ALU.add))
                step(dve.tensor_tensor(hs2[:, g, :], hs[:, g, :], u[:, SEQ:T], ALU.add))
                dve.scalar_tensor_tensor(out=dif[:, g, SEQ:T], in0=hs2[:, g, :], scalar=1.0 / win,
                                         in1=u[:, SEQ:T], op0=ALU.mult, op1=ALU.subtract).then_inc(dif_done, 1)
            lo_chunk(0, 15)
            for g in range(4):
                dve.wait_ge(mm_free, 24 + 2 * g + 2)
                dve.tensor_tensor(pT[:, 4 + g, :], pT[:, 4 + g, :], pT[:, 8 + g, :], ALU.mult).then_inc(yb_done, 1)
                lo_pieces(0, g)
                for n, c in ((2 * g, g), (2 * g + 1, 4 + g)):
                    dve.wait_ge(p_hi, n + 1)
                    if c < 4:
                        dve.wait_ge(ya_done, g + 1)
                    low(pT_r[:, c, :], pT[:, c, :], pT_hi[0][c], p_lo)
            dve.wait_ge(out_st, 16 * 4)
            dve.wait_ge(tails, 16 * MAX_OVER)
            after_projection(0)
            experts_blocks(0)
            for j in range(NT):
                combine(0, j)
                if j >= 1:
                    scale_rows(2, j - 1)
                if j >= 2:
                    evacuate(2, j - 2, hT)
                if j >= 3:
                    lo_tile(1, j - 3)
                    lo_chunk(1, j - 3)
            scale_rows(2, NT - 1)
            evacuate(2, NT - 2, hT)
            lo_tile(1, NT - 3)
            lo_tile(1, NT - 2)
            evacuate(2, NT - 1, hT)
            lo_chunk(1, 2)
            lo_tile(1, NT - 1)
            for c in range(3, 11):
                lo_chunk(1, c)

            for j in range(NT):
                r = slice(0, ROWS[j])
                lo_chunk(1, 11 + j)
                dve.wait_ge(vt_done, j + 1)
                dve.tensor_copy(xs[r, j, :], bank2(4 + 2 * (j % 2))[r, :]).then_inc(v_cp, 1)
            for p in range(2):
                lo_pieces(1, p)
            dve.wait_ge(v_rt, 1)
            step(dve.reciprocal(rs[:, 4, :], rt[:, 4, :]))
            dve.wait_ge(ld_g[0], 16)
            for j in range(NT):
                r = slice(0, ROWS[j])
                dve.scalar_tensor_tensor(out=xs[r, j, :], in0=xs[r, j, :], scalar=rs[r, 4, j:j + 1],
                                         in1=g_sgu[r, :], op0=ALU.mult, op1=ALU.mult).then_inc(vn_done, 1)
            lo_pieces(1, 2)
            dve.wait_ge(ld_g[1], 16)

            def lo_mixed(j):
                dve.wait_ge(p_hi, 8 + j + 1)
                low(pT_r[:, 0:8, tok(j)], pT[:, 0:8, tok(j)], hT_lo[:, :, tok(j)], p_lo)

            for j in range(NT):
                dve.wait_ge(mix_mm, j + 1)
                n = ROWS[j]
                mixed = ps[:, 4 + 2 * (j % 2):6 + 2 * (j % 2), :].rearrange("p b (h t) -> p (b h) t", h=4)[:, :, 0:n]
                bias = b_bc if j < 4 else bc(b_bc[:, :, 0:1], [P, NH, n])
                mx = arena_a[:, 8 * T + (j % 2) * 1024:8 * T + (j % 2 + 1) * 1024].rearrange(
                    "p (h t) -> p h t", h=NH)[:, :, 0:n]
                step(dve.tensor_tensor(mx, mixed, bias, ALU.add))
                if j == 0:
                    lo_pieces(1, 3)
                    dve.wait_ge(mm_free, 64)
                dve.tensor_tensor(pT[:, 0:8, tok(j)], pT[:, 0:8, tok(j)], mx, ALU.mult).then_inc(mix_done, 1)
                if j >= 1:
                    lo_mixed(j - 1)
            lo_mixed(NT - 1)
            dve.wait_ge(out_st, 16 * 6)
            after_projection(1)
            experts_blocks(1)
            dve.wait_ge(ld_g[2], 16)

            def finish(j):
                r = slice(0, ROWS[j])
                dve.wait_ge(v_rt, 1 + j + 1)
                step(dve.reciprocal(rs[r, 4, j:j + 1], rt[r, 4, j:j + 1]))
                dve.scalar_tensor_tensor(out=x[r, j, :], in0=x[r, j, :], scalar=rs[r, 4, j:j + 1],
                                         in1=g_fin[r, :], op0=ALU.mult, op1=ALU.mult).then_inc(fin_done, 1)

            for j in range(NT):
                combine(1, j)
                if j >= 1:
                    finish(j - 1)
            finish(NT - 1)


_INS = ["x_prompt", "x_sample", "state_pool", "state_conv", "norm_mix", "w_in_even", "w_pool", "pool_scale",
        "conv_w", "w_out_even", "w_in_odd", "sgu_norm", "w_sgu", "b_sgu", "w_out_odd", "norm_ffn",
        "w_router_group", "b_router_group", "w_router_expert", "b_router_expert", "w_gate", "w_up", "w_down",
        "norm_final"]
_OUTS = [(1, 512, 1024), (8, 1, 1024), (1, 1, 15, 512), (1, 8, 15, 512), (1, 1, 2, 512), (1, 8, 2, 512),
         (1, 1, 128, 1024), (1, 8, 1, 1024)]


def kernel(**inputs):
    import numpy as _np
    import concourse.bacc as _bacc
    from concourse import mybir as _mybir
    from concourse.bass_utils import run_bass_kernel_spmd as _run

    nc = _bacc.Bacc("TRN2", target_bir_lowering=False, num_devices=1)
    arrays, args = {}, []
    for name in _INS:
        a = _np.ascontiguousarray(inputs[name])
        arrays[f"in_{name}"] = a
        args.append(nc.dram_tensor(f"in_{name}", a.shape, _mybir.dt.from_np(a.dtype), kind="ExternalInput").ap())
    for i, shape in enumerate(_OUTS):
        args.append(nc.dram_tensor(f"out_{i}", shape, _mybir.dt.float32, kind="ExternalOutput").ap())
    trunk(nc, *args)
    r = _run(nc, [arrays], core_ids=[0])
    return tuple(r.results[0][f"out_{i}"] for i in range(len(_OUTS)))
```

```python
from contextlib import ExitStack
from functools import partial

import concourse.bass as bass
from concourse import mybir

F32 = mybir.dt.float32
F32R = mybir.dt.float32r
BF16 = mybir.dt.bfloat16
I32 = mybir.dt.int32
U32 = mybir.dt.uint32
ALU = mybir.AluOpType
ACT = mybir.ActivationFunctionType
AX_X = mybir.AxisListType.X

P = 128
D = 1024
SEQ = 512
NS = 8
T = SEQ + NS
PARTS = [(0, 2 * P), (2 * P, T)]
NT = 5
ROWS = [P, P, P, P, NS]
KC = D // P
NG, EPG = 4, 4
NE = NG * EPG
DE = 512
FC = DE // P
PH, CH = 15, 2
WINDOWS = (2, 4, 8, 16)
NH = 8
EPS = 1e-6
UP_SPLIT = 4
MAX_OVER = 8
MAX_BLOCKS = NE + MAX_OVER
TABLE = MAX_BLOCKS + 2
BIG = -3.0e38


def need(eng, sem, count):
    if isinstance(count, int) and count <= 0:
        return
    eng.wait_ge(sem, count)


class Chain:

    def __init__(self, eng, sem):
        self.eng, self.sem, self.n = eng, sem, 0

    def __call__(self, ins):
        self.aside(ins)
        self.eng.wait_ge(self.sem, self.n)

    def aside(self, ins):
        self.n += 1
        ins.then_inc(self.sem, 1)


def trunk(nc, x_prompt, x_sample, state_pool, state_conv, norm_mix, w_in_even, w_pool, pool_scale,
          conv_w, w_out_even, w_in_odd, sgu_norm, w_sgu, b_sgu, w_out_odd, norm_ffn, w_rg, b_rg,
          w_re, b_re, w_gate, w_up, w_down, norm_final, y_prompt, y_sample, pool_p, pool_s,
          conv_p, conv_s, v_p, v_s):
    with ExitStack() as ctx:
        def sb(name, shape, dt=F32):
            return ctx.enter_context(nc.sbuf_tensor(name, shape, dt))

        def sb_split(name, shape):
            offset = (nc.sbuf_base + 31) // 32 * 32
            full = sb(name, shape)
            return full, nc.alloc_sbuf_tensor_at(name + "_r", shape, F32R, offset=offset)

        def sem(name):
            return ctx.enter_context(nc.semaphore(name))

        def dram(name, shape):
            return nc.dram_tensor(name, shape, F32, kind="Internal").ap()

        xrows = dram("xrows", (T, D))
        yrows = dram("yrows", (MAX_BLOCKS * P, D))

        wpair = [[sb_split(f"wbuf_{k}{p}", [P, KC * T if (k, p) == ("gate", 1) else 4096])
                  for p in range(2)] for k in ("gate", "up", "down")]
        wbuf = [[full for full, _ in pair] for pair in wpair]
        wbuf_r = [[rounded for _, rounded in pair] for pair in wpair]
        x = sb("x", [P, NT, D])
        arena_a, arena_a_r = sb_split("arena_a", [P, 16 * T])
        arena_b, arena_b_r = sb_split("arena_b", [P, KC * T])
        arena_c, arena_c_r = sb_split("arena_c", [P, NT * D])
        ident = sb("ident", [P, P])
        upto = sb("upto", [P, P])
        ones = sb("ones", [P, P])
        ones_b = sb("ones_b", [P, P], BF16)
        before_b = sb("before_b", [P, P], BF16)
        pairs_b = sb("pairs_b", [P, NT, NE], BF16)
        wsT = sb("wsT", [P, NH, P])
        w00 = sb("w00", [NS, NH])
        wdiag = sb("wdiag", [NS, NH, NS])
        NV = 9
        vecT = sb("vecT", [P, KC, NV])
        wr = sb("wr", [P, 2, KC, NG + NE])
        br = sb("br", [P, 2, NG + NE])
        per_layer = sb("per_layer", [P, 4 * P + 4 * NS * (PH + CH)])
        wpool_sb = per_layer[:, 0:512].rearrange("p (g d) -> p g d", g=4)
        histT = per_layer[:, 512:992].rearrange("p (g b t) -> p g b t", g=4, b=NS)
        chistT = per_layer[:, 992:1056].rearrange("p (g b t) -> p g b t", g=4, b=NS)
        g_sgu = per_layer[:, 0:D]
        eps = sb("eps", [P, 1])
        root_eps = sb("root_eps", [P, 1])
        ss = sb("ss", [P, 5, NT])
        rt = sb("rt", [P, 5, NT])
        rs = sb("rs", [P, 5, NT])
        lg = sb("lg", [P, NT, NG + NE])
        lg2 = sb("lg2", [P, NT * 5, 4])
        eq = sb("eq", [P, NT * 5, 4])
        oh = sb("oh", [P, 2, NT, 5, 4])
        goh = sb("goh", [P, NT, NG])
        best = sb("best", [P, 3, NT * 5])
        ex = sb("ex", [P, NT, 2 * NG])
        ex2 = sb("ex2", [P, NT, NG])
        r1 = sb("r1", [P, 5, NT])
        sel = sb("sel", [P, 2, NT, NE])
        prod = sb("prod", [P, 2, NT, NE])
        rows = sb("rows", [P, NT, NE])
        rank1 = sb("rank1", [P, NT, NE])
        count1 = sb("count1", [P, P])
        tok_id = sb("tok_id", [P, NT, 2], BF16)
        onehot = sb("onehot", [P, 2, NT, P], BF16)
        junk = onehot[:, :, :, :].rearrange("p a j s -> p (a j s)")[:, 0:D]
        ids_f = sb("ids_f", [P, 2])
        ids = sb("ids", [P, 2], U32)
        c16 = sb("c16", [P, 5, NE])
        zero16 = sb("zero16", [P, NE])
        over = prod[:, :, :, :].rearrange("p k t e -> p (k t) e")[:, 0:MAX_OVER, :]
        over2 = sb("over2", [P, MAX_OVER, NE])
        o8 = sb("o8", [P, 4, MAX_OVER])
        slots_f = sb("slots_f", [P, 2, NT])
        slots = sb("slots", [P, 2, NT], U32)
        gates = sb("gates", [P, 2, NT])
        pri = sb("pri", [P, 4])
        eidx = sb("eidx", [P, NE])
        jidx = sb("jidx", [P, MAX_OVER])
        thr = sb("thr", [P, 4])
        thr2 = sb("thr2", [P, 4])
        valid = sb("valid", [P, NT])
        table_f = sb("table_f", [P, 2 * TABLE + 1])
        table = sb("table", [P, 2 * TABLE + 1], I32)
        rcnt = sb("rcnt", [P, 4, 16])
        hs = sb("hs", [P, 4, NS])
        hs2 = sb("hs2", [P, 4, NS])
        head = rows[:, 0:4, :]

        pT = arena_a[:, :].rearrange("p (m t) -> p m t", m=16)
        raw = arena_a
        raw_ws = raw[:, 0:1024].rearrange("p (h s) -> p h s", h=NH)
        raw_vec = raw[0:NV, 1024:2048]
        raw_hist = raw[0:NS * PH, 2048:2560]
        raw_chist = raw[0:NS * CH, 2560:3072]
        rT = arena_a[:, 0:KC * T].rearrange("p (c t) -> p c t", c=KC)
        xg = [arena_a[:, k * D:(k + 1) * D] for k in range(2)]
        xgT = arena_a[:, 2048:3072].rearrange("p (c s) -> p c s", c=KC)
        act_g = arena_a[:, 3072:3584]
        hid = arena_a[:, 3584:4096]
        hidT_lo = arena_a_r[:, 4096:4608]
        hidT = arena_a[:, 4096:4608]
        up_hi = arena_a_r[:, 4608:4608 + UP_SPLIT * DE]
        xgT_parts = [arena_a_r[:, k:k + UP_SPLIT * P].rearrange("p (c s) -> p c s", c=UP_SPLIT)
                     for k in (6656, 7168)]
        yg = [arena_a[:, k * D:(k + 1) * D] for k in range(8)]
        hT = arena_b[:, :].rearrange("p (c t) -> p c t", c=KC)
        yo = [arena_b[:, k * D:(k + 1) * D] for k in range(2)]
        g_fin = arena_b[:, 2048:3072]
        hT_lo = arena_b_r[:, :].rearrange("p (c t) -> p c t", c=KC)
        hT_hi = wbuf_r[0][1][:, :].rearrange("p (c t) -> p c t", c=KC)
        pT_r = arena_a_r[:, :].rearrange("p (m t) -> p m t", m=16)
        pT_hi = [[pT_r[:, 12 + c if c < 4 else 4 + c, :] for c in range(KC)],
                 [hT_lo[:, c, :] for c in range(KC)]]
        b_bc = arena_a[:, 8 * T + 2048:8 * T + 3072].rearrange("p (h t) -> p h t", h=NH)
        xs = arena_c[:, :].rearrange("p (j d) -> p j d", j=NT)
        down_hi = arena_c_r[:, 0:4096]
        hidT_hi = arena_c_r[:, 4096:4608]
        sumA = arena_c[:, 0:16 + SEQ]
        sumB = arena_c[:, 528:1056 + 0]
        dif = arena_c[:, 1056:1056 + 4 * T].rearrange("p (g t) -> p g t", g=4)
        ost_u = arena_c[0:PH + NS, 3136:3136 + 512]
        ost_z = arena_c[0:CH + NS, 3648:3648 + 512]
        zeros = arena_c[:, 4608:5120]

        ps = ctx.enter_context(nc.psum_tensor("ps", [P, 8, 512], F32))

        def bank2(b):
            return ps[:, b:b + 2, :].rearrange("p b n -> p (b n)")

        ld_x = [sem(f"ld_x{j}") for j in range(NT)]
        ld_vec, ld_hist, ld_ws, ld_small = sem("ld_vec"), sem("ld_hist"), sem("ld_ws"), sem("ld_small")
        ld_g = [sem("ld_gsgu"), sem("ld_bsgu"), sem("ld_gfin")]
        ld_in = [sem(f"ld_in{q}") for q in range(4)]
        ld_out = [sem(f"ld_out{h}") for h in range(2)]
        ld_w = [[[sem(f"ld_w{l}{k}{p}") for p in range(2)] for k in range(3)] for l in range(2)]
        const_step, consts = sem("const_step"), sem("consts")
        dve_step = sem("dve_step")
        tails = sem("tails")
        vec_t, vec_e = sem("vec_t"), sem("vec_e")
        table_in = sem("table_in")
        w_hi_first = sem("w_hi_first")
        sq_done, rt_done, rc_done, xs_done = sem("sq_done"), sem("rt_done"), sem("rc_done"), sem("xs_done")
        tr_done, ev_d, ev_a = sem("tr_done"), sem("ev_d"), sem("ev_a")
        mm_done, mm_free = sem("mm_done"), sem("mm_free")
        tile_hi, tile_lo, w_hi, w_lo = sem("tile_hi"), sem("tile_lo"), sem("w_hi"), sem("w_lo")
        wo_hi, wo_lo = [sem(f"wo_hi{h}") for h in range(2)], [sem(f"wo_lo{h}") for h in range(2)]
        p_hi, p_lo = sem("p_hi"), sem("p_lo")
        z_done, conv_done, dif_done, yb_done = sem("z_done"), sem("conv_done"), sem("dif_done"), sem("yb_done")
        pool_mm, ya_done = sem("pool_mm"), sem("ya_done")
        ost_t, ost_e = sem("ost_t"), sem("ost_e")
        wo_done, x_upd = sem("wo_done"), sem("x_upd")
        vt_done, v_cp, v_sq, v_rt, vn_done = sem("vt_done"), sem("v_cp"), sem("v_sq"), sem("v_rt"), sem("vn_done")
        mix_mm, mix_done = sem("mix_mm"), sem("mix_done")
        out_st, state_st = sem("out_st"), sem("state_st")
        lg_mm, lg_done = sem("lg_mm"), sem("lg_done")
        ex_in, ex_out = sem("ex_in"), sem("ex_out")
        rank_in, rank_mm, slots_ok, xs_st = sem("rank_in"), sem("rank_mm"), sem("slots_ok"), sem("xs_st")
        table_ok = sem("table_ok")
        moe = []
        for l in range(2):
            moe.append({k: sem(f"m{l}_{k}") for k in (
                "onehot", "id_mm", "ids_f", "ids", "xT_mm", "xT_d", "xT_a", "h1_mm", "silu", "h3_mm", "hid", "hT_mm", "hT_hi", "hT_e",
                "dn_hi", "dn_lo", "up_hi", "up_lo", "xT_lo",
                "y_mm", "y_d", "y_a")})
            moe[l]["turn"] = sem(f"m{l}_turn")
            moe[l]["ld_x"] = [sem(f"m{l}_ld_x{p}") for p in range(2)]
            moe[l]["st_y"] = [sem(f"m{l}_st_y{p}") for p in range(2)]
        ld_y = [sem(f"ld_y{j}") for j in range(NT)]
        y_add, results_in = sem("y_add"), sem("results_in")
        fin_rs, fin_scaled, fin_pool = sem("fin_rs"), sem("fin_scaled"), sem("fin_pool")
        fin_done, fin_st = sem("fin_done"), sem("fin_st")

        QUARTERS = [[2, 3, 0, 1], [2, 3, 0, 1]]
        quarter_buf = [wbuf[0][0], wbuf[1][0], wbuf[0][0], wbuf[1][0]]
        quarter_lo = [wbuf_r[0][0], wbuf_r[1][0], wbuf_r[0][0], wbuf_r[1][0]]
        chunk_hi = wbuf_r[1][1][:, :].rearrange("p (m c n) -> p m c n", m=4, c=KC)
        half_buf = [wbuf[2][0], wbuf[2][1]]
        half_lo = [wbuf_r[2][0], wbuf_r[2][1]]
        half_hi = [wbuf_r[0][0], wbuf_r[1][1]]
        OUT_ORDER = [[0, 4, 1, 5, 2, 6, 3, 7], list(range(KC))]
        POOL_AFTER, POOL_BANK = [26, 28, 29, 30], [6, 4, 6, 4]
        MIXED = [(0, 4, 0), (4, 8, 0)] + [(0, 8, j) for j in range(1, NT)]
        BY_POOL = 3
        PRODUCTS = ([(0, m, t) for t in range(2) for m in range(4)]
                    + [(q, m, t) for q in range(1, 4) for m in range(4) for t in range(2)])

        def tok(j):
            return slice(j * P, j * P + ROWS[j])

        def in_cols(w, q):
            return w[0].rearrange("(c p) n -> p c n", p=P)[:, :, q * 512:(q + 1) * 512]

        def as_kn(buf, k):
            return buf[:, 0:4096].rearrange("p (c n) -> p c n", c=k)

        def chunk_of(buf, m):
            return as_kn(buf, KC)[:, :, m * P:(m + 1) * P]

        def piece_of(buf, p):
            return as_kn(buf, KC)[:, 2 * p:2 * p + 2, :]

        def after_products(c):
            return 2 * c - 4

        def expert_view(w, l):
            return w[l].rearrange("e (c p) n -> e p c n", p=P)

        experts = [[expert_view(w, l) for w in (w_gate, w_up, w_down)] for l in range(2)]

        def load_pairs(eng):
            return NE // 2 + eng.value_load(table[0:1, 2 * TABLE:2 * TABLE + 1], min_val=0,
                                            max_val=MAX_OVER // 2)

        def run_blocks(eng, l, body):
            eng.wait_ge(table_ok, l + 1)
            pairs = load_pairs(eng)
            for b in range(3):
                body(b, b % 2, b, False)
            with eng.Fori(2, pairs) as i:
                body(2 * i - 1, 1, i, False)
                body(2 * i, 0, i, False)
            body(2 * pairs - 1, 1, pairs, True)
            return pairs

        def before_same(b, par, i):
            return b // 2 if isinstance(b, int) else (i - 1 if par == 1 else i)

        block = ctx.enter_context(nc.Block())

        def small_loads(sp):
            sp.dma_start(raw_hist, state_pool[0].rearrange("b t c -> (b t) c")).then_inc(ld_hist, 16)
            sp.dma_start(raw_chist, state_conv[0].rearrange("b t c -> (b t) c")).then_inc(ld_hist, 16)
            sp.dma_start(raw_ws, w_sgu[0].rearrange("h t s -> t h s")).then_inc(ld_ws, 16)
            sp.dma_start(wpool_sb[:, :, :], w_pool[0].rearrange("g c d -> c g d")).then_inc(ld_small, 16)
            for l in range(2):
                sp.dma_start(wr[:, l, :, 0:NG], w_rg[l].rearrange("(c p) e -> p c e", p=P)).then_inc(ld_small, 16)
                sp.dma_start(wr[:, l, :, NG:], w_re[l].rearrange("(c p) e -> p c e", p=P)).then_inc(ld_small, 16)
            sp.dma_start(br[:, :, 0:NG], b_rg.partition_broadcast(P)).then_inc(ld_small, 16)
            sp.dma_start(br[:, :, NG:], b_re.partition_broadcast(P)).then_inc(ld_small, 16)
            sp.dma_start(w00[:, :], w_sgu[0, :, 0, 0:1].rearrange("h a -> (h a)").partition_broadcast(NS),
                          allow_slow_non_contiguous=True).then_inc(ld_small, 16)

        @block.sync
        def _(sp):
            xp = x_prompt[0].rearrange("(j p) d -> j p d", p=P)
            for j in range(NT):
                src = xp[j] if j < 4 else x_sample.rearrange("b s d -> (b s) d")
                sp.dma_start(x[0:ROWS[j], j, :], src).then_inc(ld_x[j], 16)

            def projections(l, w_in, w_out):
                def quarter(n):
                    sp.dma_start(as_kn(quarter_buf[n], KC), in_cols(w_in, QUARTERS[l][n])
                                 ).then_inc(ld_in[n], 16)

                for n in range(2):
                    if l == 1:
                        sp.wait_ge(moe[0][("h1_mm", "h3_mm")[n]], 2 * pairs - 1)
                    quarter(n)
                    if l == 0 and n == 0:
                        small_loads(sp)
                if l == 1:
                    for j in range(NT):
                        sp.wait_ge(ld_y[j], 32)
                for h in range(2):
                    if l == 1:
                        sp.wait_ge(moe[0]["y_mm"], 2 * pairs - 1 + h)
                    sp.dma_start(as_kn(half_buf[h], KC),
                                 w_out[0].rearrange("(c p) n -> p c n", p=P)[:, :, h * 512:(h + 1) * 512]
                                 ).then_inc(ld_out[h], 16)
                for n in range(2, 4):
                    sp.wait_ge(mm_done, 32 * l + 8 * (n - 1))
                    quarter(n)

            def load_weights(l, k, par, src):
                sp.dma_start(as_kn(wbuf[k][par], KC if k < 2 else FC), src).then_inc(ld_w[l][k][par], 16)

            def experts_of(l):
                m = moe[l]
                sp.wait_ge(mm_done, 32 * (l + 1))
                load_weights(l, 1, 0, experts[l][1][0])
                load_weights(l, 0, 1, experts[l][0][1])
                def store_tokens(j):
                    sp.wait_ge(xs_done, NT * (2 * l + 1) + j + 1)
                    sp.dma_start(xrows[j * P:j * P + ROWS[j], :], xs[0:ROWS[j], j, :]).then_inc(xs_st, 16)

                for j in range(NT - 1):
                    store_tokens(j)
                sp.wait_ge(wo_done, NT * (l + 1))
                load_weights(l, 0, 0, experts[l][0][0])
                store_tokens(NT - 1)
                load_weights(l, 2, 0, experts[l][2][0])
                sp.wait_ge(m["ld_x"][1], 16)
                load_weights(l, 1, 1, experts[l][1][1])
                load_weights(l, 2, 1, experts[l][2][1])
                sp.wait_ge(table_ok, l + 1)
                pairs = load_pairs(sp)
                with sp.Fori(1, pairs) as i:
                    for par in range(2):
                        b = 2 * i + par
                        e = sp.value_load(table[0:1, bass.ds(b, 1)], min_val=0, max_val=NE - 1)
                        for k, used in enumerate(("h1_mm", "h3_mm", "y_mm")):
                            sp.wait_ge(m[used], b - 1)
                            load_weights(l, k, par, experts[l][k][bass.ds(e, 1)].rearrange(
                                "a p c n -> (a p) c n"))
                return pairs

            projections(0, w_in_even, w_out_even)
            pairs = experts_of(0)
            projections(1, w_in_odd, w_out_odd)
            experts_of(1)
            yp = y_prompt[0].rearrange("(j p) d -> j p d", p=P)
            for j in range(NT):
                if j < BY_POOL:
                    sp.wait_ge(fin_pool, j + 1)
                else:
                    sp.wait_ge(fin_done, j - BY_POOL + 1)
                dst = yp[j] if j < 4 else y_sample.rearrange("b s d -> (b s) d")
                sp.dma_start(dst, x[0:ROWS[j], j, :]).then_inc(fin_st, 16)
            sp.wait_ge(fin_st, 16 * NT)
            sp.wait_ge(out_st, 16 * 6)
            sp.wait_ge(state_st, 32)

        @block.gpsimd
        def _(pool):
            step = Chain(pool, const_step)
            step(pool.memset(ident[:, :], 0.0))
            step(pool.affine_select(out=ident[:, :], in_=ident[:, :], compare_op=ALU.not_equal, fill=1.0,
                                    base=0, pattern=[[-1, P]], channel_multiplier=1))
            step(pool.memset(ones[:, :], 1.0))
            pool.affine_select(out=before_b[:, :], in_=ones[:, :], compare_op=ALU.is_gt, fill=0.0,
                               base=0, pattern=[[1, P]], channel_multiplier=-1)
            pool.memset(ones_b[:, :], 1.0)
            pool.memset(zero16[:, :], 0.0)
            pool.affine_select(out=upto[:, :], in_=ones[:, :], compare_op=ALU.is_ge, fill=0.0,
                               base=0, pattern=[[1, P]], channel_multiplier=-1)
            flt = dict(allow_small_or_imprecise_dtypes=True)
            pool.memset(eps[:, :], EPS)
            pool.memset(ss[:, :, :], 1.0)
            pool.memset(lg[:, :, :], 0.0)
            pool.iota(pri[:, :], [[-1, 4]], base=4, channel_multiplier=0, **flt)
            pool.iota(eidx[:, :], [[1, NE]], base=0, channel_multiplier=0, **flt)
            pool.iota(jidx[:, :], [[1, MAX_OVER]], base=0, channel_multiplier=0, **flt)
            pool.iota(thr[:, :], [[P, 4]], base=P, channel_multiplier=0, **flt)
            pool.iota(count1[:, :], [[1, P]], base=1, channel_multiplier=0, **flt)
            pool.iota(tok_id[:, :, 0], [[0, NT]], base=0, channel_multiplier=1, **flt)
            pool.iota(tok_id[:, :, 1], [[P, NT]], base=0, channel_multiplier=0, **flt)
            pool.iota(thr2[:, :], [[2, 4]], base=0, channel_multiplier=0, **flt)
            pool.memset(valid[:, :], 1.0)
            step(pool.memset(table_f[:, :], 0.0))
            step(pool.affine_select(out=valid[:, NT - 1:NT], in_=ones[:, 0:1], compare_op=ALU.is_gt,
                                    fill=0.0, base=NS, pattern=[[0, 1]], channel_multiplier=-1))
            pool.sem_inc(consts, 1)
            pool.wait_ge(ld_in[0], 16)
            for m in range(2):
                pool.tensor_copy(chunk_hi[:, m, :, :], chunk_of(quarter_buf[0], m)).then_inc(w_hi_first, 1)
            pool.wait_ge(tr_done, NT)
            step(pool.memset(zeros, 0.0))
            for k in range(NE, MAX_BLOCKS):
                pool.dma_start(yrows[k * P:(k + 1) * P, :].rearrange("p (h d) -> p h d", h=2),
                               zeros.unsqueeze(1).to_broadcast([P, 2, 512])).then_inc(tails, 16)
            pool.dma_start(pool_s[0, :, 0:PH - 1, :], state_pool[0, :, 1:PH, :]).then_inc(state_st, 16)
            pool.dma_start(conv_s[0, :, 0:1, :], state_conv[0, :, 1:2, :]).then_inc(state_st, 16)

            def lo_pieces(l, places):
                for p in places:
                    pool.wait_ge(wo_hi[1], 4 * l + p + 1)
                    pool.tensor_tensor(piece_of(half_lo[1], p), piece_of(half_buf[1], p),
                                       piece_of(half_hi[1], p).bitcast(F32), ALU.subtract).then_inc(wo_lo[1], 1)

            for l in range(2):
                m = moe[l]
                if l == 1:
                    pool.dma_start(g_sgu, sgu_norm[0].partition_broadcast(P)).then_inc(ld_g[0], 16)
                    pool.wait_ge(vt_done, NT)
                    pool.dma_start(b_bc.rearrange("p h t -> p (h t)"),
                                   b_sgu[0].rearrange("h t -> (h t)").partition_broadcast(P)
                                   ).then_inc(ld_g[1], 16)
                lo_pieces(l, range(4))

                def gather_rows(b, par):
                    pool.wait_ge(m["ids"], b + 1)
                    if not isinstance(b, int):
                        pool.sem_inc(m["turn"], 1)
                    pool.indirect_dma_start(
                        out=xg[par], out_offset=None, in_=xrows[:, :],
                        in_offset=bass.IndirectOffsetOnAxis(ap=ids[:, par:par + 1], axis=0)
                    ).then_inc(m["ld_x"][par], 16)

                pool.wait_ge(xs_st, 16 * NT * (l + 1))
                gather_rows(0, 0)
                gather_rows(1, 1)
                if l == 1:
                    pool.dma_start(g_fin, norm_final.partition_broadcast(P)).then_inc(ld_g[2], 16)

                def body(b, par, i, last):
                    if not last:
                        pool.wait_ge(m["xT_mm"], b + 1)
                        gather_rows(b + 2, par)
                    if isinstance(b, int) and b == 0:
                        return
                    pool.wait_ge(m["y_d"], b)
                    pool.wait_ge(m["y_a"], b)
                    pool.dma_start(yrows[bass.ds((b - 1) * P, P), :], yo[1 - par]
                                   ).then_inc(m["st_y"][1 - par], 16)

                pairs = run_blocks(pool, l, body)
                pool.wait_ge(m["y_d"], 2 * pairs)
                pool.wait_ge(m["y_a"], 2 * pairs)
                pool.dma_start(yrows[bass.ds((2 * pairs - 1) * P, P), :], yo[1]
                               ).then_inc(m["st_y"][1], 16)
                pool.wait_ge(m["st_y"][0], 16 * pairs)
                pool.wait_ge(m["st_y"][1], 16 * pairs)
                pool.wait_ge(m["ld_x"][0], 16 * pairs + 16)
                pool.sem_inc(results_in, 1)
                pool.wait_ge(results_in, l + 1)
                pool.wait_ge(slots_ok, l + 1)
                for j in range(NT):
                    for k in range(2):
                        q = 2 * j + k
                        if q >= 8:
                            pool.wait_ge(y_add, 2 * NT * l + q - 7)
                        pool.indirect_dma_start(
                            out=yg[q % 8][0:ROWS[j], :], out_offset=None, in_=yrows[:, :],
                            in_offset=bass.IndirectOffsetOnAxis(ap=slots[0:ROWS[j], k, j:j + 1],
                                                                axis=0)).then_inc(ld_y[j], 16)
                if l == 1:
                    pool.wait_ge(ld_g[2], 16)
                    for j in range(BY_POOL):
                        pool.wait_ge(fin_scaled, j + 1)
                        pool.tensor_tensor(x[:, j, :], x[:, j, :], g_fin, ALU.mult).then_inc(fin_pool, 1)
                if l == 0:
                    for j in range(NT):
                        pool.wait_ge(tile_hi, NT + j + 1)
                        pool.tensor_tensor(hT_lo[:, :, tok(j)], hT[:, :, tok(j)], hT_hi[:, :, tok(j)].bitcast(F32),
                                           ALU.subtract).then_inc(tile_lo, 1)

        @block.tensor
        def _(pe):
            def transpose_tile(ph, j, src, first_bank):
                for c in range(KC):
                    last = pe.transpose(ps[:, first_bank + c // 4, (c % 4) * P:(c % 4) * P + ROWS[j]],
                                        src[0:ROWS[j], c * P:(c + 1) * P], ident[0:ROWS[j], 0:ROWS[j]])
                return last

            def normed_tile(ph, j):
                n = NT * ph + j
                if ph % 2:
                    pe.wait_ge(x_upd, NT * (ph // 2) + j + 1)
                else:
                    pe.wait_ge(xs_done, n + 1)
                need(pe, ev_d, n - 1)
                need(pe, ev_a, n - 1)
                if ph % 2:
                    need(pe, lg_done, NT * (ph // 2) + j - 1 if j >= 2 else 0)
                transpose_tile(ph, j, (xs, x)[ph % 2][:, j, :], 4 + 2 * (j % 2)).then_inc(tr_done, 1)

            def split_product(out, stationary, moving, chunks=range(KC), before=None, opens=True):
                terms = [(k, a, b) for k in chunks for a, b in ((0, 0), (0, 1), (1, 0))]
                for i, (k, a, b) in enumerate(terms):
                    if before and i % 3 == 0:
                        before(i // 3)
                    last = pe.matmul(out, stationary[a](k), moving[b](k), start=(opens and i == 0),
                                     stop=(i == len(terms) - 1))
                return last

            def product(l, n):
                q, m, part = PRODUCTS[n]
                t0, t1 = PARTS[part]
                if n in (0, 4):
                    pe.wait_ge(tile_lo, NT * l + (2, NT)[part])
                pe.wait_ge(w_lo, 16 * l + 4 * q + m + 1)
                need(pe, mm_free, 32 * l + n - 3)
                split_product(ps[:, n % 4, 0:t1 - t0],
                              (lambda k: chunk_hi[:, m, k, :], lambda k: chunk_of(quarter_lo[q], m)[:, k, :]),
                              (lambda k: hT_hi[:, k, t0:t1], lambda k: hT_lo[:, k, t0:t1])
                              ).then_inc(mm_done, 1)

            def project_in(l, extra):
                for j in range(NT - 1):
                    normed_tile(2 * l, j)
                if l == 0:
                    pe.wait_ge(vec_e, 2)
                product(l, 0)
                normed_tile(2 * l, NT - 1)
                for n in range(1, 32):
                    product(l, n)
                    extra(n + 1)

            def chunk_ready(l, h, n):
                pe.wait_ge(wo_lo[h], 4 * l + OUT_ORDER[l][n] // 2 + 1)
                if l == 0 and h == 0:
                    pe.wait_ge(p_lo, n + 1)

            def project_out(l, ready):
                for j in range(NT):
                    ready(j)
                    pair = 2 * (j % 2)
                    need(pe, x_upd, NT * l + j - 1 if j >= 2 else 0)
                    for h in range(2):
                        last = split_product(ps[0:ROWS[j], pair + h, :],
                                             (lambda k: pT_hi[l][k][:, tok(j)], lambda k: pT_r[:, k, tok(j)]),
                                             (lambda k: as_kn(half_hi[h], KC)[:, k, :],
                                              lambda k: as_kn(half_lo[h], KC)[:, k, :]),
                                             OUT_ORDER[l], partial(chunk_ready, l, h) if j == 0 else None)
                    last.then_inc(wo_done, 1)
                    if j >= 1:
                        normed_tile(2 * l + 1, j - 1)
                        if j >= 2:
                            router(l, j - 2)
                normed_tile(2 * l + 1, NT - 1)
                router(l, NT - 2)
                router(l, NT - 1)

            def router(l, j):
                n = NT * (2 * l + 1) + j
                pe.wait_ge(ev_d, n + 1)
                pe.wait_ge(ev_a, n + 1)
                need(pe, lg_done, NT * l + j)
                for k in range(KC):
                    last = pe.matmul(ps[0:ROWS[j], (4, 6)[j % 2], 0:NG + NE], rT[:, k, tok(j)],
                                     wr[:, l, k, :], start=(k == 0), stop=(k == KC - 1))
                last.then_inc(lg_mm, 1)

            def ranks(l):
                pe.wait_ge(rank_in, l + 1)
                for j in range(NT):
                    for i in range(j + 1):
                        pe.matmul(ps[:, 4, j * NE:(j + 1) * NE], ones_b[:, :] if i < j else before_b[:, :],
                                  pairs_b[:, i, :], start=(i == 0), stop=(i == j), skip_group_check=True)
                for i in range(NT):
                    last = pe.matmul(ps[:, 5, 0:NE], ones_b[:, :], pairs_b[:, i, :], start=(i == 0), stop=(i == NT - 1))
                last.then_inc(rank_mm, 1)

            def experts_blocks(l):
                m = moe[l]

                def rows_T(b, par):
                    pe.wait_ge(m["ld_x"][par], 16 * (before_x + 1))
                    for c in range(KC):
                        last = pe.transpose(ps[:, 5 + c // 4, (c % 4) * P:(c % 4 + 1) * P],
                                            xg[par][:, c * P:(c + 1) * P], ident[:, :])
                    last.then_inc(m["xT_mm"], 1)

                def gate(b, par, i):
                    pe.wait_ge(ld_w[l][0][par], 16 * (before_same(b, par, i) + 1))
                    w = as_kn(wbuf[0][par], KC)
                    for k in range(KC):
                        last = pe.matmul(ps[:, 0, :], xgT[:, k, :], w[:, k, :],
                                         start=(k == 0), stop=(k == KC - 1))
                    last.then_inc(m["h1_mm"], 1)

                def up_split(b, par, i):
                    pe.wait_ge(ld_w[l][1][par], 16 * (before_same(b, par, i) + 1))
                    w = as_kn(wbuf[1][par], KC)
                    for k in range(UP_SPLIT, KC):
                        pe.matmul(ps[:, 1, :], xgT[:, k, :], w[:, k, :], start=(k == UP_SPLIT), stop=False)
                    pe.wait_ge(m["up_lo"], b + 1)
                    pe.wait_ge(m["xT_lo"], b + 1)
                    w_parts = [v.rearrange("p (c n) -> p c n", c=UP_SPLIT)
                               for v in (up_hi, wbuf_r[1][par][:, 0:UP_SPLIT * DE])]
                    split_product(ps[:, 1, :],
                                  (lambda k: xgT_parts[0][:, k, :], lambda k: xgT_parts[1][:, k, :]),
                                  (lambda k: w_parts[0][:, k, :], lambda k: w_parts[1][:, k, :]),
                                  range(UP_SPLIT), opens=False).then_inc(m["h3_mm"], 1)

                def hidden_T(b):
                    need(pe, m["hid"], b + 1)
                    need(pe, m["hT_e"], b)
                    for c in range(FC):
                        last = pe.transpose(ps[:, 4, c * P:(c + 1) * P], hid[:, c * P:(c + 1) * P], ident[:, :])
                    last.then_inc(m["hT_mm"], 1)

                def down(b, par):
                    need(pe, m["hT_e"], b + 1)
                    need(pe, m["y_d"], b)
                    need(pe, m["y_a"], b)
                    need(pe, m["dn_lo"], b + 1)
                    hid_parts = [v.rearrange("p (c s) -> p c s", c=FC) for v in (hidT_hi, hidT_lo)]
                    w_parts = [v.rearrange("p (c n) -> p c n", c=FC) for v in (down_hi, wbuf_r[2][par][:, :])]
                    for h in range(2):
                        cols = slice(h * 512, (h + 1) * 512)
                        last = split_product(ps[:, 2 + h, :],
                                             (lambda k: hid_parts[0][:, k, :], lambda k: hid_parts[1][:, k, :]),
                                             (lambda k: w_parts[0][:, k, cols], lambda k: w_parts[1][:, k, cols]),
                                             range(FC))
                    last.then_inc(m["y_mm"], 1)

                def down_last(b, n):
                    pe.wait_ge(ld_w[l][2][1], 16 * n)
                    need(pe, m["hT_e"], b + 1)
                    need(pe, m["y_d"], b)
                    need(pe, m["y_a"], b)
                    w = as_kn(wbuf[2][1], FC)
                    for h in range(2):
                        for k in range(FC):
                            last = pe.matmul(ps[:, 2 + h, :], hidT[:, k * P:(k + 1) * P],
                                             w[:, k, h * 512:(h + 1) * 512], start=(k == 0), stop=(k == FC - 1))
                    last.then_inc(m["y_mm"], 1)

                def numbers(b, par):
                    pe.wait_ge(m["onehot"], b + 1)
                    need(pe, m["ids_f"], b)
                    for j in range(NT):
                        last = pe.matmul(ps[:, 7, 4 * par:4 * par + 2], onehot[:, par, j, :], tok_id[:, j, :],
                                         start=(j == 0), stop=(j == NT - 1), skip_group_check=True)
                    last.then_inc(m["id_mm"], 1)

                numbers(0, 0)
                numbers(1, 1)
                before_x = 0
                rows_T(0, 0)

                def body(b, par, i, last):
                    nonlocal before_x
                    first = isinstance(b, int) and b == 0
                    pe.wait_ge(m["xT_d"], b + 1)
                    pe.wait_ge(m["xT_a"], b + 1)
                    need(pe, m["silu"], b)
                    gate(b, par, i)
                    if not first:
                        hidden_T(b - 1)
                    if not last:
                        numbers(b + 2, par)
                    need(pe, m["hid"], b)
                    up_split(b, par, i)
                    if not last:
                        before_x = (b + 1) // 2 if isinstance(b, int) else i
                        rows_T(b + 1, 1 - par)
                    if not first:
                        down(b - 1, 1 - par)

                pairs = run_blocks(pe, l, body)
                hidden_T(2 * pairs - 1)
                down_last(2 * pairs - 1, pairs)

            pe.wait_ge(consts, 1)
            pe.wait_ge(ld_vec, 16 * 5)
            for c in range(KC):
                nv = NV if c < 4 else 5
                last = pe.transpose(ps[:, 0, c * NV:c * NV + nv], raw_vec[0:nv, c * P:(c + 1) * P],
                                    ident[0:nv, 0:nv])
            last.then_inc(vec_t, 1)

            def extra0(n):
                if n == 2:
                    pe.wait_ge(ld_hist, 32)
                    pe.wait_ge(ev_d, NT)
                    pe.wait_ge(ev_a, NT)
                    for g in range(4):
                        pe.transpose(ps[:, 4, g * NS * PH:(g + 1) * NS * PH], raw_hist[:, g * P:(g + 1) * P],
                                     ident[0:NS * PH, 0:NS * PH])
                    for g in range(4):
                        last = pe.transpose(ps[:, 5, g * NS * CH:(g + 1) * NS * CH],
                                            raw_chist[:, g * P:(g + 1) * P], ident[0:NS * CH, 0:NS * CH])
                    last.then_inc(vec_t, 1)
                if n == 6:
                    pe.wait_ge(ld_ws, 16)
                    for h in range(NH):
                        last = pe.transpose(ps[:, 6 + h // 4, (h % 4) * P:(h % 4 + 1) * P],
                                            raw_ws[:, h, :], ident[:, :])
                    last.then_inc(vec_t, 1)
                if n == 20:
                    pe.wait_ge(z_done, 4)
                    for g in range(4):
                        last = pe.transpose(ps[0:CH + NS, 4, g * P:(g + 1) * P],
                                            pT[:, 12 + g, SEQ - CH:T], ident[:, :])
                    last.then_inc(ost_t, 1)
                if n in POOL_AFTER:
                    g = POOL_AFTER.index(n)
                    if g == 0:
                        pe.wait_ge(ld_small, 16 * 8)
                        pe.wait_ge(vec_e, 4)
                    if g == 1:
                        pe.wait_ge(ost_e, 2)
                    pe.wait_ge(dif_done, g + 1)
                    need(pe, ya_done, g - 1)
                    for h, (t0, t1) in enumerate(PARTS):
                        last = pe.matmul(ps[:, POOL_BANK[g] + h, 0:t1 - t0], wpool_sb[:, g, :],
                                         dif[:, g, t0:t1], start=True, stop=True)
                    last.then_inc(pool_mm, 1)
                if n == 25:
                    pe.wait_ge(mm_free, 24)
                    for g in range(4):
                        last = pe.transpose(ps[0:PH + NS, 5, g * P:(g + 1) * P],
                                            pT[:, g, SEQ - PH:T], ident[:, :])
                    last.then_inc(ost_t, 1)

            project_in(0, extra0)
            def ready0(j):
                if j == 0:
                    pe.wait_ge(mm_free, 32)

            project_out(0, ready0)
            ranks(0)
            experts_blocks(0)

            def mix(j):
                pe.wait_ge(vn_done, j + 1)
                need(pe, mix_done, j if j >= 2 else 0)
                for h in range(NH):
                    rhs = wsT[:, h, :] if j < 4 else wdiag[:, h, :]
                    last = pe.matmul(ps[:, 4 + 2 * (j % 2) + h // 4, (h % 4) * P:(h % 4) * P + ROWS[j]],
                                     xs[0:ROWS[j], j, h * P:(h + 1) * P], rhs, start=True, stop=True,
                                     skip_group_check=True)
                last.then_inc(mix_mm, 1)

            def extra1(n):
                if n == 31:
                    mix(0)
                if 18 <= n < 18 + 2 * NT and n % 2 == 0:
                    j = (n - 18) // 2
                    pe.wait_ge(mm_free, 32 + 16)
                    need(pe, v_cp, j - 1)
                    for c in range(KC):
                        last = pe.transpose(ps[0:ROWS[j], 4 + 2 * (j % 2) + c // 4, (c % 4) * P:(c % 4 + 1) * P],
                                            pT[:, 8 + c, tok(j)], ident[:, :])
                    last.then_inc(vt_done, 1)

            project_in(1, extra1)
            for j in range(1, NT):
                mix(j)

            def ready1(j):
                pe.wait_ge(p_lo, 8 + j + 2)
                if j == 0:
                    pe.wait_ge(mm_free, 64)

            project_out(1, ready1)
            ranks(1)
            experts_blocks(1)

        @block.scalar
        def _(act):
            act.dma_start(raw_vec[0:2, :], norm_mix).then_inc(ld_vec, 16)
            act.dma_start(raw_vec[2:4, :], norm_ffn).then_inc(ld_vec, 16)
            act.dma_start(raw_vec[4:5, :], sgu_norm).then_inc(ld_vec, 16)
            act.dma_start(raw_vec[5:6, 0:512], pool_scale).then_inc(ld_vec, 16)
            act.dma_start(raw_vec[6:9, 0:512], conv_w[0]).then_inc(ld_vec, 16)

            def root(ph, j, src):
                n = NT * ph + j
                r = slice(0, ROWS[j])
                act.activation(junk[r, :], src, ACT.Square, accum_out=ss[r, ph, j:j + 1]).then_inc(sq_done, 1)
                act.wait_ge(sq_done, n + 1)
                act.activation(rt[r, ph, j:j + 1], ss[r, ph, j:j + 1], ACT.Sqrt, bias=eps[r, :], scale=1.0 / D
                               ).then_inc(rt_done, 1)

            def evacuate(ph, j, dst):
                n = NT * ph + j
                row = (0, 2, 1, 3)[ph]
                act.wait_ge(tr_done, n + 1)
                for c in range(4, KC):
                    last = act.activation(dst[:, c, tok(j)],
                                          ps[:, 5 + 2 * (j % 2), (c - 4) * P:(c - 4) * P + ROWS[j]],
                                          ACT.Copy, scale=vecT[:, c, row:row + 1])
                last.then_inc(ev_a, 1)

            def hi_tile(l, j):
                ph = 2 * l
                act.wait_ge(ev_d, NT * ph + j + 1)
                act.wait_ge(ev_a, NT * ph + j + 1)
                act.copy(hT_hi[:, :, tok(j)], hT[:, :, tok(j)]).then_inc(tile_hi, 1)

            def hi_chunk(l, c):
                q, m = c // 4, c % 4
                act.wait_ge(ld_in[q], 16 * (l + 1))
                act.copy(chunk_hi[:, m, :, :], chunk_of(quarter_buf[q], m)).then_inc(w_hi, 1)

            def hi_piece(l, h, p):
                act.wait_ge(ld_out[h], 16 * (l + 1))
                act.copy(piece_of(half_hi[h], p), piece_of(half_buf[h], p)).then_inc(wo_hi[h], 1)

            def pooled(g):
                act.wait_ge(pool_mm, g + 1)
                for dst, done in ((pT_hi[0][g], p_hi), (pT[:, g, :], ya_done)):
                    for h, (t0, t1) in enumerate(PARTS):
                        last = act.activation(dst[:, t0:t1], ps[:, POOL_BANK[g] + h, 0:t1 - t0],
                                              ACT.Copy, scale=vecT[:, g, 5:6])
                    last.then_inc(done, 1)

            def convolved_hi(g):
                act.wait_ge(yb_done, g + 1)
                act.copy(pT_hi[0][4 + g], pT[:, 4 + g, :]).then_inc(p_hi, 1)

            def take_projection(l, func):
                for n, (q, m, part) in enumerate(PRODUCTS):
                    t0, t1 = PARTS[part]
                    act.wait_ge(mm_done, 32 * l + n + 1)
                    if l == 0 and n == 16:
                        act.wait_ge(vec_e, 4)
                    act.activation(pT[:, 4 * QUARTERS[l][q] + m, t0:t1], ps[:, n % 4, 0:t1 - t0],
                                   func).then_inc(mm_free, 1)
                    for c in range(4, 16):
                        if n == after_products(c):
                            hi_chunk(l, c)
                    if n >= 24:
                        hi_piece(l, part, m)
                    if l == 0 and n == 22:
                        act.wait_ge(ost_t, 1)
                        act.copy(ost_z, ps[0:CH + NS, 4, :]).then_inc(ost_e, 1)
                    if l == 0 and n == 26:
                        act.wait_ge(ost_t, 2)
                        act.copy(ost_u, ps[0:PH + NS, 5, :]).then_inc(ost_e, 1)
                    if l == 0:
                        for step_of, g in {26: ((pooled, 0), (convolved_hi, 0)), 28: ((pooled, 1), (convolved_hi, 1)),
                                           29: ((pooled, 2),), 30: ((convolved_hi, 2), (pooled, 3))}.get(n, ()):
                            step_of(g)
                    if l == 1 and n >= 20 and n % 2 == 0 and (n - 20) // 2 < NT:
                        v_square((n - 20) // 2)
                        if n == 28:
                            act.wait_ge(v_sq, NT)
                            act.activation(rt[:, 4, :], ss[:, 4, :], ACT.Sqrt, bias=eps[:, :], scale=1.0 / D
                                           ).then_inc(v_rt, 1)

            def v_square(j):
                r = slice(0, ROWS[j])
                act.wait_ge(v_cp, j + 1)
                need(act, v_sq, j)
                act.activation(junk[r, :], xs[r, j, :], ACT.Square, accum_out=ss[r, 4, j:j + 1]).then_inc(v_sq, 1)

            def exponentials(l):
                act.wait_ge(ex_in, l + 1)
                act.activation(ex[:, :, :], ex[:, :, :], ACT.Exp).then_inc(ex_out, 1)

            def experts_blocks(l):
                m = moe[l]
                row = 2 + l

                def rows_T(b):
                    need(act, m["xT_mm"], b + 1)
                    for c in range(4, KC):
                        last = act.activation(xgT[:, c, :], ps[:, 6, (c - 4) * P:(c - 3) * P], ACT.Copy,
                                              scale=vecT[:, c, row:row + 1])
                    last.then_inc(m["xT_a"], 1)

                def result(b, par, stored):
                    act.wait_ge(m["y_mm"], b + 1)
                    need(act, m["st_y"][par], 16 * stored)
                    act.copy(yo[par][:, 512:1024], ps[:, 3, :]).then_inc(m["y_a"], 1)

                def hi_down(b, par, n):
                    act.wait_ge(ld_w[l][2][par], 16 * n)
                    need(act, m["y_mm"], b)
                    act.copy(down_hi, wbuf[2][par][:, :]).then_inc(m["dn_hi"], 1)

                def hi_up(b, par, i):
                    act.wait_ge(ld_w[l][1][par], 16 * (before_same(b, par, i) + 1))
                    need(act, m["h3_mm"], b)
                    act.copy(up_hi, wbuf[1][par][:, 0:UP_SPLIT * DE]).then_inc(m["up_hi"], 1)

                act.wait_ge(xs_st, 16 * NT * (l + 1))
                rows_T(0)

                def body(b, par, i, last):
                    hi_up(b, par, i)
                    if not (isinstance(b, int) and b == 0):
                        hi_down(b - 1, 1 - par, (b + 1) // 2 if isinstance(b, int) else i)
                    act.wait_ge(m["h1_mm"], b + 1)
                    need(act, m["hid"], b)
                    act.activation(act_g, ps[:, 0, :], ACT.Silu).then_inc(m["silu"], 1)
                    if not last:
                        act.wait_ge(m["h3_mm"], b + 1)
                        rows_T(b + 1)
                    if not (isinstance(b, int) and b == 0):
                        result(b - 1, 1 - par, (b - 1) // 2 if isinstance(b, int) else i - 1)

                pairs = run_blocks(act, l, body)
                result(2 * pairs - 1, 1, pairs - 1)

            tables = Chain(act, table_in)

            def fetch_root_table():
                tables(act.activation(root_eps[:, :], eps[:, :], ACT.Sqrt))

            act.wait_ge(consts, 1)
            fetch_root_table()
            for j in range(NT):
                act.wait_ge(ld_x[j], 16)
                root(0, j, x[0:ROWS[j], j, :])
            act.wait_ge(vec_e, 2)
            for j in range(NT):
                evacuate(0, j, hT)
                hi_tile(0, j)
            hi_chunk(0, 2)
            hi_chunk(0, 3)
            for l in range(2):
                take_projection(l, ACT.Copy if l == 0 else ACT.Gelu_apprx_tanh)
                if l == 0:
                    convolved_hi(3)
                    act.wait_ge(ost_e, 2)
                    act.dma_start(conv_p[0, 0], ost_z[0:CH, :]).then_inc(out_st, 16)
                    act.dma_start(conv_s[0, :, CH - 1, :], ost_z[CH:CH + NS, :]).then_inc(out_st, 16)
                    act.dma_start(pool_p[0, 0], ost_u[0:PH, :]).then_inc(out_st, 16)
                    act.dma_start(pool_s[0, :, PH - 1, :], ost_u[PH:PH + NS, :]).then_inc(out_st, 16)
                else:
                    for n, (c0, c1, j) in enumerate(MIXED):
                        act.wait_ge(mix_done, n + 1)
                        act.copy(hT_lo[:, c0:c1, tok(j)], pT[:, c0:c1, tok(j)]).then_inc(p_hi, 1)
                    act.wait_ge(vn_done, NT)
                    act.dma_start(v_p[0, 0], xs[:, 3, :]).then_inc(out_st, 16)
                    act.dma_start(v_s[0].rearrange("b s d -> (b s) d"), xs[0:NS, 4, :]).then_inc(out_st, 16)
                ph = 2 * l + 1
                fetch_root_table()
                for j in range(NT):
                    act.wait_ge(x_upd, NT * l + j + 1)
                    root(ph, j, x[0:ROWS[j], j, :])
                    if j >= 1:
                        evacuate(ph, j - 1, rT)
                evacuate(ph, NT - 1, rT)
                exponentials(l)
                experts_blocks(l)
                if l == 0:
                    fetch_root_table()
                    for c in range(4):
                        hi_chunk(1, c)
                    for j in range(NT):
                        act.wait_ge(y_add, 2 * (j + 1))
                        root(2, j, x[0:ROWS[j], j, :])
                        if j >= 1:
                            evacuate(2, j - 1, hT)
                            hi_tile(1, j - 1)
                    evacuate(2, NT - 1, hT)
                    hi_tile(1, NT - 1)
            fetch_root_table()
            for j in range(NT):
                r = slice(0, ROWS[j])
                act.wait_ge(y_add, 2 * NT + 2 * (j + 1))
                act.activation(junk[r, :], x[r, j, :], ACT.Square, accum_out=ss[r, 4, j:j + 1]).then_inc(v_sq, 1)
                act.wait_ge(v_sq, NT + j + 1)
                act.activation(rt[r, 4, j:j + 1], ss[r, 4, j:j + 1], ACT.Sqrt, bias=eps[r, :], scale=1.0 / D
                               ).then_inc(v_rt, 1)
                if 1 <= j <= BY_POOL:
                    act.wait_ge(fin_rs, j)
                    act.activation(x[:, j - 1, :], x[:, j - 1, :], ACT.Copy, scale=rs[:, 4, j - 1:j]
                                   ).then_inc(fin_scaled, 1)

        @block.vector
        def _(dve):
            step = Chain(dve, dve_step)

            def scale_rows(ph, j):
                n = NT * ph + j
                r = slice(0, ROWS[j])
                dve.wait_ge(rt_done, n + 1)
                dve.reciprocal(rs[r, ph, j:j + 1], rt[r, ph, j:j + 1]).then_inc(rc_done, 1)
                dve.wait_ge(rc_done, n + 1)
                dve.tensor_scalar(xs[r, j, :], x[r, j, :], rs[r, ph, j:j + 1], None, ALU.mult
                                  ).then_inc(xs_done, 1)

            def gain(row, n):
                return vecT[:, 0:4, row:row + 1].to_broadcast([P, 4, n])

            def evacuate(ph, j, dst):
                n = NT * ph + j
                row = (0, 2, 1, 3)[ph]
                dve.wait_ge(tr_done, n + 1)
                src = ps[:, 4 + 2 * (j % 2), :].rearrange("p (c t) -> p c t", c=4)[:, :, 0:ROWS[j]]
                dve.tensor_tensor(dst[:, 0:4, tok(j)], src, gain(row, ROWS[j]), ALU.mult).then_inc(ev_d, 1)

            def bc(ap, shape):
                return ap.to_broadcast(shape)

            def first_best(src, top, onehot):
                s = [P, 5 * NT, 4]
                step(dve.tensor_reduce(top, src, AX_X, ALU.max))
                step(dve.tensor_tensor(eq[:, :, :], src, bc(top.unsqueeze(2), s), ALU.is_equal))
                step(dve.tensor_tensor(eq[:, :, :], eq[:, :, :], bc(pri[:, :].unsqueeze(1), s), ALU.mult))
                step(dve.tensor_reduce(best[:, 2, :], eq[:, :, :], AX_X, ALU.max))
                step(dve.tensor_tensor(onehot, eq[:, :, :], bc(best[:, 2, :].unsqueeze(2), s), ALU.is_equal))

            def one_hot(l, b, par, e=None):
                m = moe[l]
                need(dve, m["id_mm"], b - 1)
                s = [P, NT, P]
                if e is None:
                    e, first = b, 0.0
                else:
                    first = table_f[:, bass.ds(TABLE + b, 1)]
                dve.scalar_tensor_tensor(out=onehot[:, par, :, :], in0=bc(rank1[:, :, bass.ds(e, 1)], s),
                                         scalar=first, in1=bc(count1[:, :].unsqueeze(1), s),
                                         op0=ALU.subtract, op1=ALU.is_equal).then_inc(m["onehot"], 1)

            def token_numbers(l, b, par):
                m = moe[l]
                dve.wait_ge(m["id_mm"], b + 1)
                need(dve, m["xT_mm"], b - 1)
                dve.tensor_reduce(ids_f[:, par:par + 1], ps[:, 7, 4 * par:4 * par + 2], AX_X, ALU.add
                                  ).then_inc(m["ids_f"], 1)
                dve.wait_ge(m["ids_f"], b + 1)
                dve.tensor_copy(ids[:, par:par + 1], ids_f[:, par:par + 1]).then_inc(m["ids"], 1)

            def rows_T(l, b):
                m = moe[l]
                need(dve, m["xT_mm"], b + 1)
                src = ps[:, 5, :].rearrange("p (c s) -> p c s", c=4)
                dve.tensor_tensor(xgT_parts[0], src, gain(2 + l, P), ALU.mult)
                dve.tensor_tensor(xgT[:, 0:4, :], src, gain(2 + l, P), ALU.mult).then_inc(m["xT_d"], 1)
                dve.wait_ge(m["xT_d"], b + 1)
                low(xgT_parts[1], xgT[:, 0:UP_SPLIT, :], xgT_parts[0], m["xT_lo"])

            def route(l):
                s16 = [P, NT, NG, EPG]
                flat = [oh[:, k, :, :, :].rearrange("p t a j -> p (t a) j") for k in range(2)]
                first_best(lg[:, :, :].rearrange("p t (a j) -> p (t a) j", j=4), best[:, 0, :], flat[0])
                step.aside(dve.tensor_tensor(goh[:, :, :], oh[:, 0, :, 0, :],
                                             bc(valid[:, :].unsqueeze(2), [P, NT, NG]), ALU.mult))
                step(dve.scalar_tensor_tensor(out=lg2[:, :, :], in0=flat[0], scalar=BIG,
                                              in1=lg[:, :, :].rearrange("p t (a j) -> p (t a) j", j=4),
                                              op0=ALU.mult, op1=ALU.add))
                def chosen(k):
                    return dve.tensor_tensor(sel[:, k, :, :].rearrange("p t (g j) -> p t g j", g=NG),
                                             bc(goh[:, :, :].unsqueeze(3), s16), oh[:, k, :, 1:5, :], ALU.mult)

                step.aside(chosen(0))
                first_best(lg2[:, :, :], best[:, 1, :], flat[1])
                step(chosen(1))
                dve.tensor_tensor(pairs_b[:, :, :], sel[:, 0, :, :], sel[:, 1, :, :], ALU.add).then_inc(rank_in, 1)
                tops = [best[:, k, :].rearrange("p (t a) -> p t a", t=NT) for k in range(2)]
                step(dve.tensor_tensor(ex[:, :, 0:NG], lg[:, :, 0:NG], bc(tops[0][:, :, 0:1], [P, NT, NG]),
                                       ALU.subtract))
                dve.tensor_tensor(ex[:, :, NG:], tops[1][:, :, 1:5], tops[0][:, :, 1:5], ALU.subtract
                                  ).then_inc(ex_in, 1)
                ov, ocs, oex, big, dlt = (c16[:, k, :] for k in range(5))
                dve.wait_ge(rank_mm, l + 1)
                cnt = ps[:, 5, 0:NE]
                rank = ps[:, 4, 0:NT * NE].rearrange("p (t e) -> p t e", t=NT)
                sE = [P, NT, NE]
                s2 = [P, 2, NT, NE]
                step(dve.scalar_tensor_tensor(out=rank1[:, :, :], in0=rank, scalar=1.0, in1=pairs_b[:, :, :],
                                              op0=ALU.add, op1=ALU.mult))
                th = over[:, 0:4, :].rearrange("p a e -> p (a e)").rearrange("p (e a) -> p e a", e=NE)
                step(dve.tensor_tensor(th, bc(cnt.unsqueeze(2), [P, NE, 4]),
                                       bc(thr[:, :].unsqueeze(1), [P, NE, 4]), ALU.is_gt))
                one_hot(l, 0, 0)
                one_hot(l, 1, 1)
                token_numbers(l, 0, 0)
                token_numbers(l, 1, 1)
                one_hot(l, 2, 0)
                step(dve.tensor_reduce(ov, th, AX_X, ALU.add))
                step(dve.tensor_tensor_scan(ocs, ov, zero16[:, :], 0.0, ALU.add, ALU.add))
                step(dve.tensor_tensor(oex, ocs, ov, ALU.subtract))
                sO = [P, MAX_OVER, NE]
                jb = bc(jidx[:, :].unsqueeze(2), sO)
                step(dve.tensor_tensor(over[:, :, :], bc(oex.unsqueeze(1), sO), jb, ALU.is_le))
                step(dve.tensor_tensor(over2[:, :, :], bc(ocs.unsqueeze(1), sO), jb, ALU.is_gt))
                step(dve.tensor_tensor(over[:, :, :], over[:, :, :], over2[:, :, :], ALU.mult))
                step(dve.tensor_tensor(over2[:, :, :], over[:, :, :], bc(eidx[:, :].unsqueeze(1), sO), ALU.mult))
                step(dve.tensor_reduce(table_f[:, NE:NE + MAX_OVER], over2[:, :, :], AX_X, ALU.add))
                step(dve.tensor_tensor(over2[:, :, :], over[:, :, :], bc(oex.unsqueeze(1), sO), ALU.mult))
                step(dve.tensor_reduce(o8[:, 0, :], over2[:, :, :], AX_X, ALU.add))
                step(dve.tensor_reduce(o8[:, 1, :], over[:, :, :], AX_X, ALU.add))
                step(dve.scalar_tensor_tensor(out=o8[:, 2, :], in0=jidx[:, :], scalar=1.0, in1=o8[:, 1, :],
                                              op0=ALU.add, op1=ALU.mult))
                step(dve.tensor_tensor(o8[:, 3, :], o8[:, 2, :], o8[:, 0, :], ALU.subtract))
                step(dve.tensor_scalar(table_f[:, TABLE + NE:TABLE + MAX_BLOCKS], o8[:, 3, :], float(P), None,
                                       ALU.mult))
                step(dve.tensor_tensor(o8[:, 0, 0:4], bc(ocs[:, NE - 1:NE], [P, 4]), thr2[:, :], ALU.is_gt))
                step(dve.tensor_reduce(table_f[:, 2 * TABLE:], o8[:, 0, 0:4], AX_X, ALU.add))
                step(dve.tensor_copy(table_f[:, 0:NE], eidx[:, :]))
                dve.tensor_copy(table[:, :], table_f[:, :]).then_inc(table_ok, 1)
                rows_T(l, 0)
                step(dve.tensor_scalar(big, oex, float(NE - 1), float(P), ALU.add, ALU.mult))
                step(dve.scalar_tensor_tensor(out=dlt, in0=eidx[:, :], scalar=float(P), in1=big,
                                              op0=ALU.mult, op1=ALU.subtract))
                yr = rows[:, :, :]
                step(dve.tensor_scalar(yr, rank1[:, :, :], float(P), None, ALU.is_le))
                step(dve.tensor_tensor(yr, yr, bc(dlt.unsqueeze(1), sE), ALU.mult))
                step(dve.scalar_tensor_tensor(out=yr, in0=rank1[:, :, :], scalar=-1.0, in1=yr, op0=ALU.add,
                                              op1=ALU.add))
                step(dve.tensor_tensor(yr, yr, bc(big.unsqueeze(1), sE), ALU.add))
                step(dve.tensor_tensor(prod[:, :, :, :], sel[:, :, :, :], bc(yr.unsqueeze(1), s2), ALU.mult))
                step(dve.tensor_reduce(slots_f[:, :, :], prod[:, :, :, :], AX_X, ALU.add))
                dve.tensor_copy(slots[:, :, :], slots_f[:, :, :]).then_inc(slots_ok, 1)
                dve.wait_ge(ex_out, l + 1)
                total, top, e2, both, share = (r1[:, k, :] for k in range(5))
                step(dve.tensor_reduce(total, ex[:, :, 0:NG], AX_X, ALU.add))
                step(dve.reciprocal(top, total))
                step(dve.tensor_tensor(ex2[:, :, :], ex[:, :, NG:], goh[:, :, :], ALU.mult))
                step(dve.tensor_reduce(e2, ex2[:, :, :], AX_X, ALU.add))
                step(dve.tensor_scalar(both, e2, 1.0, None, ALU.add))
                step(dve.reciprocal(share, both))
                step(dve.tensor_tensor(gates[:, 0, :], top, share, ALU.mult))
                step(dve.tensor_tensor(gates[:, 1, :], gates[:, 0, :], e2, ALU.mult))

            def experts_blocks(l):
                m = moe[l]

                def hidden_T(b, split=True):
                    dve.wait_ge(m["hT_mm"], b + 1)
                    need(dve, m["y_mm"], b)
                    if not split:
                        dve.tensor_copy(hidT, ps[:, 4, :]).then_inc(m["hT_e"], 1)
                        return
                    dve.tensor_copy(hidT_hi, ps[:, 4, :]).then_inc(m["hT_hi"], 1)
                    dve.wait_ge(m["hT_hi"], b + 1)
                    dve.tensor_tensor(hidT_lo, ps[:, 4, :], hidT_hi.bitcast(F32), ALU.subtract
                                      ).then_inc(m["hT_e"], 1)

                def lo_down(b, par):
                    dve.wait_ge(m["dn_hi"], b + 1)
                    low(wbuf_r[2][par][:, :], wbuf[2][par][:, :], down_hi, m["dn_lo"])

                def result(b, par, stored):
                    dve.wait_ge(m["y_mm"], b + 1)
                    need(dve, m["st_y"][par], 16 * stored)
                    dve.tensor_copy(yo[par][:, 0:512], ps[:, 2, :]).then_inc(m["y_d"], 1)

                def body(b, par, i, last):
                    first = isinstance(b, int) and b == 0
                    dve.wait_ge(m["up_hi"], b + 1)
                    low(wbuf_r[1][par][:, 0:UP_SPLIT * DE], wbuf[1][par][:, 0:UP_SPLIT * DE], up_hi, m["up_lo"])
                    if not first:
                        lo_down(b - 1, 1 - par)
                        hidden_T(b - 1)
                    dve.wait_ge(m["silu"], b + 1)
                    dve.wait_ge(m["h3_mm"], b + 1)
                    need(dve, m["hT_mm"], b)
                    dve.tensor_tensor(hid, act_g, ps[:, 1, :], ALU.mult).then_inc(m["hid"], 1)
                    if not last:
                        rows_T(l, b + 1)
                        token_numbers(l, b + 2, par)
                    if not first:
                        result(b - 1, 1 - par, (b - 1) // 2 if isinstance(b, int) else i - 1)
                    if not last:
                        e = dve.value_load(table[0:1, bass.ds(b + 3, 1)], min_val=0, max_val=NE - 1)
                        one_hot(l, b + 3, 1 - par, e)

                pairs = run_blocks(dve, l, body)
                hidden_T(2 * pairs - 1, split=False)
                result(2 * pairs - 1, 1, pairs - 1)

            def combine(l, j):
                r = slice(0, ROWS[j])
                dve.wait_ge(ld_y[j], 32 * (l + 1))
                for k in range(2):
                    n = 2 * NT * l + 2 * j + k
                    if k:
                        dve.wait_ge(y_add, n)
                    dve.scalar_tensor_tensor(out=x[r, j, :], in0=yg[(2 * j + k) % 8][r, :],
                                             scalar=gates[r, k, j:j + 1], in1=x[r, j, :],
                                             op0=ALU.mult, op1=ALU.add).then_inc(y_add, 1)

            def add_projection(l, j):
                r = slice(0, ROWS[j])
                dve.wait_ge(wo_done, NT * l + j + 1)
                dve.tensor_tensor(x[r, j, :], x[r, j, :], bank2(2 * (j % 2))[r, :], ALU.add).then_inc(x_upd, 1)

            def logits(l, j):
                r = slice(0, ROWS[j])
                dve.wait_ge(lg_mm, NT * l + j + 1)
                dve.scalar_tensor_tensor(out=lg[r, j, :], in0=ps[r, (4, 6)[j % 2], 0:NG + NE],
                                         scalar=rs[r, 2 * l + 1, j:j + 1], in1=br[r, l, :],
                                         op0=ALU.mult, op1=ALU.add).then_inc(lg_done, 1)

            def after_projection(l):
                ph = 2 * l + 1
                for j in range(NT):
                    add_projection(l, j)
                    if j >= 1:
                        evacuate(ph, j - 1, rT)
                    if j >= 2:
                        logits(l, j - 2)
                    if j == NT - 1:
                        evacuate(ph, j, rT)
                    scale_rows(ph, j)
                logits(l, NT - 2)
                logits(l, NT - 1)
                dve.wait_ge(lg_done, NT * (l + 1))
                route(l)

            def low(value_r, value, hi, done):
                dve.tensor_tensor(value_r, value, hi.bitcast(F32), ALU.subtract).then_inc(done, 1)

            def lo_tile(l, j):
                dve.wait_ge(tile_hi, NT * l + j + 1)
                low(hT_lo[:, :, tok(j)], hT[:, :, tok(j)], hT_hi[:, :, tok(j)], tile_lo)

            def lo_chunk(l, c):
                q, m = c // 4, c % 4
                if l == 0 and c < 2:
                    dve.wait_ge(w_hi_first, c + 1)
                else:
                    dve.wait_ge(w_hi, 16 * l + c + 1 - 2)
                low(chunk_of(quarter_lo[q], m), chunk_of(quarter_buf[q], m), chunk_hi[:, m, :, :], w_lo)

            def lo_piece(l, p):
                dve.wait_ge(wo_hi[0], 4 * l + p + 1)
                low(piece_of(half_lo[0], p), piece_of(half_buf[0], p), piece_of(half_hi[0], p), wo_lo[0])

            dve.wait_ge(consts, 1)
            dve.wait_ge(vec_t, 1)
            dve.tensor_copy(vecT[:, 0:4, :].rearrange("p c v -> p (c v)"), ps[:, 0, 0:4 * NV]).then_inc(vec_e, 1)
            dve.tensor_copy(vecT[:, 4:KC, 0:5],
                            ps[:, 0, 4 * NV:KC * NV].rearrange("p (c v) -> p c v", v=NV)[:, :, 0:5]
                            ).then_inc(vec_e, 1)
            for j in range(NT):
                dve.wait_ge(ld_x[j], 16)
                scale_rows(0, j)
            dve.wait_ge(vec_e, 2)
            for j in range(NT):
                evacuate(0, j, hT)
                if j >= 1:
                    lo_tile(0, j - 1)
                if j in (2, 3):
                    lo_chunk(0, j - 2)
            lo_tile(0, NT - 1)
            lo_chunk(0, 2)
            lo_chunk(0, 3)
            dve.wait_ge(vec_t, 2)
            step(dve.tensor_copy(histT.rearrange("p g b t -> p (g b t)"), ps[:, 4, 0:4 * NS * PH]))
            dve.tensor_copy(chistT.rearrange("p g b t -> p (g b t)"),
                            ps[:, 5, 0:4 * NS * CH]).then_inc(vec_e, 1)
            dve.wait_ge(vec_t, 3)
            dve.tensor_tensor(wsT[:, :, :], ps[:, 6:8, :].rearrange("p b (h t) -> p (b h) t", h=4),
                              bc(upto[:, :].unsqueeze(1), [P, NH, P]), ALU.mult).then_inc(vec_e, 1)
            dve.wait_ge(ld_small, 16 * 8)
            step(dve.tensor_tensor(wdiag[:, :, :], bc(ident[0:NS, 0:NS].unsqueeze(1), [NS, NH, NS]),
                                   bc(w00[:, :].unsqueeze(2), [NS, NH, NS]), ALU.mult))
            lo_chunk(0, 4)
            step(dve.memset(rcnt[:, :, :], 1.0))
            for g, win in enumerate(WINDOWS):
                for t in range(win):
                    dve.memset(rcnt[:, g, t:t + 1], 1.0 / (t + 1))
                if win < 16:
                    dve.memset(rcnt[:, g, win:16], 1.0 / win)
            step(dve.memset(sumA[:, 0:16], 0.0))
            step(dve.memset(sumB[:, 0:16], 0.0))

            for c in range(5, 8):
                lo_chunk(0, c)
            for g in range(4):
                if g:
                    lo_chunk(0, 7 + g)
                dve.wait_ge(mm_free, 8 + 2 * g + 2)
                z, acc = pT[:, 12 + g, :], pT[:, 8 + g, :]
                dve.tensor_tensor(z, acc, z, ALU.mult).then_inc(z_done, 1)
                dve.wait_ge(z_done, g + 1)
                cw = [vecT[:, g, 6 + k:7 + k] for k in range(3)]
                step(dve.tensor_scalar(acc, z, cw[2], None, ALU.mult))
                for k, back in ((1, 1), (0, 2)):
                    step(dve.scalar_tensor_tensor(out=acc[:, back:SEQ], in0=z[:, 0:SEQ - back], scalar=cw[k],
                                                  in1=acc[:, back:SEQ], op0=ALU.mult, op1=ALU.add))
                    step(dve.scalar_tensor_tensor(out=acc[:, SEQ:T], in0=chistT[:, g, :, k], scalar=cw[k],
                                                  in1=acc[:, SEQ:T], op0=ALU.mult, op1=ALU.add))
            for g, win in enumerate(WINDOWS):
                lo_chunk(0, 11 + g)
                dve.wait_ge(mm_free, 16 + 2 * g + 2)
                u = pT[:, g, :]
                cur, nxt = sumA, sumB
                step(dve.tensor_copy(cur[:, 16:17], u[:, 0:1]))
                step(dve.tensor_tensor(cur[:, 17:16 + SEQ], u[:, 1:SEQ], u[:, 0:SEQ - 1], ALU.add))
                for k in range(1, g + 1):
                    back = 2 ** k
                    step(dve.tensor_tensor(nxt[:, 16:16 + SEQ], cur[:, 16:16 + SEQ],
                                           cur[:, 16 - back:16 + SEQ - back], ALU.add))
                    cur, nxt = nxt, cur
                step(dve.scalar_tensor_tensor(out=dif[:, g, 16:SEQ], in0=cur[:, 32:16 + SEQ], scalar=1.0 / win,
                                              in1=u[:, 16:SEQ], op0=ALU.mult, op1=ALU.subtract))
                step(dve.tensor_tensor(head[:, g, :], cur[:, 16:32], rcnt[:, g, :], ALU.mult))
                step(dve.tensor_tensor(dif[:, g, 0:16], head[:, g, :], u[:, 0:16], ALU.subtract))
                step(dve.tensor_reduce(hs[:, g, :], histT[:, g, :, PH - win + 1:PH], AX_X, ALU.add))
                step(dve.tensor_tensor(hs2[:, g, :], hs[:, g, :], u[:, SEQ:T], ALU.add))
                dve.scalar_tensor_tensor(out=dif[:, g, SEQ:T], in0=hs2[:, g, :], scalar=1.0 / win,
                                         in1=u[:, SEQ:T], op0=ALU.mult, op1=ALU.subtract).then_inc(dif_done, 1)
            lo_chunk(0, 15)
            for g in range(4):
                dve.wait_ge(mm_free, 24 + 2 * g + 2)
                dve.tensor_tensor(pT[:, 4 + g, :], pT[:, 4 + g, :], pT[:, 8 + g, :], ALU.mult).then_inc(yb_done, 1)
                lo_piece(0, g)
                for n, c in ((2 * g, g), (2 * g + 1, 4 + g)):
                    dve.wait_ge(p_hi, n + 1)
                    if c < 4:
                        dve.wait_ge(ya_done, g + 1)
                    low(pT_r[:, c, :], pT[:, c, :], pT_hi[0][c], p_lo)
            dve.wait_ge(out_st, 16 * 4)
            dve.wait_ge(tails, 16 * MAX_OVER)
            after_projection(0)
            experts_blocks(0)
            for c in range(4):
                lo_chunk(1, c)
            for j in range(NT):
                combine(0, j)
                if j >= 1:
                    scale_rows(2, j - 1)
                if j >= 2:
                    evacuate(2, j - 2, hT)
            scale_rows(2, NT - 1)
            evacuate(2, NT - 2, hT)
            evacuate(2, NT - 1, hT)
            for c in range(4, 11):
                lo_chunk(1, c)

            for j in range(NT):
                r = slice(0, ROWS[j])
                lo_chunk(1, 11 + j)
                dve.wait_ge(vt_done, j + 1)
                dve.tensor_copy(xs[r, j, :], bank2(4 + 2 * (j % 2))[r, :]).then_inc(v_cp, 1)
            for p in range(2):
                lo_piece(1, p)
            dve.wait_ge(v_rt, 1)
            step(dve.reciprocal(rs[:, 4, :], rt[:, 4, :]))
            dve.wait_ge(ld_g[0], 16)
            for j in range(NT):
                r = slice(0, ROWS[j])
                dve.scalar_tensor_tensor(out=xs[r, j, :], in0=xs[r, j, :], scalar=rs[r, 4, j:j + 1],
                                         in1=g_sgu[r, :], op0=ALU.mult, op1=ALU.mult).then_inc(vn_done, 1)
            lo_piece(1, 2)
            dve.wait_ge(ld_g[1], 16)

            def lo_mixed(n):
                c0, c1, j = MIXED[n]
                dve.wait_ge(p_hi, 8 + n + 1)
                low(pT_r[:, c0:c1, tok(j)], pT[:, c0:c1, tok(j)], hT_lo[:, c0:c1, tok(j)], p_lo)

            def mixing_sums(j):
                dve.wait_ge(mix_mm, j + 1)
                n = ROWS[j]
                mixed = ps[:, 4 + 2 * (j % 2):6 + 2 * (j % 2), :].rearrange("p b (h t) -> p (b h) t", h=4)[:, :, 0:n]
                bias = b_bc if j < 4 else bc(b_bc[:, :, 0:1], [P, NH, n])
                mx = arena_a[:, 8 * T + (j % 2) * 1024:8 * T + (j % 2 + 1) * 1024].rearrange(
                    "p (h t) -> p h t", h=NH)[:, :, 0:n]
                step(dve.tensor_tensor(mx, mixed, bias, ALU.add))
                return mx

            for n, (c0, c1, j) in enumerate(MIXED):
                if n != 1:
                    mx = mixing_sums(j)
                if n == 0:
                    dve.wait_ge(mm_free, 32 + 24)
                if n == 1:
                    lo_piece(1, 3)
                    dve.wait_ge(mm_free, 64)
                dve.tensor_tensor(pT[:, c0:c1, tok(j)], pT[:, c0:c1, tok(j)], mx[:, c0:c1, :], ALU.mult
                                  ).then_inc(mix_done, 1)
                if n >= 1:
                    lo_mixed(n - 1)
            lo_mixed(NT)
            dve.wait_ge(out_st, 16 * 6)
            after_projection(1)
            experts_blocks(1)
            dve.wait_ge(ld_g[2], 16)

            def finish(j):
                r = slice(0, ROWS[j])
                dve.wait_ge(v_rt, 1 + j + 1)
                if j < BY_POOL:
                    dve.reciprocal(rs[r, 4, j:j + 1], rt[r, 4, j:j + 1]).then_inc(fin_rs, 1)
                    return
                step(dve.reciprocal(rs[r, 4, j:j + 1], rt[r, 4, j:j + 1]))
                dve.scalar_tensor_tensor(out=x[r, j, :], in0=x[r, j, :], scalar=rs[r, 4, j:j + 1],
                                         in1=g_fin[r, :], op0=ALU.mult, op1=ALU.mult).then_inc(fin_done, 1)

            for j in range(NT):
                combine(1, j)
                if j >= 1:
                    finish(j - 1)
            finish(NT - 1)


_INS = ["x_prompt", "x_sample", "state_pool", "state_conv", "norm_mix", "w_in_even", "w_pool", "pool_scale",
        "conv_w", "w_out_even", "w_in_odd", "sgu_norm", "w_sgu", "b_sgu", "w_out_odd", "norm_ffn",
        "w_router_group", "b_router_group", "w_router_expert", "b_router_expert", "w_gate", "w_up", "w_down",
        "norm_final"]
_OUTS = [(1, 512, 1024), (8, 1, 1024), (1, 1, 15, 512), (1, 8, 15, 512), (1, 1, 2, 512), (1, 8, 2, 512),
         (1, 1, 128, 1024), (1, 8, 1, 1024)]


def kernel(**inputs):
    import numpy as _np
    import concourse.bacc as _bacc
    from concourse import mybir as _mybir
    from concourse.bass_utils import run_bass_kernel_spmd as _run

    nc = _bacc.Bacc("TRN2", target_bir_lowering=False, num_devices=1)
    arrays, args = {}, []
    for name in _INS:
        a = _np.ascontiguousarray(inputs[name])
        arrays[f"in_{name}"] = a
        args.append(nc.dram_tensor(f"in_{name}", a.shape, _mybir.dt.from_np(a.dtype), kind="ExternalInput").ap())
    for i, shape in enumerate(_OUTS):
        args.append(nc.dram_tensor(f"out_{i}", shape, _mybir.dt.float32, kind="ExternalOutput").ap())
    trunk(nc, *args)
    r = _run(nc, [arrays], core_ids=[0])
    return tuple(r.results[0][f"out_{i}"] for i in range(len(_OUTS)))
```
